# Optimizing a Trainium2 kernel written in Bass

```python
import math
import jax, jax.numpy as jnp
from jax import lax
import numpy as np

D_MODEL = 1024
BATCH = 1
SEQ = 1024
DEPTH = 1
DEC_BATCH = 8
DEC_SEQ = 8
PAST_LEN = 2048
PAGE_SIZE = 128

HEAD_DIM = 64
MIX_WIDTH = D_MODEL
ATT_HEADS = MIX_WIDTH // (2 * HEAD_DIM)
ATT_KV_HEADS = ATT_HEADS // 4
ATT_GROUP = ATT_HEADS // ATT_KV_HEADS
WINDOW = 128
ATT_BLOCK = WINDOW
ATT_Q = ATT_HEADS * HEAD_DIM
ATT_KV = ATT_KV_HEADS * HEAD_DIM
DN_HEADS = 8
DN_DK = HEAD_DIM
DN_DV = HEAD_DIM
DN_WIDTH = DN_HEADS * DN_DV
DN_QKV = 2 * DN_HEADS * DN_DK + DN_WIDTH
CONV_W = 4
DN_CHUNK = 64
IN_WIDTH = ATT_Q + 2 * ATT_KV + DN_QKV + DN_WIDTH + 2 * DN_HEADS
N_KEYS = 128
N_EXPERTS = N_KEYS * N_KEYS
PEER_HEADS = 8
PEER_QDIM = 256
PEER_TOPK = 16
PEER_BLOCK = 256
PLE_DIM = 256
EPS = 1e-6

kernel_name = 'hymba_swa_gdn_peer_step'

def rmsnorm(x, g):
    xf = x.astype(jnp.float32)
    y = xf * lax.rsqrt(jnp.mean(xf * xf, axis=-1, keepdims=True) + EPS)
    return (y * g.astype(jnp.float32)).astype(x.dtype)

def l2norm(x):
    return x * lax.rsqrt(jnp.sum(x * x, axis=-1, keepdims=True) + EPS)

def alibi_slopes():
    h = jnp.arange(1, ATT_HEADS + 1, dtype=jnp.float32)
    return jnp.exp2(-8.0 * h / ATT_HEADS)

def _attend(q, k, v, dist, valid, sinks):
    s = jnp.einsum('bnqhgd,bnkhd->bnhgqk', q, k).astype(jnp.float32) * (HEAD_DIM ** -0.5)
    slopes = alibi_slopes().reshape(ATT_KV_HEADS, ATT_GROUP)[None, None, :, :, None, None]
    s = s - slopes * dist.astype(jnp.float32)[None, :, None, None]
    s = jnp.where(valid[None, :, None, None], s, -jnp.inf)
    sink = sinks.astype(jnp.float32).reshape(ATT_KV_HEADS, ATT_GROUP)[None, None, :, :, None, None]
    m = jnp.maximum(jnp.max(s, axis=-1, keepdims=True), sink)
    e = jnp.exp(s - m)
    probs = e / (jnp.sum(e, axis=-1, keepdims=True) + jnp.exp(sink - m))
    return jnp.einsum('bnhgqk,bnkhd->bnqhgd', probs.astype(v.dtype), v)

def swa_prompt(q, k, v, sinks):
    B, L = q.shape[0], q.shape[1]
    N = L // ATT_BLOCK
    qb = q.reshape(B, N, ATT_BLOCK, ATT_KV_HEADS, ATT_GROUP, HEAD_DIM)

    def band(t):
        tp = jnp.pad(t, ((0, 0), (ATT_BLOCK, 0), (0, 0), (0, 0)))
        tp = tp.reshape(B, N + 1, ATT_BLOCK, ATT_KV_HEADS, HEAD_DIM)
        return jnp.concatenate([tp[:, :-1], tp[:, 1:]], axis=2)

    i = jnp.arange(ATT_BLOCK)[:, None]
    j = jnp.arange(2 * ATT_BLOCK)[None, :]
    dist = ATT_BLOCK + i - j
    kpos = jnp.arange(N)[:, None, None] * ATT_BLOCK - ATT_BLOCK + j[None]
    valid = (dist >= 0) & (dist <= WINDOW) & (kpos >= 0)
    out = _attend(qb, band(k), band(v), jnp.broadcast_to(dist, valid.shape), valid, sinks)
    return out.reshape(B, L, ATT_Q), k[:, -WINDOW:], v[:, -WINDOW:]

def swa_sample(q, k, v, k_buf, v_buf, sinks):
    B, L = q.shape[0], q.shape[1]
    kc = jnp.concatenate([k_buf.astype(k.dtype), k], axis=1)
    vc = jnp.concatenate([v_buf.astype(v.dtype), v], axis=1)
    dist = jnp.arange(L)[:, None] - (jnp.arange(WINDOW + L)[None, :] - WINDOW)
    valid = (dist >= 0) & (dist <= WINDOW)
    qb = q.reshape(B, 1, L, ATT_KV_HEADS, ATT_GROUP, HEAD_DIM)
    out = _attend(qb, kc[:, None], vc[:, None], dist[None], valid[None], sinks)
    return out.reshape(B, L, ATT_Q), kc[:, -WINDOW:], vc[:, -WINDOW:]

def causal_conv(x, prefix, w):
    L = x.shape[1]
    xp = jnp.concatenate([prefix.astype(x.dtype), x], axis=1)
    y = xp[:, 0:L] * w[0]
    for j in range(1, CONV_W):
        y = y + xp[:, j:j + L] * w[j]
    return jax.nn.silu(y), xp[:, -(CONV_W - 1):]

def gated_delta_rule(q, k, v, g, beta, s0):
    B, L, H, dk = q.shape
    dv = v.shape[-1]
    C = min(DN_CHUNK, L)
    pad = (-L) % C
    N = (L + pad) // C

    def chunks(t):
        t = jnp.pad(t, [(0, 0), (0, pad)] + [(0, 0)] * (t.ndim - 2))
        t = t.reshape((B, N, C) + t.shape[2:])
        return jnp.moveaxis(t, 3, 1)

    q, k, v, g, beta = chunks(q), chunks(k), chunks(v), chunks(g), chunks(beta)
    G = jnp.cumsum(g, axis=-1)
    idx = jnp.arange(C)
    lower = idx[:, None] >= idx[None, :]
    strict = idx[:, None] > idx[None, :]
    decay = jnp.exp(jnp.where(lower, G[..., :, None] - G[..., None, :], -jnp.inf))
    kb = k * beta[..., None]
    Lm = jnp.where(strict, jnp.einsum('bhnid,bhnjd->bhnij', kb, k) * decay, 0.0)
    M = Lm + jnp.eye(C, dtype=Lm.dtype)
    rhs = jnp.concatenate([v * beta[..., None], kb * jnp.exp(G)[..., None]], axis=-1)
    X = lax.linalg.triangular_solve(M, rhs, left_side=True, lower=True, unit_diagonal=True)
    u, w = X[..., :dv], X[..., dv:]
    qk = jnp.einsum('bhnid,bhnjd->bhnij', q, k) * decay
    g_last = G[..., -1]
    k_tail = k * jnp.exp(g_last[..., None] - G)[..., None]
    q_head = q * jnp.exp(G)[..., None]

    def step(S, xs):
        qh, kt, uc, wc, qkc, gl = xs
        v_new = uc - jnp.einsum('bhcd,bhde->bhce', wc, S)
        o = jnp.einsum('bhcd,bhde->bhce', qh, S) + jnp.einsum('bhij,bhje->bhie', qkc, v_new)
        S = S * jnp.exp(gl)[..., None, None] + jnp.einsum('bhcd,bhce->bhde', kt, v_new)
        return S, o

    xs = tuple(jnp.moveaxis(t, 2, 0) for t in (q_head, k_tail, u, w, qk, g_last))
    S, o = lax.scan(step, s0, xs)
    o = jnp.moveaxis(jnp.moveaxis(o, 0, 2), 1, 3).reshape(B, N * C, H, dv)[:, :L]
    return o, S

def delta_branch(qkv_raw, z, a_raw, b_raw, conv_prefix, s0, conv_w, a_log, dt_bias, dn_norm):
    B, L = qkv_raw.shape[0], qkv_raw.shape[1]
    qkv, conv_new = causal_conv(qkv_raw, conv_prefix, conv_w)
    q, k, v = jnp.split(qkv, [DN_HEADS * DN_DK, 2 * DN_HEADS * DN_DK], axis=-1)
    q = l2norm(q.reshape(B, L, DN_HEADS, DN_DK).astype(jnp.float32)) * (DN_DK ** -0.5)
    k = l2norm(k.reshape(B, L, DN_HEADS, DN_DK).astype(jnp.float32))
    v = v.reshape(B, L, DN_HEADS, DN_DV).astype(jnp.float32)
    beta = jax.nn.sigmoid(b_raw.astype(jnp.float32))
    g = -jnp.exp(a_log.astype(jnp.float32)) * jax.nn.softplus(a_raw.astype(jnp.float32) + dt_bias.astype(jnp.float32))
    o, s_new = gated_delta_rule(q, k, v, g, beta, s0.astype(jnp.float32))
    o = rmsnorm(o, dn_norm) * jax.nn.silu(z.reshape(B, L, DN_HEADS, DN_DV).astype(jnp.float32))
    return o.reshape(B, L, DN_WIDTH).astype(qkv_raw.dtype), conv_new, s_new

def hybrid_mixer(a, kv_buf, conv_prefix, s0, w_in, conv_w, sinks, a_log, dt_bias, dn_norm, w_out):
    B, L = a.shape[0], a.shape[1]
    proj = a @ w_in
    cuts = [ATT_Q, ATT_Q + ATT_KV, ATT_Q + 2 * ATT_KV, ATT_Q + 2 * ATT_KV + DN_QKV,
            ATT_Q + 2 * ATT_KV + DN_QKV + DN_WIDTH, ATT_Q + 2 * ATT_KV + DN_QKV + DN_WIDTH + DN_HEADS]
    qa, ka, va, dqkv, z, ar, br = jnp.split(proj, cuts, axis=-1)
    qa = qa.reshape(B, L, ATT_HEADS, HEAD_DIM)
    ka = ka.reshape(B, L, ATT_KV_HEADS, HEAD_DIM)
    va = va.reshape(B, L, ATT_KV_HEADS, HEAD_DIM)
    if kv_buf is None:
        att, k_new, v_new = swa_prompt(qa, ka, va, sinks)
    else:
        att, k_new, v_new = swa_sample(qa, ka, va, kv_buf[0], kv_buf[1], sinks)
    dn, conv_new, s_new = delta_branch(dqkv, z, ar, br, conv_prefix, s0, conv_w, a_log, dt_bias, dn_norm)
    out = jnp.concatenate([att, dn], axis=-1) @ w_out
    return out, k_new, v_new, conv_new, s_new

def peer(x, wq, keys1, keys2, u_tab, v_tab):
    B, L, D = x.shape
    T = B * L
    blk = min(PEER_BLOCK, T)
    pad = (-T) % blk
    xt = jnp.pad(x.reshape(T, D), ((0, pad), (0, 0))).reshape(-1, blk, D)
    half = PEER_QDIM // 2

    def block(xb):
        q = (xb @ wq).reshape(blk, PEER_HEADS, PEER_QDIM).astype(jnp.float32)
        s1 = jnp.einsum('thd,hnd->thn', q[..., :half], keys1.astype(jnp.float32))
        s2 = jnp.einsum('thd,hnd->thn', q[..., half:], keys2.astype(jnp.float32))
        v1, i1 = lax.top_k(s1, PEER_TOPK)
        v2, i2 = lax.top_k(s2, PEER_TOPK)
        cand = (v1[..., :, None] + v2[..., None, :]).reshape(blk, PEER_HEADS, PEER_TOPK * PEER_TOPK)
        sc, ci = lax.top_k(cand, PEER_TOPK)
        e1 = jnp.take_along_axis(i1, ci // PEER_TOPK, axis=-1)
        e2 = jnp.take_along_axis(i2, ci % PEER_TOPK, axis=-1)
        expert = e1 * N_KEYS + e2
        gate = jax.nn.softmax(sc, axis=-1)
        act = jax.nn.gelu(jnp.einsum('td,thkd->thk', xb, u_tab[expert]).astype(jnp.float32), approximate=False)
        return jnp.einsum('thk,thkd->td', (gate * act).astype(xb.dtype), v_tab[expert])

    y = lax.map(block, xt).reshape(-1, D)[:T]
    return y.reshape(B, L, D)

def decoder_layer(h, p_l, kv_buf, conv_prefix, s0, norm_mix, w_in, conv_w, sinks, a_log, dt_bias, dn_norm,
                  w_out, norm_ffn, peer_wq, keys1, keys2, peer_u, peer_v, norm_ple, ple_in, ple_gate):
    mix, k_new, v_new, conv_new, s_new = hybrid_mixer(rmsnorm(h, norm_mix), kv_buf, conv_prefix, s0, w_in,
                                                      conv_w, sinks, a_log, dt_bias, dn_norm, w_out)
    h = h + mix
    h = h + peer(rmsnorm(h, norm_ffn), peer_wq, keys1, keys2, peer_u, peer_v)
    gate = jax.nn.sigmoid((rmsnorm(h, norm_ple) @ ple_gate).astype(jnp.float32))
    h = h + ((p_l @ ple_in).astype(jnp.float32) * gate).astype(h.dtype)
    return h, k_new, v_new, conv_new, s_new

def setup_inputs(seed: int = 0) -> dict:
    key = jax.random.key(seed)
    ks = jax.random.split(key, 32)
    f32 = jnp.float32
    nrm = lambda k, shape, scale: jax.random.normal(k, shape, f32) * scale
    dt = jnp.exp(jax.random.uniform(ks[10], (DEPTH, DN_HEADS), f32, math.log(1e-3), math.log(1e-1)))
    return {
        'x_prompt': nrm(ks[0], (BATCH, SEQ, D_MODEL), 1.0),
        'x_sample': nrm(ks[1], (DEC_BATCH, DEC_SEQ, D_MODEL), 1.0),
        'p_prompt': nrm(ks[2], (DEPTH, BATCH, SEQ, PLE_DIM), 1.0),
        'p_sample': nrm(ks[3], (DEPTH, DEC_BATCH, DEC_SEQ, PLE_DIM), 1.0),
        'cache_swa_k': nrm(ks[4], (DEPTH, DEC_BATCH, WINDOW, ATT_KV_HEADS, HEAD_DIM), 1.0),
        'cache_swa_v': nrm(ks[5], (DEPTH, DEC_BATCH, WINDOW, ATT_KV_HEADS, HEAD_DIM), 1.0),
        'state_conv': nrm(ks[6], (DEPTH, DEC_BATCH, CONV_W - 1, DN_QKV), 1.0),
        'state_delta': nrm(ks[7], (DEPTH, DEC_BATCH, DN_HEADS, DN_DK, DN_DV), DN_DK ** -0.5),
        'norm_mix': 1.0 + nrm(ks[8], (DEPTH, D_MODEL), 0.02),
        'w_in': nrm(ks[9], (DEPTH, D_MODEL, IN_WIDTH), D_MODEL ** -0.5),
        'conv_w': nrm(ks[11], (DEPTH, CONV_W, DN_QKV), 0.5),
        'attn_sinks': nrm(ks[12], (DEPTH, ATT_HEADS), 0.5),
        'dn_a_log': jnp.log(jax.random.uniform(ks[13], (DEPTH, DN_HEADS), f32, 1.0, 16.0)),
        'dn_dt_bias': dt + jnp.log(-jnp.expm1(-dt)),
        'dn_norm': 1.0 + nrm(ks[14], (DEPTH, DN_DV), 0.02),
        'w_out': nrm(ks[15], (DEPTH, MIX_WIDTH, D_MODEL), MIX_WIDTH ** -0.5),
        'norm_ffn': 1.0 + nrm(ks[16], (DEPTH, D_MODEL), 0.02),
        'peer_wq': nrm(ks[17], (DEPTH, D_MODEL, PEER_HEADS * PEER_QDIM), D_MODEL ** -0.5),
        'peer_keys1': nrm(ks[18], (DEPTH, PEER_HEADS, N_KEYS, PEER_QDIM // 2), (PEER_QDIM // 2) ** -0.5),
        'peer_keys2': nrm(ks[19], (DEPTH, PEER_HEADS, N_KEYS, PEER_QDIM // 2), (PEER_QDIM // 2) ** -0.5),
        'peer_u': nrm(ks[20], (DEPTH, N_EXPERTS, D_MODEL), D_MODEL ** -0.5),
        'peer_v': nrm(ks[21], (DEPTH, N_EXPERTS, D_MODEL), 0.25),
        'norm_ple': 1.0 + nrm(ks[22], (DEPTH, D_MODEL), 0.02),
        'ple_in': nrm(ks[23], (DEPTH, PLE_DIM, D_MODEL), PLE_DIM ** -0.5),
        'ple_gate': nrm(ks[24], (DEPTH, D_MODEL, D_MODEL), D_MODEL ** -0.5),
        'norm_final': 1.0 + nrm(ks[25], (D_MODEL,), 0.02),
    }

def reference(x_prompt, x_sample, p_prompt, p_sample, cache_swa_k, cache_swa_v, state_conv, state_delta,
              norm_mix, w_in, conv_w, attn_sinks, dn_a_log, dn_dt_bias, dn_norm, w_out, norm_ffn,
              peer_wq, peer_keys1, peer_keys2, peer_u, peer_v, norm_ple, ple_in, ple_gate, norm_final):
    hp, hs = x_prompt, x_sample
    Bp = x_prompt.shape[0]
    kp_l, vp_l, cp_l, sp_l, ks_l, vs_l, cs_l, ss_l = [], [], [], [], [], [], [], []
    for l in range(DEPTH):
        w = (norm_mix[l], w_in[l], conv_w[l], attn_sinks[l], dn_a_log[l], dn_dt_bias[l], dn_norm[l],
             w_out[l], norm_ffn[l], peer_wq[l], peer_keys1[l], peer_keys2[l], peer_u[l], peer_v[l],
             norm_ple[l], ple_in[l], ple_gate[l])
        conv0 = jnp.zeros((Bp, CONV_W - 1, DN_QKV), x_prompt.dtype)
        s0 = jnp.zeros((Bp, DN_HEADS, DN_DK, DN_DV), jnp.float32)
        hp, kp, vp, cp, sp = decoder_layer(hp, p_prompt[l], None, conv0, s0, *w)
        hs, kn, vn, cn, sn = decoder_layer(hs, p_sample[l], (cache_swa_k[l], cache_swa_v[l]),
                                           state_conv[l], state_delta[l], *w)
        kp_l.append(kp); vp_l.append(vp); cp_l.append(cp); sp_l.append(sp.astype(state_delta.dtype))
        ks_l.append(kn); vs_l.append(vn); cs_l.append(cn); ss_l.append(sn.astype(state_delta.dtype))
    y_prompt = rmsnorm(hp, norm_final)
    y_sample = rmsnorm(hs, norm_final)
    return (y_prompt, y_sample,
            jnp.stack(kp_l), jnp.stack(vp_l), jnp.stack(cp_l), jnp.stack(sp_l),
            jnp.stack(ks_l), jnp.stack(vs_l), jnp.stack(cs_l), jnp.stack(ss_l))


_drawn_inputs = setup_inputs


def setup_inputs(seed=0):
    import zlib

    import numpy as np

    out = dict(_drawn_inputs(seed))
    spreads = {}
    factors = {'attn_sinks': 5.994,
     'dn_norm': 4.949,
     'norm_ffn': 3.631,
     'norm_ple': 200.0,
     'norm_final': 22.079}
    for name, (base, spread) in spreads.items():
        noise = np.random.default_rng([zlib.crc32(name.encode()), seed]).standard_normal(out[name].shape)
        drawn = base * np.exp(spread * noise) if base else spread * noise
        out[name] = __import__('jax').numpy.asarray(drawn.astype(out[name].dtype))
    for name, factor in factors.items():
        out[name] = (out[name] * factor).astype(out[name].dtype)
    return out
```

```python
import concourse.bass as bass
from concourse import mybir
from contextlib import ExitStack

F32 = mybir.dt.float32
I32 = mybir.dt.int32
U32 = mybir.dt.uint32
ALU = mybir.AluOpType
ACT = mybir.ActivationFunctionType
AXX = mybir.AxisListType.X

P = 128
D = 1024
KD = D // P
SEQ = 1024
TILES = SEQ // P
DB, DS = 8, 8
NS = DB * DS
ALLT = TILES + 1
HD = 64
AH, KVH, GRP = 8, 2, 4
WIN = 128
DH = 8
PAIRS = DH // 2
DQKV = 3 * DH * HD
CB = DQKV // P
TAPS = 4
C_K, C_V, C_DN = 512, 640, 768
C_Z = C_DN + DQKV
C_AB = C_Z + DH * HD
INW = C_AB + 2 * DH
NK = 128
NEXP = NK * NK
PH, TOPK = 8, 16
SLOTS = PH * TOPK
PLE = 256
EPS = 1e-6
FAR = 1e32
LOW = -3e38
LEVELS = (1, 2, 4, 8, 16, 32, 64)
SKEYS = WIN + DS
SLOPE = [-(2.0 ** (-8.0 * (h + 1) / AH)) for h in range(AH)]


def mixer_block(nc, sems, a, out, h_rows):
    with ExitStack() as ctx:
        def sb(name, shape, dt=F32):
            return ctx.enter_context(nc.sbuf_tensor(name, shape, dt))

        def sem(name):
            return sems.enter_context(nc.semaphore("mixer_" + name))

        bank = [ctx.enter_context(nc.psum_tensor(f"mbank{b}", [P, 512], F32)) for b in range(8)]

        w_in = sb("w_in_sb", [P, KD, INW])
        w_flat = w_in[:, :, :].rearrange("p k n -> p (k n)")
        w_out = sb("w_out_sb", [P, KD, D])
        ident = sb("m_ident", [P, P])
        tri = sb("m_tri", [P, P])
        tri8 = sb("m_tri8", [P, NS])
        level = sb("m_level", [P, len(LEVELS), P])
        ones = sb("m_ones", [P, P])
        same8 = sb("m_same8", [P, NS])
        seq_of = sb("m_seq_of", [P, DB])
        pair_diag = sb("m_pair_diag", [P, P])
        g_mix = sb("g_mix_sb", [P, KD])
        cw = sb("conv_w_sb", [P, TAPS, CB])
        sinks = sb("sinks_sb", [P, AH])
        neg_a = sb("neg_a_sb", [P, DH])
        dtb = sb("dtb_sb", [P, DH])
        dnn = sb("dn_norm_sb", [P, HD])
        dist = sb("att_dist", [P, 2 * WIN])
        dist_old = sb("att_dist_old", [P, WIN])
        dist_s = sb("att_dist_s", [GRP * DS, SKEYS])
        slope_s = sb("att_slope_s", [GRP * DS, KVH])
        eps = sb("m_eps", [P, 1])
        one = sb("m_one", [P, 1])

        xh = sb("x_and_h", [P, D])
        x = xn = h = xh
        st = sb("m_stats", [P, 4])
        aT = sb("aT_sb", [P, KD, P])
        a_tail = sb("aT_tail", [P, KD, TAPS - 1])
        cin = sb("cin_sb", [P, CB, TAPS - 1 + P])
        cacc = sb("cacc_sb", [P, CB, P])
        cs = sb("cs_sb", [P, CB, P])
        qT = sb("qT_sb", [P, GRP, P])
        kT = sb("kT_sb", [P, 2 * P])
        kv = sb("kv_sb", [P, 2, P])
        v_old = sb("v_old_sb", [P, P])
        zs = sb("zs_sb", [P, 512])
        sc = sb("att_sc", [P, AH, 2 * WIN])
        am = sb("att_m", [P, 6, AH])
        pT = sb("att_pT", [P, AH, 2, P])
        gt = sb("gate_small", [P, 12, DH])
        rn = sb("m_rn", [P, 3, 16])
        rows = sb("dn_rows", [P, 6, 512])
        vb = sb("dn_vb", [P, 512])
        rT = sb("dn_rT", [P, 5, 4, P])
        s2 = sb("dn_s2", [P, PAIRS, P])
        eg = sb("dn_eg", [P, PAIRS])
        dn = sb("dn_out", [P, 512])
        qT_s = qT[:, :, :].rearrange("p c t -> p (c t)")[:, 0:DB * GRP * DS].rearrange("p (b h t) -> p b h t", b=DB, h=GRP)
        mT = aT
        x_res = rT[:, 0:2, :, :].rearrange("p a c t -> p (a c t)")
        dt_ = cacc[:, 0:DH, :]
        cs_flat = cs[:, :, :].rearrange("p c t -> p (c t)")
        sq = cs_flat[:, 0:1024]
        y0, y1, ty = (cs_flat[:, n * 512:(n + 1) * 512] for n in range(3))
        rows_flat = rows[:, :, :].rearrange("p c t -> p (c t)")
        lt = rows_flat[:, 0:1024].rearrange("p (h t) -> p h t", h=DH)
        qk = rows_flat[:, 1024:2048].rearrange("p (h t) -> p h t", h=DH)
        vn = rows[:, 4, :]
        stconv = rows_flat[0:24, 0:DQKV]
        pT_flat = pT[:, :, :, :].rearrange("p h c t -> p (h c t)")
        bt = pT_flat[:, 0:1024].rearrange("p (h t) -> p h t", h=DH)
        t1 = pT_flat[:, 1024:2048].rearrange("p (h t) -> p h t", h=DH)
        xx = sc[:, :, :].rearrange("p h (c t) -> p h c t", c=2)
        s2n = vb[:, :].rearrange("p (c t) -> p c t", c=PAIRS)
        stage3 = cin[:, :, :].rearrange("p c t -> p (c t)")[:, 0:DQKV]

        at = [0]

        def over(n):
            at[0] += n
            assert at[0] <= KD * INW
            return w_flat[:, at[0] - n:at[0]]

        s2s = over(DB * PAIRS * P).rearrange("p (b c v) -> p b c v", b=DB, c=PAIRS)
        kgm = over(DB * PAIRS * NS).rearrange("p (b c t) -> p b c t", b=DB, c=PAIRS)
        qgm = over(DB * PAIRS * NS).rearrange("p (b c t) -> p b c t", b=DB, c=PAIRS)
        ktm = over(2 * 512).rearrange("p (r n) -> p r n", r=2)
        kc = over(DB * P).rearrange("p (b n) -> p b n", b=DB)
        vc = over(DB * P).rearrange("p (b n) -> p b n", b=DB)
        kcT = over(DB * P).rearrange("p (b n) -> p b n", b=DB)
        vnew = over(DB * P).rearrange("p (b n) -> p b n", b=DB)
        ssc = over(2 * DB * SKEYS).rearrange("p (b k) -> p b k", k=SKEYS)
        sm = over(6 * 2 * DB).rearrange("p (r n) -> p r n", r=6)
        spT = over(512).rearrange("p (b r) -> p b r", b=2 * DB)
        spTn = over(512).rearrange("p (b r) -> p b r", b=2 * DB)
        egb = over(DB * PAIRS).rearrange("p (b c) -> p b c", b=DB)
        gmb = over(DB * DH).rearrange("p (b c) -> p b c", b=DB)
        crow = over(DQKV)
        sink_s = sb("sink_s", [P, 2])

        names = ("const_in w_in_in w_out_in misc_in consts x_in rms xn_ready xT_ps aT_ready dqkv_ps "
                 "cin_ready ab_ps z_ps qkv_ps qkv_sb silu_done conv_done rows_ps sq_done ssq_done rn_sqrt "
                 "soft_in soft_out gate_ready gsum_ps e_in exp_ready drow_ready rT_ps rT_a rT_v gram_ps "
                 "kgs_ps y0_ready b_ready t_ps t_sb zz_ps xx_ready y1_ps y1_sb ty_ps ty_sb yz_ps vn_ready "
                 "o_ps upd_ps osq_done ossq orms dn_ready dnT_ps dnT_sb score_ps sc_ready nm_ready "
                 "prob_done probs_ready pT_ps pT_sb att_ps att_sb proj_ps h_ready h_out tile_free "
                 "state_out zsilu stc_in stc_ps stc_sb cache_in state_in vnew_in kcT_ps kcT_sb over_clear "
                 "ktm_ready supd_ps supd_done conv_ps conv_sb out_done mm_masked sexp kmask_ready sprobs "
                 "xres_in").split()
        s = {n: sem(n) for n in names}
        block = ctx.enter_context(nc.Block())

        @block.sync
        def _(sp):
            wv = a["w_in"][0].rearrange("(k p) n -> p k n", p=P)
            for k in range(KD):
                sp.dma_start(w_in[:, k, C_DN:INW], wv[:, k, C_DN:INW]).then_inc(s["w_in_in"], 16)
            for b in range(GRP):
                for g in range(KVH):
                    c = (g * GRP + b) * HD
                    sp.dma_start(w_in[:, :, b * P + g * HD:b * P + (g + 1) * HD],
                                 wv[:, :, c:c + HD]).then_inc(s["w_in_in"], 16)
            sp.dma_start(w_in[:, :, C_K:C_DN], wv[:, :, C_K:C_DN]).then_inc(s["w_in_in"], 16)
            wo = a["w_out"][0]
            for b in range(GRP):
                for g in range(KVH):
                    r = (g * GRP + b) * HD
                    sp.dma_start(w_out[g * HD:(g + 1) * HD, b, :], wo[r:r + HD, :]).then_inc(s["w_out_in"], 16)
            sp.dma_start(w_out[:, 4:8, :], wo[512:1024, :].rearrange("(k p) n -> p k n", p=P)).then_inc(s["w_out_in"], 16)

            def tile(i, r, src, dst):
                sp.wait_ge(s["tile_free"], i + 1)
                sp.dma_start(x[0:r, :], src).then_inc(s["x_in"], 16)
                sp.wait_ge(s["gram_ps"], i + 1)
                sp.dma_start(x_res[0:r, :], src).then_inc(s["xres_in"], 16)
                sp.wait_ge(s["h_ready"], i + 1)
                sp.dma_start(dst, h[0:r, :]).then_inc(s["h_out"], 16)

            with sp.Fori(0, TILES) as i:
                tile(i, P, a["x_prompt"][0, bass.ds(i * P, P), :], h_rows[bass.ds(i * P, P), :])
            sp.wait_ge(s["tile_free"], TILES + 1)
            sp.dma_start(out["k_p"][0, 0].rearrange("t g d -> t (g d)"), kv[:, 0, :]).then_inc(s["state_out"], 16)
            sp.dma_start(out["v_p"][0, 0].rearrange("t g d -> t (g d)"), kv[:, 1, :]).then_inc(s["state_out"], 16)
            for hh in range(DH):
                q, c = divmod(hh, 2)
                sp.dma_start(out["s_p"][0, 0, hh], s2[c * HD:(c + 1) * HD, q, c * HD:(c + 1) * HD]).then_inc(s["state_out"], 16)
            sp.dma_start(x[0:NS, :], a["x_sample"].rearrange("b t d -> (b t) d")).then_inc(s["x_in"], 16)
            sp.dma_start(stconv[:, :], a["state_conv"][0].rearrange("b t c -> (b t) c")).then_inc(s["stc_in"], 16)
            sp.wait_ge(s["over_clear"], 1)
            for c in range(2):
                for b in range(DB):
                    sp.dma_start(s2s[c * HD:(c + 1) * HD, b, :, c * HD:(c + 1) * HD],
                                 a["state_delta"][0, b, c:DH:2].rearrange("h k v -> k h v")).then_inc(s["state_in"], 16)
            sp.dma_start(kc[:, :, :], a["cache_swa_k"][0].rearrange("b t g d -> t b (g d)")).then_inc(s["cache_in"], 16)
            sp.dma_start(vc[:, :, :], a["cache_swa_v"][0].rearrange("b t g d -> t b (g d)")).then_inc(s["cache_in"], 16)
            for src, dst in (("cache_swa_k", "k_s"), ("cache_swa_v", "v_s")):
                sp.dma_start(out[dst][0][:, 0:WIN - DS], a[src][0][:, DS:WIN]).then_inc(s["out_done"], 16)
            sp.wait_ge(s["qkv_sb"], TILES + 1)
            for b in range(DB):
                sp.dma_start(vnew[0:DS, b, :], kv[b * DS:(b + 1) * DS, 1, :]).then_inc(s["vnew_in"], 16)
                sp.dma_start(out["k_s"][0, b, WIN - DS:WIN].rearrange("t g d -> t (g d)"),
                             kv[b * DS:(b + 1) * DS, 0, :]).then_inc(s["out_done"], 16)
                sp.dma_start(out["v_s"][0, b, WIN - DS:WIN].rearrange("t g d -> t (g d)"),
                             kv[b * DS:(b + 1) * DS, 1, :]).then_inc(s["out_done"], 16)
            sp.wait_ge(s["conv_sb"], 2)
            for b in range(DB):
                sp.dma_start(out["c_s"][0, b], crow[b * DS + DS - 3:(b + 1) * DS, :]).then_inc(s["out_done"], 16)
            sp.wait_ge(s["gram_ps"], TILES + 1)
            sp.dma_start(x_res[0:NS, :], a["x_sample"].rearrange("b t d -> (b t) d")).then_inc(s["xres_in"], 16)
            sp.wait_ge(s["supd_done"], DB)
            for b in range(DB):
                for hh in range(DH):
                    q, c = divmod(hh, 2)
                    sp.dma_start(out["s_s"][0, b, hh], s2s[c * HD:(c + 1) * HD, b, q, c * HD:(c + 1) * HD]).then_inc(s["out_done"], 16)
            sp.wait_ge(s["h_ready"], TILES + 1)
            sp.dma_start(h_rows[SEQ:SEQ + P, :], h[:, :]).then_inc(s["h_out"], 16)
            sp.wait_ge(s["h_out"], 16 * (TILES + 1))
            sp.wait_ge(s["state_out"], 16 * (2 + DH))
            sp.wait_ge(s["out_done"], 16 * (2 + 2 * DB + DB + DB * DH))

        @block.gpsimd
        def _(pool):
            g = nc.gpsimd
            row = lambda ap, n: ap.rearrange("(o n) -> o n", o=1).to_broadcast([P, n])
            pool.dma_start(sinks[:, :], row(a["attn_sinks"][0], AH)).then_inc(s["const_in"], 16)
            pool.dma_start(neg_a[:, :], row(a["dn_a_log"][0], DH)).then_inc(s["const_in"], 16)
            pool.dma_start(dtb[:, :], row(a["dn_dt_bias"][0], DH)).then_inc(s["const_in"], 16)
            pool.dma_start(dnn[:, :], row(a["dn_norm"][0], HD)).then_inc(s["const_in"], 16)
            pool.dma_start(dist_s[:, :], a["c_dist"]).then_inc(s["const_in"], 16)
            pool.dma_start(slope_s[:, :], a["c_slope"]).then_inc(s["const_in"], 16)
            with nc.allow_non_contiguous_dma(reason="small weights onto the partitions"):
                pool.dma_start(g_mix[:, :], a["norm_mix"][0].rearrange("(k p) -> p k", p=P)).then_inc(s["const_in"], 16)
                for j in range(TAPS):
                    pool.dma_start(cw[:, j, :], a["conv_w"][0, j].rearrange("(c p) -> p c", p=P)).then_inc(s["const_in"], 16)
                for hh in range(AH):
                    gg, p = divmod(hh, GRP)
                    pool.dma_start(sink_s[p * DS:(p + 1) * DS, gg:gg + 1],
                                   a["attn_sinks"][0:1, hh:hh + 1].to_broadcast([DS, 1])).then_inc(s["const_in"], 16)
            g.memset(eps[:, :], EPS)
            g.memset(one[:, :], 1.0)
            g.memset(ones[:, :], 1.0)
            g.memset(ident[:, :], 0.0)
            g.memset(tri[:, :], 1.0)
            g.memset(pair_diag[:, :], 1.0)
            g.memset(seq_of[:, :], 1.0)
            g.memset(same8[:, :], 1.0)
            g.memset(level[:, :, :], 1.0)
            g.memset(cin[:, :, 0:TAPS - 1], 0.0)
            g.memset(kT[:, :], 0.0)
            g.memset(v_old[:, :], 0.0)
            g.memset(s2[:, :, :], 0.0)
            pool.drain()
            g.affine_select(out=ident[:, :], in_=ident[:, :], compare_op=ALU.not_equal, fill=1.0,
                            base=0, pattern=[[-1, P]], channel_multiplier=1)
            g.affine_select(out=tri[:, :], in_=tri[:, :], compare_op=ALU.is_ge, fill=0.0,
                            base=0, pattern=[[1, P]], channel_multiplier=-1)
            g.affine_select(out=pair_diag[:, 0:HD], in_=pair_diag[:, 0:HD], compare_op=ALU.is_gt, fill=0.0,
                            base=HD, pattern=[[0, HD]], channel_multiplier=-1)
            g.affine_select(out=pair_diag[:, HD:P], in_=pair_diag[:, HD:P], compare_op=ALU.is_ge, fill=0.0,
                            base=-HD, pattern=[[0, HD]], channel_multiplier=1)
            for n, w in enumerate(LEVELS):
                v = level[:, n, :].rearrange("p (a c) -> p a c", c=2 * w)
                g.affine_select(out=v, in_=v, compare_op=ALU.is_ge, fill=0.0, base=0,
                                pattern=[[-2 * w, P // (2 * w)], [0, 2 * w]], channel_multiplier=1)
            sv = same8[:, :].rearrange("p (b t) -> p b t", t=DS)
            g.affine_select(out=sv, in_=sv, compare_op=ALU.is_ge, fill=0.0, base=0,
                            pattern=[[-DS, DB], [0, DS]], channel_multiplier=1)
            g.affine_select(out=seq_of[:, :], in_=seq_of[:, :], compare_op=ALU.is_ge, fill=0.0, base=0,
                            pattern=[[-DS, DB]], channel_multiplier=1)
            pool.drain()
            for n, w in enumerate(LEVELS):
                v = level[:, n, :].rearrange("p (a c) -> p a c", c=2 * w)
                g.affine_select(out=v, in_=v, compare_op=ALU.is_gt, fill=0.0, base=w,
                                pattern=[[2 * w, P // (2 * w)], [0, 2 * w]], channel_multiplier=-1)
            g.affine_select(out=sv, in_=sv, compare_op=ALU.is_gt, fill=0.0, base=DS,
                            pattern=[[DS, DB], [0, DS]], channel_multiplier=-1)
            g.affine_select(out=seq_of[:, :], in_=seq_of[:, :], compare_op=ALU.is_gt, fill=0.0, base=DS,
                            pattern=[[DS, DB]], channel_multiplier=-1)
            pool.drain()
            for n, w in enumerate(LEVELS):
                v = level[:, n, :].rearrange("p (a c) -> p a c", c=2 * w)
                g.affine_select(out=v, in_=v, compare_op=ALU.is_ge, fill=0.0, base=-w,
                                pattern=[[0, P // (2 * w)], [1, 2 * w]], channel_multiplier=0)
            g.tensor_tensor(tri8[:, :], tri[:, 0:NS], same8[:, :], ALU.mult)
            d_int = sc[:, 0, :].bitcast(I32)
            g.iota(d_int, pattern=[[-1, 2 * WIN]], base=WIN, channel_multiplier=1)
            pool.drain()
            g.tensor_copy(dist[:, :], d_int)
            pool.drain()
            g.affine_select(out=dist[:, :], in_=dist[:, :], compare_op=ALU.is_ge, fill=FAR,
                            base=WIN, pattern=[[-1, 2 * WIN]], channel_multiplier=1)
            pool.drain()
            g.affine_select(out=dist[:, :], in_=dist[:, :], compare_op=ALU.is_ge, fill=FAR,
                            base=0, pattern=[[1, 2 * WIN]], channel_multiplier=-1)
            pool.drain()
            g.tensor_copy(dist_old[:, :], dist[:, 0:WIN])
            pool.drain()
            g.memset(dist[:, 0:WIN], FAR)
            pool.drain()
            pool.sem_inc(s["consts"], 1)
            pool.sem_inc(s["tile_free"], 1)
            pool.wait_ge(s["conv_ps"], 4)
            g.memset(s2s[:, :, :, :], 0.0)
            g.memset(kgm[:, :, :, :], 0.0)
            g.memset(qgm[:, :, :, :], 0.0)
            pool.drain()
            pool.sem_inc(s["over_clear"], 1)

        @block.tensor
        def _(pe):
            t = nc.tensor
            pe.wait_ge(s["consts"], 1)
            pe.wait_ge(s["w_in_in"], 16 * (KD + 2 * GRP + 1))

            def tile(i, r, sampled):
                pe.wait_ge(s["xn_ready"], i + 1)
                for k in range(KD):
                    m = t.transpose(bank[k // 4][:, (k % 4) * P:(k % 4) * P + r], xn[0:r, k * P:(k + 1) * P], ident[0:r, 0:r])
                m.then_inc(s["xT_ps"], 1)
                pe.wait_ge(s["aT_ready"], i + 1)
                for b in range(3):
                    for c in range(4):
                        w = C_DN + (b * 4 + c) * P
                        for k in range(KD):
                            m = t.matmul(bank[4 + b][:, c * P:c * P + r], w_in[:, k, w:w + P], aT[:, k, 0:r],
                                         start=(k == 0), stop=(k == KD - 1))
                    m.then_inc(s["dqkv_ps"], 1)
                for k in range(KD):
                    m = t.matmul(bank[3][0:r, 384:400], aT[:, k, 0:r], w_in[:, k, C_AB:INW],
                                 start=(k == 0), stop=(k == KD - 1))
                m.then_inc(s["ab_ps"], 1)
                for k in range(KD):
                    m = t.matmul(bank[7][0:r, :], aT[:, k, 0:r], w_in[:, k, C_Z:C_AB],
                                 start=(k == 0), stop=(k == KD - 1))
                m.then_inc(s["z_ps"], 1)
                for c in range(GRP):
                    for k in range(KD):
                        t.matmul(bank[2][:, c * P:c * P + r], w_in[:, k, c * P:(c + 1) * P], aT[:, k, 0:r],
                                 start=(k == 0), stop=(k == KD - 1))
                pe.wait_ge(s["soft_in"], i + 1)
                for k in range(KD):
                    t.matmul(bank[3][0:r, 0:256], aT[:, k, 0:r], w_in[:, k, C_K:C_DN],
                             start=(k == 0), stop=(k == KD - 1))
                for k in range(KD):
                    m = t.matmul(bank[3][:, 256:256 + r], w_in[:, k, C_K:C_K + P], aT[:, k, 0:r],
                                 start=(k == 0), stop=(k == KD - 1))
                m.then_inc(s["qkv_ps"], 1)
                if not sampled:
                    pe.wait_ge(s["qkv_sb"], i + 1)
                    for hh in range(AH):
                        g, p = divmod(hh, GRP)
                        m = t.matmul(bank[hh // 2][:, (hh % 2) * 256:(hh % 2) * 256 + 256],
                                     qT[g * HD:(g + 1) * HD, p, :], kT[g * HD:(g + 1) * HD, :], start=True, stop=True)
                    m.then_inc(s["score_ps"], 1)
                else:
                    pe.wait_ge(s["qkv_sb"], i + 1)
                    for b in range(3):
                        for k in range(KD):
                            m = t.matmul(bank[b][0:r, :], aT[:, k, 0:r], w_in[:, k, C_DN + b * 512:C_DN + (b + 1) * 512],
                                         start=(k == 0), stop=(k == KD - 1))
                        m.then_inc(s["conv_ps"], 1)
                    pe.wait_ge(s["stc_in"], 16)
                    for c in range(CB):
                        m = t.transpose(bank[3][:, c * 24:(c + 1) * 24], stconv[:, c * P:(c + 1) * P], ident[0:24, 0:24])
                    m.then_inc(s["stc_ps"], 1)
                pe.wait_ge(s["silu_done"], i + 1)
                for c in range(CB):
                    m = t.transpose(bank[4 + c // 4][0:r, (c % 4) * P:(c % 4 + 1) * P], cs[:, c, 0:r], ident[:, :])
                m.then_inc(s["rows_ps"], 1)
                pe.wait_ge(s["gate_ready"], i + 1)
                pe.wait_ge(s["zsilu"], i + 1)
                cum = tri8 if sampled else tri
                same = same8 if sampled else ones
                t.matmul(bank[7][0:r, 0:DH], cum[0:r, 0:r], gt[0:r, 5, :], start=True, stop=True)
                t.matmul(bank[7][0:r, DH:2 * DH], same[0:r, 0:r], gt[0:r, 5, :], start=True, stop=True)
                if sampled:
                    pe.wait_ge(s["mm_masked"], 1)
                    m = t.matmul(bank[7][:, 64:128], ones[0:r, :], gmb[0:r, :, :], start=True, stop=True)
                    pe.wait_ge(s["conv_sb"], 2)
                else:
                    m = t.matmul(bank[7][:, 64:64 + DH], ones[0:r, :], gt[0:r, 5, :], start=True, stop=True)
                    pe.wait_ge(s["sc_ready"], i + 1)
                for hh in range(DH):
                    m = t.matmul(bank[hh // 4][0:r, (hh % 4) * P:(hh % 4) * P + r],
                                 gt[0:r, 5, hh:hh + 1].to_broadcast([r, r]), cum[0:r, 0:r], start=True, stop=True)
                m.then_inc(s["gsum_ps"], 1)
                if not sampled:
                    pe.wait_ge(s["probs_ready"], i + 1)
                    pe.wait_ge(s["e_in"], i + 1)
                    for hh in range(AH):
                        for b in range(2):
                            m = t.transpose(bank[hh // 2][:, ((hh % 2) * 2 + b) * P:((hh % 2) * 2 + b + 1) * P],
                                            sc[:, hh, b * P:(b + 1) * P], ident[:, :])
                    m.then_inc(s["pT_ps"], 1)
                pe.wait_ge(s["drow_ready"], i + 1)
                for n, b in ((1, 4), (2, 5), (0, 6), (3, 7)):
                    for c in range(4):
                        m = t.transpose(bank[b][:, c * P:c * P + r], rows[0:r, n, c * P:(c + 1) * P], ident[0:r, 0:r])
                m.then_inc(s["rT_ps"], 1)
                if not sampled:
                    pe.wait_ge(s["pT_sb"], i + 1)
                for c in range(4):
                    m = t.transpose(bank[0][:, c * P:c * P + r], rows[0:r, 4, c * P:(c + 1) * P], ident[0:r, 0:r])
                m.then_inc(s["rT_ps"], 1)
                if not sampled:
                    for hh in range(AH):
                        g, p = divmod(hh, GRP)
                        for b, v in enumerate((v_old[:, :], kv[:, 1, :])):
                            m = t.matmul(bank[1][g * HD:(g + 1) * HD, p * P:(p + 1) * P],
                                         v[:, g * HD:(g + 1) * HD], pT[:, hh, b, :], start=(b == 0), stop=(b == 1))
                    m.then_inc(s["att_ps"], 1)
                pe.wait_ge(s["rT_a"], i + 1)
                pe.wait_ge(s["rT_v"], i + 1)
                for hh in range(DH):
                    c, o = hh // 2, (hh % 2) * HD
                    t.matmul(bank[2 + hh % 2][0:r, c * P:c * P + r],
                             rT[o:o + HD, 1, c, 0:r], rT[o:o + HD, 2, c, 0:r], start=True, stop=True)
                    m = t.matmul(bank[4 + hh % 2][0:r, c * P:c * P + r],
                                 rT[o:o + HD, 1, c, 0:r], rT[o:o + HD, 0, c, 0:r], start=True, stop=True)
                m.then_inc(s["gram_ps"], 1)
                if sampled:
                    pe.wait_ge(s["kmask_ready"], 1)
                    pe.wait_ge(s["state_in"], 16 * 2 * DB)
                    for c in range(PAIRS):
                        for b in range(DB):
                            m = t.matmul(bank[6][0:r, c * P:(c + 1) * P], kgm[:, b, c, :], s2s[:, b, c, :],
                                         start=(b == 0), stop=(b == DB - 1))
                else:
                    for c in range(PAIRS):
                        m = t.matmul(bank[6][0:r, c * P:(c + 1) * P], rT[:, 3, c, 0:r], s2[:, c, :], start=True, stop=True)
                m.then_inc(s["kgs_ps"], 1)
                n_lv = 3 if sampled else len(LEVELS) - 1
                if not sampled:
                    pe.wait_ge(s["att_sb"], i + 1)
                for n in range(n_lv):
                    pe.wait_ge(s["b_ready"], NB * i + n + 1)
                    if n:
                        pe.wait_ge(s["xx_ready"], NX * i + n)
                    for hh in range(DH):
                        rhs = xx[0:r, hh, 0, 0:r] if n else ident[0:r, 0:r]
                        m = t.matmul(bank[hh // 4][0:r, (hh % 4) * P:(hh % 4) * P + r], bt[0:r, hh, 0:r], rhs,
                                     start=True, stop=True)
                    m.then_inc(s["t_ps"], 1)
                    if n:
                        pe.wait_ge(s["t_sb"], (NX - 1) * i + n)
                        for hh in range(DH):
                            b, o = 2 + hh // 2, (hh % 2) * 256
                            t.matmul(bank[b][0:r, o:o + r], xx[0:r, hh, 1, 0:r], t1[0:r, hh, 0:r], start=True, stop=True)
                            m = t.matmul(bank[b][0:r, o + P:o + P + r], t1[0:r, hh, 0:r], xx[0:r, hh, 1, 0:r], start=True, stop=True)
                        m.then_inc(s["zz_ps"], 1)
                pe.wait_ge(s["y0_ready"], i + 1)
                pe.wait_ge(s["xx_ready"], NX * i + n_lv)

                def heads(b, lhs, rhs, done):
                    for hh in range(DH):
                        m = t.matmul(bank[b][0:r, hh * HD:(hh + 1) * HD], lhs(hh), rhs[0:r, hh * HD:(hh + 1) * HD],
                                     start=True, stop=True)
                    m.then_inc(done, 1)

                heads(6, lambda hh: xx[0:r, hh, 1, 0:r], y0, s["y1_ps"])
                if not sampled:
                    pe.wait_ge(s["b_ready"], NB * i + NB)
                    pe.wait_ge(s["y1_sb"], i + 1)
                    heads(7, lambda hh: bt[0:r, hh, 0:r], y1, s["ty_ps"])
                    pe.wait_ge(s["ty_sb"], i + 1)
                    heads(6, lambda hh: xx[0:r, hh, 1, 0:r], ty, s["yz_ps"])
                pe.wait_ge(s["vn_ready"], i + 1)
                for c in range(PAIRS):
                    o = bank[0][0:r, c * P:(c + 1) * P]
                    if sampled:
                        for b in range(DB):
                            t.matmul(o, qgm[:, b, c, :], s2s[:, b, c, :], start=(b == 0), stop=False)
                    else:
                        t.matmul(o, rT[:, 4, c, 0:r], s2[:, c, :], start=True, stop=False)
                    for e in range(2):
                        hh = 2 * c + e
                        m = t.matmul(bank[0][0:r, hh * HD:(hh + 1) * HD], qk[0:r, hh, 0:r],
                                     vn[0:r, hh * HD:(hh + 1) * HD], start=False, stop=(e == 1))
                m.then_inc(s["o_ps"], 1)
                if sampled:
                    for b in range(DB):
                        pe.wait_ge(s["ktm_ready"], b + 1)
                        if b >= 2:
                            pe.wait_ge(s["supd_done"], b - 1)
                        for c in range(PAIRS):
                            m = t.matmul(bank[1 + b % 2][:, c * P:(c + 1) * P], ktm[0:r, b % 2, c * P:(c + 1) * P],
                                         vn[0:r, c * P:(c + 1) * P], start=True, stop=True)
                        m.then_inc(s["supd_ps"], 1)
                else:
                    for c in range(PAIRS):
                        m = t.matmul(bank[1][:, c * P:(c + 1) * P], rows[0:r, 5, c * P:(c + 1) * P],
                                     vn[0:r, c * P:(c + 1) * P], start=True, stop=True)
                    m.then_inc(s["upd_ps"], 1)
                pe.wait_ge(s["dn_ready"], i + 1)
                if sampled:
                    sampled_attention()
                for c in range(4):
                    m = t.transpose(bank[3][:, c * P:c * P + r], dn[0:r, c * P:(c + 1) * P], ident[0:r, 0:r])
                m.then_inc(s["dnT_ps"], 1)
                pe.wait_ge(s["dnT_sb"], i + 1)
                pe.wait_ge(s["w_out_in"], 16 * 9)
                for n in range(2):
                    for k in range(KD):
                        m = t.matmul(bank[4 + n][0:r, :], mT[:, k, 0:r], w_out[:, k, n * 512:(n + 1) * 512],
                                     start=(k == 0), stop=(k == KD - 1))
                m.then_inc(s["proj_ps"], 1)

            def sampled_attention():
                pe.wait_ge(s["cache_in"], 32)
                for b in range(DB):
                    m = t.transpose(bank[1 + b // 4][:, (b % 4) * P:(b % 4 + 1) * P], kc[:, b, :], ident[:, :])
                m.then_inc(s["kcT_ps"], 1)
                pe.wait_ge(s["kcT_sb"], 1)
                for b in range(DB):
                    for g in range(2):
                        o = (b % 3) * SKEYS
                        q = qT[:, :, :].rearrange("p c t -> p (c t)")[g * HD:(g + 1) * HD, b * GRP * DS:(b + 1) * GRP * DS]
                        bk = bank[1 + 3 * g + b // 3]
                        t.matmul(bk[0:GRP * DS, o:o + WIN], q, kcT[g * HD:(g + 1) * HD, b, :], start=True, stop=True)
                        m = t.matmul(bk[0:GRP * DS, o + WIN:o + SKEYS], q,
                                     kT[g * HD:(g + 1) * HD, P + b * DS:P + (b + 1) * DS], start=True, stop=True)
                m.then_inc(s["score_ps"], 1)
                pe.wait_ge(s["sprobs"], 1)
                for n in range(2 * DB):
                    t.transpose(bank[1][:, n * 32:(n + 1) * 32], ssc[0:32, n, 0:WIN], ident[0:32, 0:32])
                    m = t.transpose(bank[2][0:DS, n * 32:(n + 1) * 32], ssc[0:32, n, WIN:SKEYS], ident[0:32, 0:32])
                m.then_inc(s["pT_ps"], 1)
                pe.wait_ge(s["pT_sb"], TILES + 1)
                pe.wait_ge(s["vnew_in"], 16 * DB)
                for b in range(DB):
                    for g in range(2):
                        n = b * 2 + g
                        o = bank[3][g * HD:(g + 1) * HD, n * 32 % 512 - g * 32:n * 32 % 512 - g * 32 + 32]
                        t.matmul(o, vc[:, b, g * HD:(g + 1) * HD], spT[:, n, :], start=True, stop=False)
                        m = t.matmul(o, vnew[0:DS, b, g * HD:(g + 1) * HD], spTn[0:DS, n, :], start=False, stop=True)
                m.then_inc(s["att_ps"], 1)
                pe.wait_ge(s["att_sb"], TILES + 1)

            NB = len(LEVELS)
            NX = len(LEVELS) - 1
            with pe.Fori(0, TILES) as i:
                tile(i, P, False)
            for b in range(3):
                for k in range(KD):
                    m = t.matmul(bank[b][0:3, :], a_tail[:, k, :], w_in[:, k, C_DN + b * 512:C_DN + (b + 1) * 512],
                                 start=(k == 0), stop=(k == KD - 1))
            m.then_inc(s["conv_ps"], 1)
            tile(TILES, NS, True)

        @block.scalar
        def _(act):
            ac = nc.scalar
            act.wait_ge(s["consts"], 1)
            act.wait_ge(s["const_in"], 16 * (6 + 1 + TAPS + AH))
            ac.activation(neg_a[:, :], neg_a[:, :], ACT.Exp)
            act.drain()
            ac.mul(neg_a[:, :], neg_a[:, :], -1.0)

            def tile(i, r, sampled):
                act.wait_ge(s["x_in"], 16 * (i + 1))
                ac.activation(aT[0:r, :, :].rearrange("p k t -> p (k t)"), x[0:r, :], ACT.Square, accum_out=st[0:r, 0:1])
                act.drain()
                ac.activation(st[0:r, 1:2], st[0:r, 0:1], ACT.Sqrt, scale=1.0 / D, bias=eps[0:r, :]).then_inc(s["rms"], 1)
                for b in range(3):
                    act.wait_ge(s["dqkv_ps"], 3 * i + b + 1)
                    if sampled:
                        src = bank[4 + b][:, :].rearrange("p (c t) -> p c t", c=4)[:, :, 0:r].rearrange("p c (q t) -> p c q t", t=DS)
                        for c in range(4):
                            dst = cin[:, b * 4 + c, 0:DB * 11].rearrange("p (q t) -> p q t", t=11)[:, :, 3:11]
                            m = ac.activation(dst, src[:, c], ACT.Copy)
                    else:
                        m = ac.activation(cin[:, b * 4:b * 4 + 4, 3:3 + P],
                                          bank[4 + b][:, :].rearrange("p (c t) -> p c t", c=4), ACT.Copy)
                    m.then_inc(s["cin_ready"], 1)
                act.wait_ge(s["soft_in"], i + 1)
                ac.activation(gt[0:r, 2, :], gt[0:r, 1, :], ACT.Exp, scale=-1.0)
                ac.activation(gt[0:r, 3, :], gt[0:r, 3, :], ACT.Exp, scale=-1.0)
                act.drain()
                ac.activation(gt[0:r, 2, :], gt[0:r, 2, :], ACT.Ln, bias=one[0:r, :]).then_inc(s["soft_out"], 1)
                act.wait_ge(s["z_ps"], i + 1)
                ac.activation(zs[0:r, :], bank[7][0:r, :], ACT.Silu).then_inc(s["zsilu"], 1)
                act.wait_ge(s["qkv_ps"], i + 1)
                if sampled:
                    act.wait_ge(s["state_out"], 16 * (2 + DH))
                if sampled:
                    for p in range(GRP):
                        ac.activation(qT_s[:, :, p, :], bank[2][:, p * P:p * P + NS].rearrange("p (b t) -> p b t", b=DB), ACT.Copy, scale=HD ** -0.5)
                else:
                    ac.activation(qT[:, :, 0:r], bank[2][:, :].rearrange("p (c t) -> p c t", c=GRP)[:, :, 0:r], ACT.Copy, scale=HD ** -0.5)
                ac.activation(kT[:, P:P + r], bank[3][:, 256:256 + r], ACT.Copy)
                ac.activation(kv[0:r, :, :], bank[3][0:r, 0:256].rearrange("p (c t) -> p c t", c=2), ACT.Copy).then_inc(s["qkv_sb"], 1)
                if sampled:
                    act.wait_ge(s["over_clear"], 1)
                    act.wait_ge(s["conv_ps"], 4)
                    for b in range(3):
                        m = ac.activation(crow[0:r, b * 512:(b + 1) * 512], bank[b][0:r, :], ACT.Copy)
                    m.then_inc(s["conv_sb"], 1)
                    act.wait_ge(s["stc_ps"], 1)
                    for c in range(CB):
                        m = ac.activation(cin[:, c, 0:DB * 11].rearrange("p (q t) -> p q t", t=11)[:, :, 0:3],
                                          bank[3][:, c * 24:(c + 1) * 24].rearrange("p (q t) -> p q t", t=3), ACT.Copy)
                    m.then_inc(s["stc_sb"], 1)
                act.wait_ge(s["conv_done"], i + 1)
                ac.activation(cs[:, :, 0:r], cacc[:, :, 0:r], ACT.Silu).then_inc(s["silu_done"], 1)
                act.wait_ge(s["rows_ps"], i + 1)
                for n in range(2):
                    m = ac.activation(sq[0:r, n * 512:(n + 1) * 512], bank[4 + n][0:r, :], ACT.Square)
                m.then_inc(s["sq_done"], 1)
                act.wait_ge(s["ssq_done"], i + 1)
                ac.activation(rn[0:r, 1, :], rn[0:r, 0, :], ACT.Sqrt, bias=eps[0:r, :]).then_inc(s["rn_sqrt"], 1)
                if not sampled:
                    act.wait_ge(s["nm_ready"], i + 1)
                    for hh in range(AH):
                        ac.activation(sc[:, hh, :], sc[:, hh, :], ACT.Exp, bias=am[:, 2, hh:hh + 1], accum_out=am[:, 4, hh:hh + 1])
                    act.drain()
                    ac.activation(am[:, 3, :], am[:, 3, :], ACT.Exp).then_inc(s["prob_done"], 1)
                act.wait_ge(s["e_in"], i + 1)
                ac.activation(gt[0:r, 8, :], gt[0:r, 6, :], ACT.Exp)
                ac.activation(gt[0:r, 9, :], gt[0:r, 7, :], ACT.Exp)
                if sampled:
                    ac.activation(egb[:, :, :], egb[:, :, :], ACT.Exp)
                else:
                    ac.activation(eg[:, :], eg[:, :], ACT.Exp)
                ac.activation(dt_[0:r, :, 0:r], dt_[0:r, :, 0:r], ACT.Exp).then_inc(s["exp_ready"], 1)
                if not sampled:
                    act.wait_ge(s["pT_ps"], i + 1)
                    for b in range(4):
                        m = ac.activation(pT[:, 2 * b:2 * b + 2, :, :], bank[b][:, :].rearrange("p (h c t) -> p h c t", h=2, c=2), ACT.Copy)
                    m.then_inc(s["pT_sb"], 1)
                act.wait_ge(s["rT_ps"], 2 * i + 2)
                for n, b in ((1, 4), (2, 5), (4, 0)):
                    m = ac.activation(rT[:, n, :, 0:r], bank[b][:, :].rearrange("p (c t) -> p c t", c=4)[:, :, 0:r], ACT.Copy)
                m.then_inc(s["rT_a"], 1)
                if not sampled:
                    act.wait_ge(s["att_ps"], i + 1)
                    ac.activation(mT[:, 0:4, :], bank[1][:, :].rearrange("p (c t) -> p c t", c=4), ACT.Copy)
                    ac.activation(kT[:, 0:P], kT[:, P:2 * P], ACT.Copy)
                    ac.activation(v_old[:, :], kv[:, 1, :], ACT.Copy)
                    ac.activation(dist[:, 0:WIN], dist_old[:, :], ACT.Copy).then_inc(s["att_sb"], 1)
                n_lv = 3 if sampled else len(LEVELS) - 1
                for n in range(1, n_lv):
                    act.wait_ge(s["t_ps"], NX * i + n + 1)
                    for b in range(2):
                        m = ac.activation(t1[0:r, 4 * b:4 * b + 4, 0:r],
                                          bank[b][0:r, :].rearrange("p (c t) -> p c t", c=4)[:, :, 0:r], ACT.Copy)
                    m.then_inc(s["t_sb"], 1)
                if not sampled:
                    act.wait_ge(s["y1_ps"], i + 1)
                    ac.activation(y1[0:r, :], bank[6][0:r, :], ACT.Copy).then_inc(s["y1_sb"], 1)
                    act.wait_ge(s["ty_ps"], i + 1)
                    ac.activation(ty[0:r, :], bank[7][0:r, :], ACT.Copy).then_inc(s["ty_sb"], 1)
                act.wait_ge(s["o_ps"], i + 1)
                ac.activation(sq[0:r, 0:512], bank[0][0:r, :], ACT.Square).then_inc(s["osq_done"], 1)
                act.wait_ge(s["ossq"], i + 1)
                ac.activation(rn[0:r, 1, 0:DH], rn[0:r, 0, 0:DH], ACT.Sqrt, scale=1.0 / HD, bias=eps[0:r, :]).then_inc(s["orms"], 1)
                if sampled:
                    act.wait_ge(s["kcT_ps"], 1)
                    for b in range(2):
                        m = ac.activation(kcT[:, 4 * b:4 * b + 4, :], bank[1 + b][:, :].rearrange("p (c t) -> p c t", c=4), ACT.Copy)
                    m.then_inc(s["kcT_sb"], 1)
                    act.wait_ge(s["nm_ready"], TILES + 1)
                    ac.activation(ssc[0:32, :, :], ssc[0:32, :, :], ACT.Exp)
                    ac.activation(sm[0:32, 3, :], sm[0:32, 3, :], ACT.Exp).then_inc(s["sexp"], 1)
                    act.wait_ge(s["pT_ps"], TILES + 1)
                    ac.activation(spT[:, :, :], bank[1][:, :].rearrange("p (n r) -> p n r", r=32), ACT.Copy)
                    ac.activation(spTn[0:DS, :, :], bank[2][0:DS, :].rearrange("p (n r) -> p n r", r=32), ACT.Copy).then_inc(s["pT_sb"], 1)
                    act.wait_ge(s["att_ps"], TILES + 1)
                    for p in range(GRP):
                        src = bank[3][:, :].rearrange("p (b g r) -> p b g r", b=DB, g=2)[:, :, 0, p * DS:(p + 1) * DS]
                        m = ac.activation(mT[:, p, 0:NS].rearrange("p (b t) -> p b t", b=DB), src, ACT.Copy)
                    m.then_inc(s["att_sb"], 1)
                act.wait_ge(s["dnT_ps"], i + 1)
                ac.activation(mT[:, 4:8, 0:r], bank[3][:, :].rearrange("p (c t) -> p c t", c=4)[:, :, 0:r], ACT.Copy).then_inc(s["dnT_sb"], 1)

            NX = len(LEVELS) - 1
            with act.Fori(0, TILES) as i:
                tile(i, P, False)
            act.wait_ge(s["conv_ps"], 1)
            for b in range(3):
                m = ac.activation(stage3[0:3, b * 512:(b + 1) * 512], bank[b][0:3, :], ACT.Copy)
            m.then_inc(s["conv_sb"], 1)
            act.wait_ge(s["conv_sb"], 1)
            act.dma_start(out["c_p"][0, 0], stage3[0:3, :]).then_inc(s["misc_in"], 16)
            act.wait_ge(s["misc_in"], 16)
            tile(TILES, NS, True)

        @block.vector
        def _(dve):
            v = nc.vector

            def bc(ap, n):
                sh = list(ap.shape)
                return ap.rearrange("p (h o) -> p h o", o=1).to_broadcast([sh[0], sh[1], n])

            def hd(ap):
                return ap.rearrange("p (h d) -> p h d", d=HD)

            dve.wait_ge(s["consts"], 1)
            dve.wait_ge(s["const_in"], 16 * (6 + 1 + TAPS + AH))

            def tile(i, r, sampled):
                dve.wait_ge(s["rms"], i + 1)
                v.reciprocal(st[0:r, 2:3], st[0:r, 1:2])
                dve.drain()
                v.tensor_scalar(xn[0:r, :], x[0:r, :], st[0:r, 2:3], None, ALU.mult).then_inc(s["xn_ready"], 1)
                dve.wait_ge(s["xT_ps"], i + 1)
                for b in range(2):
                    m = v.tensor_tensor(aT[:, 4 * b:4 * b + 4, 0:r], bank[b][:, :].rearrange("p (k t) -> p k t", k=4)[:, :, 0:r],
                                        bc(g_mix[:, 4 * b:4 * b + 4], r), ALU.mult)
                if not sampled:
                    dve.drain()
                    m = v.tensor_copy(a_tail[:, :, :], aT[:, :, P - TAPS + 1:P])
                m.then_inc(s["aT_ready"], 1)
                dve.wait_ge(s["ab_ps"], i + 1)
                v.tensor_tensor(gt[0:r, 0, :], bank[3][0:r, 384:384 + DH], dtb[0:r, :], ALU.add)
                v.tensor_copy(gt[0:r, 3, :], bank[3][0:r, 384 + DH:400])
                dve.drain()
                v.tensor_scalar(gt[0:r, 1, :], gt[0:r, 0, :], -1.0, None, ALU.mult)
                dve.drain()
                v.tensor_tensor(gt[0:r, 1, :], gt[0:r, 0, :], gt[0:r, 1, :], ALU.max).then_inc(s["soft_in"], 1)
                dve.wait_ge(s["cin_ready"], 3 * i + 3)
                if sampled:
                    dve.wait_ge(s["stc_sb"], 1)
                for j in range(TAPS):
                    for c in range(CB):
                        if sampled:
                            src = cin[:, c, 0:DB * 11].rearrange("p (q t) -> p q t", t=11)[:, :, j:j + DS]
                            dst = cacc[:, c, 0:NS].rearrange("p (q t) -> p q t", t=DS)
                        else:
                            src, dst = cin[:, c, j:j + P], cacc[:, c, :]
                        if j == 0:
                            m = v.tensor_scalar(dst, src, cw[:, j, c:c + 1], None, ALU.mult)
                        else:
                            m = v.scalar_tensor_tensor(dst, src, cw[:, j, c:c + 1], dst, ALU.mult, ALU.add)
                    if j < TAPS - 1:
                        dve.drain()
                m.then_inc(s["conv_done"], 1)
                if not sampled:
                    dve.drain()
                    v.tensor_copy(cin[:, :, 0:TAPS - 1], cin[:, :, P:P + TAPS - 1])
                dve.wait_ge(s["soft_out"], i + 1)
                v.tensor_scalar(gt[0:r, 0, :], gt[0:r, 0, :], 0.0, None, ALU.max)
                v.tensor_scalar(gt[0:r, 3, :], gt[0:r, 3, :], 1.0, None, ALU.add)
                dve.drain()
                v.tensor_tensor(gt[0:r, 0, :], gt[0:r, 0, :], gt[0:r, 2, :], ALU.add)
                v.reciprocal(gt[0:r, 4, :], gt[0:r, 3, :])
                dve.drain()
                v.tensor_tensor(gt[0:r, 5, :], gt[0:r, 0, :], neg_a[0:r, :], ALU.mult).then_inc(s["gate_ready"], 1)
                if sampled:
                    dve.drain()
                    dve.wait_ge(s["over_clear"], 1)
                    v.tensor_tensor(gmb[0:r, :, :], gt[0:r, 5, :].rearrange("p (o h) -> p o h", o=1).to_broadcast([r, DB, DH]),
                                    bc(seq_of[0:r, :], DH), ALU.mult).then_inc(s["mm_masked"], 1)
                if not sampled:
                    dve.wait_ge(s["score_ps"], i + 1)
                    for hh in range(AH):
                        m = v.scalar_tensor_tensor(sc[:, hh, :], dist[:, :], SLOPE[hh],
                                                   bank[hh // 2][:, (hh % 2) * 256:(hh % 2 + 1) * 256], ALU.mult, ALU.add)
                    m.then_inc(s["sc_ready"], 1)
                    dve.drain()
                    v.tensor_reduce(am[:, 0, :], sc[:, :, :], AXX, ALU.max)
                    dve.drain()
                    v.tensor_tensor(am[:, 1, :], am[:, 0, :], sinks[:, :], ALU.max)
                    dve.drain()
                    v.tensor_tensor(am[:, 3, :], sinks[:, :], am[:, 1, :], ALU.subtract)
                    v.tensor_scalar(am[:, 2, :], am[:, 1, :], -1.0, None, ALU.mult).then_inc(s["nm_ready"], 1)
                dve.wait_ge(s["sq_done"], i + 1)
                v.tensor_reduce(rn[0:r, 0, :], hd(sq[0:r, :]), AXX, ALU.add).then_inc(s["ssq_done"], 1)
                dve.wait_ge(s["gsum_ps"], i + 1)
                v.tensor_copy(gt[0:r, 6, :], bank[7][0:r, 0:DH])
                dve.drain()
                v.tensor_tensor(gt[0:r, 7, :], bank[7][0:r, DH:2 * DH], gt[0:r, 6, :], ALU.subtract)
                for c in range(2):
                    if sampled:
                        v.tensor_copy(egb[c * HD:(c + 1) * HD, :, :],
                                      bank[7][c * HD:(c + 1) * HD, 64:128].rearrange("p (b h e) -> p b h e", b=DB, e=2)[:, :, :, c])
                    else:
                        v.tensor_copy(eg[c * HD:(c + 1) * HD, :],
                                      bank[7][c * HD:(c + 1) * HD, 64:64 + DH].rearrange("p (h e) -> p h e", e=2)[:, :, c])
                for hh in range(DH):
                    m = v.tensor_scalar(dt_[0:r, hh, 0:r], bank[hh // 4][0:r, (hh % 4) * P:(hh % 4) * P + r],
                                        gt[0:r, 6, hh:hh + 1], 0.0, ALU.subtract, ALU.min)
                m.then_inc(s["e_in"], 1)
                if not sampled:
                    dve.wait_ge(s["prob_done"], i + 1)
                    v.tensor_tensor(am[:, 5, :], am[:, 4, :], am[:, 3, :], ALU.add)
                    dve.drain()
                    v.reciprocal(am[:, 0, :], am[:, 5, :])
                    dve.drain()
                    v.tensor_tensor(sc[:, :, :], sc[:, :, :], bc(am[:, 0, :], 2 * WIN), ALU.mult).then_inc(s["probs_ready"], 1)
                dve.wait_ge(s["rn_sqrt"], i + 1)
                v.reciprocal(rn[0:r, 2, :], rn[0:r, 1, :])
                dve.drain()
                dve.wait_ge(s["exp_ready"], i + 1)
                v.tensor_scalar(gt[0:r, 10, :], rn[0:r, 2, 0:DH], HD ** -0.5, None, ALU.mult)
                v.tensor_tensor(gt[0:r, 11, :], rn[0:r, 2, DH:16], gt[0:r, 4, :], ALU.mult)
                v.tensor_tensor(gt[0:r, 7, :], rn[0:r, 2, DH:16], gt[0:r, 9, :], ALU.mult)
                dve.drain()
                v.tensor_tensor(gt[0:r, 0, :], gt[0:r, 11, :], gt[0:r, 8, :], ALU.mult)
                v.tensor_tensor(gt[0:r, 1, :], gt[0:r, 10, :], gt[0:r, 8, :], ALU.mult)
                dve.drain()
                for n, b, f in ((1, 5, rn[0:r, 2, DH:16]), (2, 5, gt[0:r, 11, :]), (0, 4, gt[0:r, 10, :]),
                                (3, 5, gt[0:r, 0, :]), (4, 4, gt[0:r, 1, :]), (5, 5, gt[0:r, 7, :])):
                    v.tensor_tensor(hd(rows[0:r, n, :]), hd(bank[b][0:r, :]), bc(f, HD), ALU.mult)
                v.tensor_tensor(hd(vb[0:r, :]), hd(bank[6][0:r, :]), bc(gt[0:r, 4, :], HD), ALU.mult).then_inc(s["drow_ready"], 1)
                cum = tri8 if sampled else tri
                v.tensor_tensor(dt_[0:r, :, 0:r], dt_[0:r, :, 0:r],
                                cum[0:r, 0:r].rearrange("p (o t) -> p o t", o=1).to_broadcast([r, DH, r]), ALU.mult)
                dve.wait_ge(s["rT_ps"], 2 * i + 1)
                for n, b in ((0, 6), (3, 7)):
                    m = v.tensor_copy(rT[:, n, :, 0:r], bank[b][:, :].rearrange("p (c t) -> p c t", c=4)[:, :, 0:r])
                m.then_inc(s["rT_v"], 1)
                if sampled:
                    dve.drain()
                    dve.wait_ge(s["rT_a"], TILES + 1)
                    for b in range(DB):
                        v.tensor_copy(kgm[:, b, :, b * DS:(b + 1) * DS], rT[:, 3, :, b * DS:(b + 1) * DS])
                        m = v.tensor_copy(qgm[:, b, :, b * DS:(b + 1) * DS], rT[:, 4, :, b * DS:(b + 1) * DS])
                    m.then_inc(s["kmask_ready"], 1)
                dve.wait_ge(s["gram_ps"], i + 1)
                for b in range(2):
                    v.tensor_tensor(lt[0:r, b:DH:2, 0:r], bank[2 + b][0:r, :].rearrange("p (c t) -> p c t", c=4)[:, :, 0:r],
                                    dt_[0:r, b:DH:2, 0:r], ALU.mult)
                    v.tensor_tensor(qk[0:r, b:DH:2, 0:r], bank[4 + b][0:r, :].rearrange("p (c t) -> p c t", c=4)[:, :, 0:r],
                                    dt_[0:r, b:DH:2, 0:r], ALU.mult)
                dve.drain()

                def cut(n):
                    v.tensor_tensor(bt[0:r, :, 0:r], lt[0:r, :, 0:r],
                                    level[0:r, n, 0:r].rearrange("p (o t) -> p o t", o=1).to_broadcast([r, DH, r]),
                                    ALU.mult).then_inc(s["b_ready"], 1)

                cut(0)
                dve.wait_ge(s["kgs_ps"], i + 1)
                v.tensor_tensor(y0[0:r, :], vb[0:r, :], bank[6][0:r, :], ALU.subtract).then_inc(s["y0_ready"], 1)
                ident_b = ident[0:r, 0:r].rearrange("p (o t) -> p o t", o=1)
                n_lv = 3 if sampled else len(LEVELS) - 1
                for n in range(n_lv):
                    dve.wait_ge(s["t_ps"], NX * i + n + 1)
                    if n == 0:
                        for b in range(2):
                            v.tensor_tensor(xx[0:r, 4 * b:4 * b + 4, 0, 0:r], ident_b.to_broadcast([r, 4, r]),
                                            bank[b][0:r, :].rearrange("p (c t) -> p c t", c=4)[:, :, 0:r], ALU.subtract)
                        m = v.tensor_tensor(xx[0:r, :, 1, 0:r], ident_b.to_broadcast([r, DH, r]), bt[0:r, :, 0:r], ALU.subtract)
                        m.then_inc(s["xx_ready"], 1)
                        dve.drain()
                        cut(n + 1)
                    else:
                        if n + 1 < (n_lv if sampled else n_lv + 1):
                            cut(n + 1)
                        dve.wait_ge(s["zz_ps"], (NX - 1) * i + n)
                        for b in range(4):
                            xv = xx[0:r, 2 * b:2 * b + 2, :, 0:r]
                            zv = bank[2 + b][0:r, :].rearrange("p (h c t) -> p h c t", h=2, c=2)[:, :, :, 0:r]
                            m = v.tensor_tensor(xv, xv, zv, ALU.subtract)
                        m.then_inc(s["xx_ready"], 1)
                if sampled:
                    dve.wait_ge(s["y1_ps"], i + 1)
                    v.tensor_copy(vn[0:r, :], bank[6][0:r, :]).then_inc(s["vn_ready"], 1)
                else:
                    dve.wait_ge(s["yz_ps"], i + 1)
                    v.tensor_tensor(vn[0:r, :], y1[0:r, :], bank[6][0:r, :], ALU.subtract).then_inc(s["vn_ready"], 1)
                    v.tensor_tensor(s2n[:, :, :], s2[:, :, :], bc(eg[:, :], P), ALU.mult)
                if sampled:
                    for b in range(DB):
                        if b >= 2:
                            dve.wait_ge(s["supd_ps"], b - 1)
                        v.tensor_scalar(ktm[0:r, b % 2, :], rows[0:r, 5, :], seq_of[0:r, b:b + 1], None, ALU.mult).then_inc(s["ktm_ready"], 1)
                        if b >= 1:
                            state_update(b - 1)
                    state_update(DB - 1)
                dve.wait_ge(s["osq_done"], i + 1)
                v.tensor_reduce(rn[0:r, 0, 0:DH], hd(sq[0:r, 0:512]), AXX, ALU.add).then_inc(s["ossq"], 1)
                if not sampled:
                    dve.drain()
                    dve.wait_ge(s["upd_ps"], i + 1)
                    for c in range(PAIRS):
                        v.tensor_tensor(s2[:, c, :], bank[1][:, c * P:(c + 1) * P], pair_diag[:, :], ALU.mult)
                    dve.drain()
                    v.tensor_tensor(s2[:, :, :], s2[:, :, :], s2n[:, :, :], ALU.add)
                dve.wait_ge(s["orms"], i + 1)
                v.reciprocal(rn[0:r, 2, 0:DH], rn[0:r, 1, 0:DH])
                dve.drain()
                v.tensor_tensor(hd(dn[0:r, :]), hd(bank[0][0:r, :]), bc(rn[0:r, 2, 0:DH], HD), ALU.mult)
                dve.drain()
                v.tensor_tensor(hd(dn[0:r, :]), hd(dn[0:r, :]),
                                dnn[0:r, :].rearrange("p (o d) -> p o d", o=1).to_broadcast([r, DH, HD]), ALU.mult)
                dve.drain()
                v.tensor_tensor(dn[0:r, :], dn[0:r, :], zs[0:r, :], ALU.mult).then_inc(s["dn_ready"], 1)
                if sampled:
                    sampled_softmax()
                    v.memset(h[NS:P, :], 0.0)
                dve.wait_ge(s["proj_ps"], i + 1)
                dve.wait_ge(s["xres_in"], 16 * (i + 1))
                for n in range(2):
                    m = v.tensor_tensor(h[0:r, n * 512:(n + 1) * 512], x_res[0:r, n * 512:(n + 1) * 512], bank[4 + n][0:r, :], ALU.add)
                m.then_inc(s["h_ready"], 1)
                if not sampled:
                    dve.wait_ge(s["h_out"], 16 * (i + 1))
                    dve.sem_inc(s["tile_free"], 1)

            def state_update(b):
                dve.wait_ge(s["supd_ps"], b + 1)
                if b == 0:
                    dve.wait_ge(s["o_ps"], TILES + 1)
                for c in range(PAIRS):
                    v.tensor_scalar(s2s[:, b, c, :], s2s[:, b, c, :], egb[:, b, c:c + 1], None, ALU.mult)
                    v.tensor_tensor(s2n[:, c, :], bank[1 + b % 2][:, c * P:(c + 1) * P], pair_diag[:, :], ALU.mult)
                dve.drain()
                v.tensor_tensor(s2s[:, b, :, :], s2s[:, b, :, :], s2n[:, :, :], ALU.add).then_inc(s["supd_done"], 1)
                dve.drain()

            def sampled_softmax():
                dve.wait_ge(s["score_ps"], TILES + 1)
                for n in range(2 * DB):
                    v.scalar_tensor_tensor(ssc[0:32, n, :], dist_s[:, :], slope_s[:, n % 2:n % 2 + 1],
                                           bank[1 + 3 * (n % 2) + n // 6][0:32, (n // 2 % 3) * SKEYS:(n // 2 % 3 + 1) * SKEYS], ALU.mult, ALU.add)
                dve.drain()
                v.tensor_reduce(sm[0:32, 0, :], ssc[0:32, :, :], AXX, ALU.max)
                dve.drain()
                sk = sink_s[0:32, :].rearrange("p (o g) -> p o g", o=1).to_broadcast([32, DB, 2])
                as_bg = lambda ap: ap.rearrange("p (b g) -> p b g", g=2)
                v.tensor_tensor(as_bg(sm[0:32, 1, :]), as_bg(sm[0:32, 0, :]), sk, ALU.max)
                dve.drain()
                v.tensor_tensor(as_bg(sm[0:32, 3, :]), sk, as_bg(sm[0:32, 1, :]), ALU.subtract)
                v.tensor_tensor(ssc[0:32, :, :], ssc[0:32, :, :], bc(sm[0:32, 1, :], SKEYS), ALU.subtract).then_inc(s["nm_ready"], 1)
                dve.wait_ge(s["sexp"], 1)
                v.tensor_reduce(sm[0:32, 4, :], ssc[0:32, :, :], AXX, ALU.add)
                dve.drain()
                v.tensor_tensor(sm[0:32, 5, :], sm[0:32, 4, :], sm[0:32, 3, :], ALU.add)
                dve.drain()
                v.reciprocal(sm[0:32, 2, :], sm[0:32, 5, :])
                dve.drain()
                v.tensor_tensor(ssc[0:32, :, :], ssc[0:32, :, :], bc(sm[0:32, 2, :], SKEYS), ALU.mult).then_inc(s["sprobs"], 1)

            NX = len(LEVELS) - 1
            with dve.Fori(0, TILES) as i:
                tile(i, P, False)
            tile(TILES, NS, True)


def peer_block(nc, sems, a, h_rows, h2_rows):
    RING = 8
    STEP = 16
    ON_PE = tuple(range(1, STEP, 2))
    NPE = len(ON_PE)
    with ExitStack() as ctx:
        def sb(name, shape, dt=F32):
            return ctx.enter_context(nc.sbuf_tensor(name, shape, dt))

        def sem(name):
            return sems.enter_context(nc.semaphore("peer_" + name))

        bank = [ctx.enter_context(nc.psum_tensor(f"pbank{b}", [P, 512], F32)) for b in range(8)]
        wq = sb("wq_sb", [P, KD, PH * 2 * P])
        keys = sb("keys_sb", [P, 16, P])
        keysT = sb("keysT_sb", [P, 16, P])
        ident = sb("p_ident", [P, P])
        g_ffn = sb("g_ffn_sb", [P, D])
        iota16 = sb("iota16", [P, TOPK])
        iota_i = sb("iota16i", [P, TOPK], I32)
        eps = sb("p_eps", [P, 1])
        junk = sb("p_junk", [P, D])
        h_nxt = sb("h_nxt", [P, D])
        c_nxt = sb("c_nxt", [P, D])
        h_cur = sb("h_cur", [P, D])
        c_cur = sb("c_cur", [P, D])
        st = sb("p_stats", [P, 4])
        cT = sb("cT_sb", [P, KD, P])
        qT = sb("pqT_sb", [P, 16, P])
        sco = sb("key_scores", [P, 16, P])
        sst = sb("scores_here", [P, 2, P])
        sst2 = sb("scores_left", [P, 2, P])
        v1 = sb("top_val", [P, 2, TOPK])
        x1 = sb("top_idx", [P, 2, TOPK], U32)
        x1f = sb("top_idxf", [P, 2, TOPK])
        cand = sb("cand", [P, TOPK, TOPK])
        cand2 = sb("cand_left", [P, TOPK * TOPK])
        sc16 = sb("best_val", [P, TOPK])
        ci = sb("best_idx", [P, TOPK], U32)
        cab = sb("best_ab", [P, 2, TOPK], U32)
        cabf = sb("best_abf", [P, 2, TOPK])
        eq = sb("onehot", [P, 2, TOPK, TOPK])
        e12 = sb("best_keys", [P, 2, TOPK])
        sc_all = sb("gate_raw", [P, SLOTS])
        gate = sb("gate_all", [P, ALLT * SLOTS])
        idx = sb("expert_all", [P, ALLT * SLOTS], I32)
        gs = sb("gate_sum", [P, 2, PH])
        stage = [sb(f"idx_stage{k}", [P, RING], I32) for k in range(2)]
        rows = sb("expert_rows", [P, RING, D])
        dot16 = sb("dots_here", [P, STEP])
        dots = sb("dots", [P, SLOTS])
        wgt = sb("weights", [P, SLOTS])
        w16 = sb("weights_here", [P, STEP])
        diag = sb("weight_diag", [P, 4, P])
        zero = sb("p_zero", [P, P])

        names = ("p_consts w_in2 keysT_ps keysT_sb h_in rms c_ready cT_ps cT_sb q_ps q_sb s_ps s_sb "
                 "idx_ready gate_sub gate_exp dots_ready gelu_done cur_free h_out cur_ready k_in passed "
                 "passed2 staged diag_ready w_ready act_passed pe_passed vacc_ps vacc_free").split()
        s = {n: sem(n) for n in names}
        got = [sem(f"row_in{k}") for k in range(RING)]
        used = [sem(f"row_used{k}") for k in range(RING)]

        def turn(i, part, j, half):
            return (i * 2 + part) * (SLOTS // RING) + j * (STEP // RING) + half

        u_tab, v_tab = a["peer_u"][0], a["peer_v"][0]
        block = ctx.enter_context(nc.Block())

        @block.sync
        def _(sp):
            sp.dma_start(keys[:, 0:16:2, :], a["peer_keys1"][0].rearrange("h n d -> n h d")).then_inc(s["k_in"], 16)
            sp.dma_start(keys[:, 1:16:2, :], a["peer_keys2"][0].rearrange("h n d -> n h d")).then_inc(s["k_in"], 16)
            sp.dma_start(g_ffn[:, :], a["norm_ffn"].to_broadcast([P, D])).then_inc(s["k_in"], 16)
            sp.dma_start(h_nxt[:, :], h_rows[0:P, :]).then_inc(s["h_in"], 16)
            for k in range(KD):
                sp.dma_start(wq[:, k, :], a["peer_wq"][0, k * P:(k + 1) * P, :]).then_inc(s["w_in2"], 16)
            with sp.Fori(0, TILES) as i:
                sp.wait_ge(s["cur_ready"], i + 1)
                sp.dma_start(h_nxt[:, :], h_rows[bass.ds(i * P + P, P), :]).then_inc(s["h_in"], 16)
                sp.wait_ge(s["cur_free"], i + 2)
                sp.dma_start(h2_rows[bass.ds(i * P, P), :], h_cur[:, :]).then_inc(s["h_out"], 16)
            sp.wait_ge(s["cur_free"], TILES + 2)
            sp.dma_start(h2_rows[SEQ:SEQ + P, :], h_cur[:, :]).then_inc(s["h_out"], 16)
            sp.wait_ge(s["h_out"], 16 * (ALLT + 1))

        @block.gpsimd
        def _(pool):
            g = nc.gpsimd
            g.memset(eps[:, :], EPS)
            g.memset(zero[:, :], 0.0)
            g.memset(ident[:, :], 0.0)
            g.iota(iota_i[:, :], pattern=[[1, TOPK]], base=0, channel_multiplier=0)
            pool.drain()
            g.affine_select(out=ident[:, :], in_=ident[:, :], compare_op=ALU.not_equal, fill=1.0,
                            base=0, pattern=[[-1, P]], channel_multiplier=1)
            g.tensor_copy(iota16[:, :], iota_i[:, :])
            pool.drain()
            pool.sem_inc(s["p_consts"], 1)
            pool.sem_inc(s["cur_free"], 1)
            pool.sem_inc(s["vacc_free"], 1)
            pool.sem_inc(s["h_out"], 16)
            for k in range(RING):
                pool.sem_inc(used[k], 1)

            def gathers(i, part, r, table):
                with pool.Fori(0, SLOTS // STEP) as j:
                    for half in range(2):
                        g.tensor_copy(stage[half][:, :], idx[:, bass.ds(i * SLOTS + j * STEP + half * RING, RING)]).then_inc(s["staged"], 1)
                        pool.wait_ge(s["staged"], turn(i, part, j, half) + 1)
                        for k in range(RING):
                            pool.wait_ge(used[k], turn(i, part, j, half) + 1)
                            pool.sem_inc(s["passed"], 1)
                            g.indirect_dma_start(rows[0:r, k, :], None, table,
                                                 bass.IndirectOffsetOnAxis(ap=stage[half][0:r, k:k + 1], axis=0)).then_inc(got[k], 16)

            with pool.Fori(0, TILES) as i:
                pool.wait_ge(s["idx_ready"], PH * i + PH)
                pool.sem_inc(s["passed"], 1)
                gathers(i, 0, P, u_tab)
                gathers(i, 1, P, v_tab)
            pool.wait_ge(s["idx_ready"], PH * ALLT)
            gathers(TILES, 0, NS, u_tab)
            gathers(TILES, 1, NS, v_tab)

        @block.tensor
        def _(pe):
            t = nc.tensor
            pe.wait_ge(s["p_consts"], 1)
            pe.wait_ge(s["k_in"], 48)
            for n in range(16):
                m = t.transpose(bank[n // 4][:, (n % 4) * P:(n % 4 + 1) * P], keys[:, n, :], ident[:, :])
            m.then_inc(s["keysT_ps"], 1)
            pe.wait_ge(s["keysT_sb"], 1)
            pe.wait_ge(s["w_in2"], 16 * KD)

            def scores(i):
                pe.wait_ge(s["c_ready"], i + 1)
                for k in range(KD):
                    m = t.transpose(bank[2 + k // 4][:, (k % 4) * P:(k % 4 + 1) * P], c_nxt[:, k * P:(k + 1) * P], ident[:, :])
                m.then_inc(s["cT_ps"], 1)
                pe.wait_ge(s["cT_sb"], i + 1)
                for b in range(4):
                    for c in range(4):
                        n = b * 4 + c
                        for k in range(KD):
                            m = t.matmul(bank[4 + b % 2][:, c * P:(c + 1) * P], wq[:, k, n * P:(n + 1) * P], cT[:, k, :],
                                         start=(k == 0), stop=(k == KD - 1))
                    m.then_inc(s["q_ps"], 1)
                    if b == 0:
                        continue
                    pe.wait_ge(s["q_sb"], 4 * i + b)
                pe.wait_ge(s["q_sb"], 4 * i + 4)
                for n in range(16):
                    m = t.matmul(bank[4 + n // 4][:, (n % 4) * P:(n % 4 + 1) * P], qT[:, n, :], keysT[:, n, :], start=True, stop=True)
                m.then_inc(s["s_ps"], 1)

            def accumulate(i, r):
                pe.wait_ge(s["vacc_free"], i + 1)
                for n in range(2):
                    t.matmul(bank[n][0:r, :], zero[0:r, 0:r], g_ffn[0:r, n * 512:(n + 1) * 512], start=True, stop=False)
                with pe.Fori(0, SLOTS // STEP) as j:
                    for n, k in enumerate(ON_PE):
                        pe.wait_ge(s["diag_ready"], (i * (SLOTS // STEP) + j) * NPE + n + 1)
                        pe.wait_ge(got[k % RING], 16 * (turn(i, 1, j, k // RING) + 1))
                        if r < P:
                            pe.sem_inc(s["pe_passed"], 1)
                        for c in range(2):
                            m = t.matmul(bank[c][0:r, :], diag[0:r, n % 4, 0:r], rows[0:r, k % RING, c * 512:(c + 1) * 512],
                                         start=False, stop=False)
                        m.then_inc(used[k % RING], 1)
                for n in range(2):
                    m = t.matmul(bank[n][0:r, :], zero[0:r, 0:r], g_ffn[0:r, n * 512:(n + 1) * 512], start=False, stop=True)
                m.then_inc(s["vacc_ps"], 1)

            scores(0)
            with pe.Fori(0, TILES) as i:
                scores(i + 1)
                accumulate(i, P)
            accumulate(TILES, NS)

        @block.scalar
        def _(act):
            ac = nc.scalar
            act.wait_ge(s["p_consts"], 1)
            act.wait_ge(s["keysT_ps"], 1)
            for b in range(4):
                m = ac.activation(keysT[:, 4 * b:4 * b + 4, :], bank[b][:, :].rearrange("p (c t) -> p c t", c=4), ACT.Copy)
            m.then_inc(s["keysT_sb"], 1)

            def scores(i):
                act.wait_ge(s["h_in"], 16 * i + 16)
                ac.activation(junk[:, :], h_nxt[:, :], ACT.Square, accum_out=st[:, 0:1])
                act.drain()
                ac.activation(st[:, 1:2], st[:, 0:1], ACT.Sqrt, scale=1.0 / D, bias=eps[:, :]).then_inc(s["rms"], 1)
                act.wait_ge(s["cT_ps"], i + 1)
                for b in range(2):
                    m = ac.activation(cT[:, 4 * b:4 * b + 4, :], bank[2 + b][:, :].rearrange("p (c t) -> p c t", c=4), ACT.Copy)
                m.then_inc(s["cT_sb"], 1)
                for b in range(4):
                    act.wait_ge(s["q_ps"], 4 * i + b + 1)
                    ac.activation(qT[:, 4 * b:4 * b + 4, :], bank[4 + b % 2][:, :].rearrange("p (c t) -> p c t", c=4), ACT.Copy).then_inc(s["q_sb"], 1)
                act.wait_ge(s["s_ps"], i + 1)
                for b in range(4):
                    m = ac.activation(sco[:, 4 * b:4 * b + 4, :], bank[4 + b][:, :].rearrange("p (c t) -> p c t", c=4), ACT.Copy)
                m.then_inc(s["s_sb"], 1)

            def take_over(i):
                act.wait_ge(s["cur_free"], i + 1)
                act.wait_ge(s["h_out"], 16 * i + 16)
                ac.activation(c_cur[:, :], c_nxt[:, :], ACT.Copy)
                ac.activation(h_cur[:, :], h_nxt[:, :], ACT.Copy).then_inc(s["cur_ready"], 1)

            def gates(i):
                act.wait_ge(s["gate_sub"], i + 1)
                ac.activation(sc_all[:, :], sc_all[:, :], ACT.Exp).then_inc(s["gate_exp"], 1)

            def diagonals(i, r):
                act.wait_ge(s["w_ready"], i + 1)
                act.sem_inc(s["act_passed"], 1)
                with act.Fori(0, SLOTS // STEP) as j:
                    for n, k in enumerate(ON_PE):
                        act.wait_ge(used[k % RING], turn(i, 1, j, k // RING) + 1)
                        act.sem_inc(s["act_passed"], 1)
                        ac.activation(diag[0:r, n % 4, 0:r], ident[0:r, 0:r], ACT.Copy,
                                      scale=wgt[0:r, bass.ds(j * STEP + k, 1)]).then_inc(s["diag_ready"], 1)

            scores(0)
            gates(0)
            with act.Fori(0, TILES) as i:
                take_over(i)
                scores(i + 1)
                act.wait_ge(s["dots_ready"], i + 1)
                ac.activation(wgt[:, :], dots[:, :], ACT.Gelu).then_inc(s["gelu_done"], 1)
                diagonals(i, P)
                gates(i + 1)
            take_over(TILES)
            act.wait_ge(s["dots_ready"], ALLT)
            ac.activation(wgt[0:NS, :], dots[0:NS, :], ACT.Gelu).then_inc(s["gelu_done"], 1)
            diagonals(TILES, NS)

        @block.vector
        def _(dve):
            v = nc.vector
            dve.wait_ge(s["p_consts"], 1)
            dve.wait_ge(s["k_in"], 48)

            def norm(i):
                dve.wait_ge(s["rms"], i + 1)
                v.reciprocal(st[:, 2:3], st[:, 1:2])
                dve.drain()
                v.scalar_tensor_tensor(c_nxt[:, :], h_nxt[:, :], st[:, 2:3], g_ffn[:, :], ALU.mult, ALU.mult).then_inc(s["c_ready"], 1)

            def best(i, j):
                v.tensor_copy(sst[:, :, :], sco[:, bass.ds(j * 2, 2), :])
                dve.drain()
                for f in range(2):
                    v.max(v1[:, f, 0:8], sst[:, f, :])
                dve.drain()
                for f in range(2):
                    v.max_index(x1[:, f, 0:8], v1[:, f, 0:8], sst[:, f, :])
                    v.match_replace(sst2[:, f, :], v1[:, f, 0:8], sst[:, f, :], LOW)
                dve.drain()
                for f in range(2):
                    v.max(v1[:, f, 8:16], sst2[:, f, :])
                dve.drain()
                for f in range(2):
                    v.max_index(x1[:, f, 8:16], v1[:, f, 8:16], sst2[:, f, :])
                v.tensor_tensor(cand[:, :, :], v1[:, 0, :].rearrange("p (a o) -> p a o", o=1).to_broadcast([P, TOPK, TOPK]),
                                v1[:, 1, :].rearrange("p (o b) -> p o b", o=1).to_broadcast([P, TOPK, TOPK]), ALU.add)
                dve.drain()
                flat = cand[:, :, :].rearrange("p a b -> p (a b)")
                v.tensor_copy(x1f[:, :, :], x1[:, :, :])
                v.max(sc16[:, 0:8], flat)
                dve.drain()
                v.max_index(ci[:, 0:8], sc16[:, 0:8], flat)
                v.match_replace(cand2[:, :], sc16[:, 0:8], flat, LOW)
                dve.drain()
                v.max(sc16[:, 8:16], cand2[:, :])
                dve.drain()
                v.max_index(ci[:, 8:16], sc16[:, 8:16], cand2[:, :])
                dve.drain()
                v.tensor_scalar(cab[:, 0, :], ci[:, :], 4, None, ALU.logical_shift_right)
                v.tensor_scalar(cab[:, 1, :], ci[:, :], 15, None, ALU.bitwise_and)
                dve.drain()
                v.tensor_copy(cabf[:, :, :], cab[:, :, :])
                dve.drain()
                for f in range(2):
                    v.tensor_tensor(eq[:, f], cabf[:, f, :].rearrange("p (k o) -> p k o", o=1).to_broadcast([P, TOPK, TOPK]),
                                    iota16[:, :].rearrange("p (o a) -> p o a", o=1).to_broadcast([P, TOPK, TOPK]), ALU.is_equal)
                dve.drain()
                for f in range(2):
                    v.tensor_tensor(eq[:, f], eq[:, f],
                                    x1f[:, f, :].rearrange("p (o a) -> p o a", o=1).to_broadcast([P, TOPK, TOPK]), ALU.mult)
                dve.drain()
                v.tensor_reduce(e12[:, :, :], eq[:, :, :, :], AXX, ALU.add)
                dve.drain()
                v.scalar_tensor_tensor(idx[:, bass.ds(i * SLOTS + j * TOPK, TOPK)], e12[:, 0, :], float(NK), e12[:, 1, :],
                                       ALU.mult, ALU.add).then_inc(s["idx_ready"], 1)
                v.tensor_scalar(sc_all[:, bass.ds(j * TOPK, TOPK)], sc16[:, :], sc16[:, 0:1], None, ALU.subtract)
                dve.drain()

            def gates(i):
                dve.sem_inc(s["gate_sub"], 1)
                dve.wait_ge(s["gate_exp"], i + 1)
                by_head = sc_all[:, :].rearrange("p (h k) -> p h k", k=TOPK)
                v.tensor_reduce(gs[:, 0, :], by_head, AXX, ALU.add)
                dve.drain()
                v.reciprocal(gs[:, 1, :], gs[:, 0, :])
                dve.drain()
                v.tensor_tensor(gate[:, bass.ds(i * SLOTS, SLOTS)].rearrange("p (h k) -> p h k", k=TOPK), by_head,
                                gs[:, 1, :].rearrange("p (h o) -> p h o", o=1).to_broadcast([P, PH, TOPK]), ALU.mult)
                dve.drain()

            norm(0)
            dve.wait_ge(s["s_sb"], 1)
            with dve.Fori(0, PH) as j:
                best(0, j)
            gates(0)

            def tile(i, r, last):
                dve.wait_ge(s["cur_ready"], i + 1)
                if not last:
                    norm(i + 1)
                with dve.Fori(0, SLOTS // STEP) as j:
                    for k in range(STEP):
                        dve.wait_ge(got[k % RING], 16 * (turn(i, 0, j, k // RING) + 1))
                        v.tensor_tensor_reduce(out=rows[0:r, k % RING, :], in0=rows[0:r, k % RING, :], in1=c_cur[0:r, :], scale=1.0,
                                               scalar=0.0, op0=ALU.mult, op1=ALU.add,
                                               accum_out=dot16[0:r, k:k + 1]).then_inc(used[k % RING], 1)
                    dve.drain()
                    v.tensor_copy(dots[0:r, bass.ds(j * STEP, STEP)], dot16[0:r, :])
                    dve.drain()
                dve.sem_inc(s["dots_ready"], 1)
                dve.wait_ge(s["gelu_done"], i + 1)
                v.tensor_tensor(wgt[0:r, :], wgt[0:r, :], gate[0:r, bass.ds(i * SLOTS, SLOTS)], ALU.mult).then_inc(s["w_ready"], 1)
                dve.drain()
                if not last:
                    dve.wait_ge(s["s_sb"], i + 2)
                    dve.sem_inc(s["passed2"], 1)
                with dve.Fori(0, SLOTS // STEP) as j:
                    v.tensor_copy(w16[0:r, :], wgt[0:r, bass.ds(j * STEP, STEP)])
                    if not last:
                        best(i + 1, j)
                    else:
                        dve.drain()
                    for k in range(STEP):
                        if k in ON_PE:
                            continue
                        dve.wait_ge(got[k % RING], 16 * (turn(i, 1, j, k // RING) + 1))
                        v.scalar_tensor_tensor(h_cur[0:r, :], rows[0:r, k % RING, :], w16[0:r, k:k + 1], h_cur[0:r, :],
                                               ALU.mult, ALU.add).then_inc(used[k % RING], 1)
                        dve.drain()
                dve.wait_ge(s["vacc_ps"], i + 1)
                for n in range(2):
                    m = v.tensor_tensor(h_cur[0:r, n * 512:(n + 1) * 512], h_cur[0:r, n * 512:(n + 1) * 512], bank[n][0:r, :], ALU.add)
                m.then_inc(s["vacc_free"], 1)
                dve.drain()
                dve.sem_inc(s["cur_free"], 1)
                if not last:
                    gates(i + 1)

            with dve.Fori(0, TILES) as i:
                tile(i, P, False)
            tile(TILES, NS, True)


def gate_block(nc, sems, a, out, h2_rows):
    PB = PLE // P
    with ExitStack() as ctx:
        def sb(name, shape, dt=F32):
            return ctx.enter_context(nc.sbuf_tensor(name, shape, dt))

        def sem(name):
            return sems.enter_context(nc.semaphore("gate_" + name))

        bank = [ctx.enter_context(nc.psum_tensor(f"gbank{b}", [P, 512], F32)) for b in range(8)]
        wg = sb("ple_gate_sb", [P, KD, D])
        wi = sb("ple_in_sb", [P, PB, D])
        g_ple = sb("g_ple_sb", [P, KD])
        g_fin = sb("g_fin_sb", [P, D])
        ident = sb("g_ident", [P, P])
        eps = sb("g_eps", [P, 1])
        h = [sb(f"gh{k}", [P, D]) for k in range(2)]
        p = [sb(f"gp{k}", [P, PLE]) for k in range(2)]
        en = [sb(f"gen{k}", [P, D]) for k in range(2)]
        st = sb("g_stats", [P, 2, 6])
        junk = sb("g_junk", [P, D])
        eT = [sb(f"geT{k}", [P, KD, P]) for k in range(2)]
        pT = [sb(f"gpT{k}", [P, PB, P]) for k in range(2)]
        sg = [sb(f"gsg{k}", [P, D]) for k in range(2)]
        y = [sb(f"gy{k}", [P, D]) for k in range(2)]
        names = ("g_consts w_in3 w_in4 in0 in1 rms en_ready T_ps T_sb pT_sb gate_ps sig_done sum_ready "
                 "rms2 y_ready y_out0 y_out1").split()
        s = {n: sem(n) for n in names}
        block = ctx.enter_context(nc.Block())

        @block.sync
        def _(sp):
            sp.dma_start(h[0][:, :], h2_rows[0:P, :]).then_inc(s["in0"], 16)
            sp.dma_start(p[0][:, :], a["p_prompt"][0, 0, 0:P, :]).then_inc(s["in0"], 16)
            for k in range(KD):
                sp.dma_start(wg[:, k, :], a["ple_gate"][0, k * P:(k + 1) * P, :]).then_inc(s["w_in3"], 16)
            sp.dma_start(wi[:, :, :], a["ple_in"][0].rearrange("(k p) n -> p k n", p=P)).then_inc(s["w_in3"], 16)
            for i in range(1, ALLT):
                if i >= 2:
                    sp.wait_ge(s["y_ready"], i - 1)
                r = P if i < TILES else NS
                src = a["p_prompt"][0, 0, i * P:(i + 1) * P, :] if i < TILES else a["p_sample"][0].rearrange("b t d -> (b t) d")
                sp.dma_start(h[i % 2][0:r, :], h2_rows[i * P:i * P + r, :]).then_inc(s[f"in{i % 2}"], 16)
                sp.dma_start(p[i % 2][0:r, :], src).then_inc(s[f"in{i % 2}"], 16)

        @block.gpsimd
        def _(pool):
            g = nc.gpsimd
            g.memset(eps[:, :], EPS)
            g.memset(ident[:, :], 0.0)
            pool.drain()
            g.affine_select(out=ident[:, :], in_=ident[:, :], compare_op=ALU.not_equal, fill=1.0,
                            base=0, pattern=[[-1, P]], channel_multiplier=1)
            pool.drain()
            pool.sem_inc(s["g_consts"], 1)
            pool.dma_start(g_fin[:, :], a["norm_final"].rearrange("(o n) -> o n", o=1).to_broadcast([P, D])).then_inc(s["w_in4"], 16)
            with nc.allow_non_contiguous_dma(reason="a weight per channel onto the partitions"):
                pool.dma_start(g_ple[:, :], a["norm_ple"][0].rearrange("(k p) -> p k", p=P)).then_inc(s["w_in4"], 16)
            for i in range(ALLT):
                r = P if i < TILES else NS
                dst = out["y_p"][0, i * P:(i + 1) * P, :] if i < TILES else out["y_s"].rearrange("b t d -> (b t) d")
                pool.wait_ge(s["y_ready"], i + 1)
                pool.dma_start(dst, y[i % 2][0:r, :]).then_inc(s[f"y_out{i % 2}"], 16)
            pool.wait_ge(s["y_out0"], 16 * ((ALLT + 1) // 2))
            pool.wait_ge(s["y_out1"], 16 * (ALLT // 2))

        @block.tensor
        def _(pe):
            t = nc.tensor
            pe.wait_ge(s["g_consts"], 1)
            for i in range(ALLT):
                r = P if i < TILES else NS
                e = i % 2
                pe.wait_ge(s["en_ready"], i + 1)
                for k in range(KD):
                    t.transpose(bank[k // 4][:, (k % 4) * P:(k % 4) * P + r], en[e][0:r, k * P:(k + 1) * P], ident[0:r, 0:r])
                for k in range(PB):
                    m = t.transpose(bank[2][:, k * P:k * P + r], p[e][0:r, k * P:(k + 1) * P], ident[0:r, 0:r])
                m.then_inc(s["T_ps"], 1)
                pe.wait_ge(s["T_sb"], i + 1)
                pe.wait_ge(s["pT_sb"], i + 1)
                if i == 0:
                    pe.wait_ge(s["w_in3"], 16 * (KD + 1))
                else:
                    pe.wait_ge(s["sum_ready"], i)
                for n in range(2):
                    for k in range(KD):
                        t.matmul(bank[3 + n][0:r, :], eT[e][:, k, 0:r], wg[:, k, n * 512:(n + 1) * 512], start=(k == 0), stop=(k == KD - 1))
                for n in range(2):
                    for k in range(PB):
                        m = t.matmul(bank[5 + n][0:r, :], pT[e][:, k, 0:r], wi[:, k, n * 512:(n + 1) * 512], start=(k == 0), stop=(k == PB - 1))
                m.then_inc(s["gate_ps"], 1)

        @block.scalar
        def _(act):
            ac = nc.scalar
            act.wait_ge(s["g_consts"], 1)

            def first(i):
                r, e = (P if i < TILES else NS), i % 2
                act.wait_ge(s[f"in{e}"], 32 * (i // 2 + 1))
                ac.activation(junk[0:r, :], h[e][0:r, :], ACT.Square, accum_out=st[0:r, e, 0:1])
                act.drain()
                ac.activation(st[0:r, e, 1:2], st[0:r, e, 0:1], ACT.Sqrt, scale=1.0 / D, bias=eps[0:r, :]).then_inc(s["rms"], 1)

            first(0)
            for i in range(ALLT):
                r, e = (P if i < TILES else NS), i % 2
                act.wait_ge(s["T_ps"], i + 1)
                ac.activation(pT[e][:, :, 0:r], bank[2][:, 0:PLE].rearrange("p (k t) -> p k t", k=PB)[:, :, 0:r], ACT.Copy).then_inc(s["pT_sb"], 1)
                if i + 1 < ALLT:
                    first(i + 1)
                act.wait_ge(s["gate_ps"], i + 1)
                for n in range(2):
                    m = ac.activation(sg[e][0:r, n * 512:(n + 1) * 512], bank[3 + n][0:r, :], ACT.Sigmoid)
                m.then_inc(s["sig_done"], 1)
                act.wait_ge(s["sum_ready"], i + 1)
                ac.activation(junk[0:r, :], sg[e][0:r, :], ACT.Square, accum_out=st[0:r, e, 3:4])
                act.drain()
                ac.activation(st[0:r, e, 4:5], st[0:r, e, 3:4], ACT.Sqrt, scale=1.0 / D, bias=eps[0:r, :]).then_inc(s["rms2"], 1)

        @block.vector
        def _(dve):
            v = nc.vector
            dve.wait_ge(s["g_consts"], 1)
            dve.wait_ge(s["w_in4"], 32)

            def first(i):
                r, e = (P if i < TILES else NS), i % 2
                dve.wait_ge(s["rms"], i + 1)
                v.reciprocal(st[0:r, e, 2:3], st[0:r, e, 1:2])
                dve.drain()
                v.tensor_scalar(en[e][0:r, :], h[e][0:r, :], st[0:r, e, 2:3], None, ALU.mult).then_inc(s["en_ready"], 1)

            first(0)
            for i in range(ALLT):
                r, e = (P if i < TILES else NS), i % 2
                dve.wait_ge(s["T_ps"], i + 1)
                for b in range(2):
                    m = v.tensor_tensor(eT[e][:, 4 * b:4 * b + 4, 0:r], bank[b][:, :].rearrange("p (k t) -> p k t", k=4)[:, :, 0:r],
                                        g_ple[:, 4 * b:4 * b + 4].rearrange("p (k o) -> p k o", o=1).to_broadcast([P, 4, r]), ALU.mult)
                m.then_inc(s["T_sb"], 1)
                if i + 1 < ALLT:
                    first(i + 1)
                dve.wait_ge(s["sig_done"], i + 1)
                for n in range(2):
                    v.tensor_tensor(sg[e][0:r, n * 512:(n + 1) * 512], sg[e][0:r, n * 512:(n + 1) * 512], bank[5 + n][0:r, :], ALU.mult)
                dve.drain()
                v.tensor_tensor(sg[e][0:r, :], sg[e][0:r, :], h[e][0:r, :], ALU.add).then_inc(s["sum_ready"], 1)
                dve.wait_ge(s["rms2"], i + 1)
                v.reciprocal(st[0:r, e, 5:6], st[0:r, e, 4:5])
                if i >= 2:
                    dve.wait_ge(s[f"y_out{e}"], 16 * (i // 2))
                dve.drain()
                v.scalar_tensor_tensor(y[e][0:r, :], sg[e][0:r, :], st[0:r, e, 5:6], g_fin[0:r, :], ALU.mult, ALU.mult).then_inc(s["y_ready"], 1)


def program(nc, a, out):
    h_rows = nc.dram_tensor("h_after_mixer", [ALLT * P, D], F32).ap()
    h2_rows = nc.dram_tensor("h_after_peer", [ALLT * P, D], F32).ap()
    with ExitStack() as sems:
        mixer_block(nc, sems, a, out, h_rows)
        peer_block(nc, sems, a, h_rows, h2_rows)
        gate_block(nc, sems, a, out, h2_rows)


_INS = ['x_prompt', 'x_sample', 'p_prompt', 'p_sample', 'cache_swa_k', 'cache_swa_v', 'state_conv', 'state_delta',
        'norm_mix', 'w_in', 'conv_w', 'attn_sinks', 'dn_a_log', 'dn_dt_bias', 'dn_norm', 'w_out', 'norm_ffn',
        'peer_wq', 'peer_keys1', 'peer_keys2', 'peer_u', 'peer_v', 'norm_ple', 'ple_in', 'ple_gate', 'norm_final']
_OUTS = [('y_p', (1, SEQ, D)), ('y_s', (DB, DS, D)), ('k_p', (1, 1, WIN, KVH, HD)), ('v_p', (1, 1, WIN, KVH, HD)),
         ('c_p', (1, 1, TAPS - 1, DQKV)), ('s_p', (1, 1, DH, HD, HD)), ('k_s', (1, DB, WIN, KVH, HD)),
         ('v_s', (1, DB, WIN, KVH, HD)), ('c_s', (1, DB, TAPS - 1, DQKV)), ('s_s', (1, DB, DH, HD, HD))]


def kernel(**inputs):
    import numpy as _np
    import concourse.bacc as _bacc
    from concourse.bass_utils import run_bass_kernel_spmd as _run

    nc = _bacc.Bacc("TRN2", target_bir_lowering=False, num_devices=1)
    arrays, a, out = {}, {}, {}
    for name in _INS:
        arrays[f"in_{name}_dram"] = _np.ascontiguousarray(inputs[name])
        a[name] = nc.dram_tensor(f"in_{name}_dram", arrays[f"in_{name}_dram"].shape, F32, kind="ExternalInput").ap()
    i, j = _np.arange(GRP * DS)[:, None] % DS, _np.arange(SKEYS)[None]
    far = (WIN + i - j < 0) | (WIN + i - j > WIN)
    consts = {"c_dist": _np.where(far, FAR, WIN + i - j).astype(_np.float32),
              "c_slope": _np.array([[SLOPE[g * GRP + n // DS] for g in range(KVH)] for n in range(GRP * DS)], _np.float32)}
    for name, value in consts.items():
        arrays[f"in_{name}_dram"] = value
        a[name] = nc.dram_tensor(f"in_{name}_dram", value.shape, F32, kind="ExternalInput").ap()
    for name, shape in _OUTS:
        out[name] = nc.dram_tensor(f"out_{name}_dram", shape, F32, kind="ExternalOutput").ap()
    program(nc, a, out)
    r = _run(nc, [arrays], core_ids=[0])
    return tuple(r.results[0][f"out_{name}_dram"] for name, _ in _OUTS)
```

```python
import concourse.bass as bass
from concourse import mybir
from contextlib import ExitStack

F32 = mybir.dt.float32
I32 = mybir.dt.int32
U32 = mybir.dt.uint32
ALU = mybir.AluOpType
ACT = mybir.ActivationFunctionType
AXX = mybir.AxisListType.X

P = 128
D = 1024
KD = D // P
SEQ = 1024
TILES = SEQ // P
DB, DS = 8, 8
NS = DB * DS
ALLT = TILES + 1
HD = 64
AH, KVH, GRP = 8, 2, 4
WIN = 128
DH = 8
PAIRS = DH // 2
DQKV = 3 * DH * HD
CB = DQKV // P
TAPS = 4
C_K, C_V, C_DN = 512, 640, 768
C_Z = C_DN + DQKV
C_AB = C_Z + DH * HD
INW = C_AB + 2 * DH
NK = 128
NEXP = NK * NK
PH, TOPK = 8, 16
SLOTS = PH * TOPK
PLE = 256
EPS = 1e-6
FAR = 1e32
LOW = -3e38
LEVELS = (1, 2, 4, 8, 16, 32, 64)
SKEYS = WIN + DS
SLOPE = [-(2.0 ** (-8.0 * (h + 1) / AH)) for h in range(AH)]


def mixer_block(nc, sems, a, out, h_rows):
    with ExitStack() as ctx:
        def sb(name, shape, dt=F32):
            return ctx.enter_context(nc.sbuf_tensor(name, shape, dt))

        def sem(name):
            return sems.enter_context(nc.semaphore("mixer_" + name))

        bank = [ctx.enter_context(nc.psum_tensor(f"mbank{b}", [P, 512], F32)) for b in range(8)]

        w_in = sb("w_in_sb", [P, KD, INW])
        w_flat = w_in[:, :, :].rearrange("p k n -> p (k n)")
        w_out = sb("w_out_sb", [P, KD, D])
        ident = sb("m_ident", [P, P])
        tri = sb("m_tri", [P, P])
        tri8 = sb("m_tri8", [P, NS])
        level = sb("m_level", [P, len(LEVELS), P])
        ones = sb("m_ones", [P, P])
        same8 = sb("m_same8", [P, NS])
        seq_of = sb("m_seq_of", [P, DB])
        pair_diag = sb("m_pair_diag", [P, P])
        g_mix = sb("g_mix_sb", [P, KD])
        cw = sb("conv_w_sb", [P, TAPS, CB])
        sinks = sb("sinks_sb", [P, AH])
        neg_a = sb("neg_a_sb", [P, DH])
        dtb = sb("dtb_sb", [P, DH])
        dnn = sb("dn_norm_sb", [P, HD])
        dist = sb("att_dist", [P, 2 * WIN])
        dist_old = sb("att_dist_old", [P, WIN])
        dist_s = sb("att_dist_s", [GRP * DS, SKEYS])
        slope_s = sb("att_slope_s", [GRP * DS, KVH])
        eps = sb("m_eps", [P, 1])
        one = sb("m_one", [P, 1])

        xh = sb("x_and_h", [P, D])
        x = xn = h = xh
        st = sb("m_stats", [P, 4])
        aT = sb("aT_sb", [P, KD, P])
        attT = sb("att_T", [P, 4, P])
        cin = sb("cin_sb", [P, CB, TAPS - 1 + P])
        cacc = sb("cacc_sb", [P, CB, P])
        cs = sb("cs_sb", [P, CB, P])
        qT = sb("qT_sb", [P, GRP, P])
        kT = sb("kT_sb", [P, 2 * P])
        kv = sb("kv_sb", [P, 2, P])
        v_old = sb("v_old_sb", [P, P])
        zs = sb("zs_sb", [P, 512])
        ab_raw = sb("ab_raw_sb", [P, 2 * DH])
        sc = sb("att_sc", [P, AH, 2 * WIN])
        am = sb("att_m", [P, 6, AH])
        pT = sb("att_pT", [P, AH, 2, P])
        gt = sb("gate_small", [P, 12, DH])
        rn = sb("m_rn", [P, 3, 16])
        rows = sb("dn_rows", [P, 6, 512])
        vb = sb("dn_vb", [P, 512])
        rT = sb("dn_rT", [P, 5, 4, P])
        s2 = sb("dn_s2", [P, PAIRS, P])
        eg = sb("dn_eg", [P, PAIRS])
        qT_s = qT[:, :, :].rearrange("p c t -> p (c t)")[:, 0:DB * GRP * DS].rearrange("p (b h t) -> p b h t", b=DB, h=GRP)
        x_res = rT[:, 0:2, :, :].rearrange("p a c t -> p (a c t)")
        dt_ = cacc[:, 0:DH, :]
        cs_flat = cs[:, :, :].rearrange("p c t -> p (c t)")
        sq = cs_flat[:, 0:1024]
        y0, y1, ty = (cs_flat[:, n * 512:(n + 1) * 512] for n in range(3))
        rows_flat = rows[:, :, :].rearrange("p c t -> p (c t)")
        lt = rows_flat[:, 0:1024].rearrange("p (h t) -> p h t", h=DH)
        qk = rows_flat[:, 1024:2048].rearrange("p (h t) -> p h t", h=DH)
        vn = rows[:, 4, :]
        stconv = rows_flat[0:24, 0:DQKV]
        pT_flat = pT[:, :, :, :].rearrange("p h c t -> p (h c t)")
        bt = pT_flat[:, 0:1024].rearrange("p (h t) -> p h t", h=DH)
        t1 = pT_flat[:, 1024:2048].rearrange("p (h t) -> p h t", h=DH)
        xx = sc[:, :, :].rearrange("p h (c t) -> p h c t", c=2)
        sc_flat = sc[:, :, :].rearrange("p h t -> p (h t)")
        z_raw, dn = sc_flat[:, 0:512], sc_flat[:, 512:1024]
        dnT = sc_flat[:, 1024:1536].rearrange("p (c t) -> p c t", c=4)
        s2n = vb[:, :].rearrange("p (c t) -> p c t", c=PAIRS)
        stage3 = cin[:, :, :].rearrange("p c t -> p (c t)")[:, 0:DQKV]

        at = [0]

        def over(n):
            at[0] += n
            assert at[0] <= KD * INW
            return w_flat[:, at[0] - n:at[0]]

        s2s = over(DB * PAIRS * P).rearrange("p (b c v) -> p b c v", b=DB, c=PAIRS)
        kgm = over(DB * PAIRS * NS).rearrange("p (b c t) -> p b c t", b=DB, c=PAIRS)
        qgm = over(DB * PAIRS * NS).rearrange("p (b c t) -> p b c t", b=DB, c=PAIRS)
        ktm = over(2 * 512).rearrange("p (r n) -> p r n", r=2)
        kc = over(DB * P).rearrange("p (b n) -> p b n", b=DB)
        vc = over(DB * P).rearrange("p (b n) -> p b n", b=DB)
        kcT = over(DB * P).rearrange("p (b n) -> p b n", b=DB)
        vnew = over(DB * P).rearrange("p (b n) -> p b n", b=DB)
        ssc = over(2 * DB * SKEYS).rearrange("p (b k) -> p b k", k=SKEYS)
        sm = over(6 * 2 * DB).rearrange("p (r n) -> p r n", r=6)
        spT = over(512).rearrange("p (b r) -> p b r", b=2 * DB)
        spTn = over(512).rearrange("p (b r) -> p b r", b=2 * DB)
        egb = over(DB * PAIRS).rearrange("p (b c) -> p b c", b=DB)
        gmb = over(DB * DH).rearrange("p (b c) -> p b c", b=DB)
        crow = over(DQKV)
        sink_s = sb("sink_s", [P, 2])

        names = ("const_in w_in_in w_out_in misc_in consts x_in rms xn_ready xT_ps aT_ready dqkv_ps "
                 "cin_ready kv_ps kv_sb q_ps q_sb z_ps z_sb silu_done conv_done rows_ps sq_done ssq_done rn_sqrt "
                 "soft_in soft_out gate_ready gsum_ps e_in exp_ready drow_ready rT_ps rT_a rT_v gram_ps "
                 "kgs_ps y0_ready b_ready t_ps t_sb zz_ps xx_ready y1_ps y1_sb ty_ps ty_sb yz_ps vn_ready "
                 "o_ps upd_ps osq_done ossq orms dn_ready dnT_ps dnT_sb score_ps sc_ready nm_ready "
                 "prob_done probs_ready pT_ps pT_sb att_ps att_sb proj_ps h_ready h_out sp_passed "
                 "state_out stc_in stc_ps stc_sb cache_in state_in vnew_in kcT_ps kcT_sb over_clear "
                 "ktm_ready supd_ps supd_done conv_ps conv_sb out_done mm_masked sexp kmask_ready sprobs "
                 "xres_in").split()
        s = {n: sem(n) for n in names}
        block = ctx.enter_context(nc.Block())

        @block.sync
        def _(sp):
            wv = a["w_in"][0].rearrange("(k p) n -> p k n", p=P)
            for k in range(KD):
                sp.dma_start(w_in[:, k, C_DN:INW], wv[:, k, C_DN:INW]).then_inc(s["w_in_in"], 16)
            for b in range(GRP):
                for g in range(KVH):
                    c = (g * GRP + b) * HD
                    sp.dma_start(w_in[:, :, b * P + g * HD:b * P + (g + 1) * HD],
                                 wv[:, :, c:c + HD]).then_inc(s["w_in_in"], 16)
            sp.dma_start(w_in[:, :, C_K:C_DN], wv[:, :, C_K:C_DN]).then_inc(s["w_in_in"], 16)
            wo = a["w_out"][0]
            for b in range(GRP):
                for g in range(KVH):
                    r = (g * GRP + b) * HD
                    sp.dma_start(w_out[g * HD:(g + 1) * HD, b, :], wo[r:r + HD, :]).then_inc(s["w_out_in"], 16)
            sp.dma_start(w_out[:, 4:8, :], wo[512:1024, :].rearrange("(k p) n -> p k n", p=P)).then_inc(s["w_out_in"], 16)

            def tile(i):
                sp.wait_ge(s["gram_ps"], i + 1)
                sp.sem_inc(s["sp_passed"], 1)
                sp.dma_start(x_res[:, :], a["x_prompt"][0, bass.ds(i * P, P), :]).then_inc(s["xres_in"], 16)

            def store(i):
                sp.wait_ge(s["h_ready"], i + 1)
                sp.sem_inc(s["sp_passed"], 1)
                sp.dma_start(h_rows[bass.ds(i * P, P), :], h[:, :]).then_inc(s["h_out"], 16)

            sp.dma_start(x[:, :], a["x_prompt"][0, 0:P, :]).then_inc(s["x_in"], 16)
            with sp.Fori(0, TILES - 1) as i:
                sp.wait_ge(s["h_out"], 16 * i + 16)
                sp.sem_inc(s["sp_passed"], 1)
                sp.wait_ge(s["xT_ps"], i + 1)
                sp.sem_inc(s["sp_passed"], 1)
                sp.dma_start(x[:, :], a["x_prompt"][0, bass.ds(i * P + P, P), :]).then_inc(s["x_in"], 16)
                tile(i)
                store(i)
            tile(TILES - 1)
            store(TILES - 1)
            sp.wait_ge(s["h_ready"], TILES)
            sp.wait_ge(s["h_out"], 16 * (TILES + 1))
            sp.dma_start(out["k_p"][0, 0].rearrange("t g d -> t (g d)"), kv[:, 0, :]).then_inc(s["state_out"], 16)
            sp.dma_start(out["v_p"][0, 0].rearrange("t g d -> t (g d)"), kv[:, 1, :]).then_inc(s["state_out"], 16)
            for hh in range(DH):
                q, c = divmod(hh, 2)
                sp.dma_start(out["s_p"][0, 0, hh], s2[c * HD:(c + 1) * HD, q, c * HD:(c + 1) * HD]).then_inc(s["state_out"], 16)
            sp.dma_start(x[0:NS, :], a["x_sample"].rearrange("b t d -> (b t) d")).then_inc(s["x_in"], 16)
            sp.dma_start(stconv[:, :], a["state_conv"][0].rearrange("b t c -> (b t) c")).then_inc(s["stc_in"], 16)
            sp.wait_ge(s["over_clear"], 1)
            for c in range(2):
                for b in range(DB):
                    sp.dma_start(s2s[c * HD:(c + 1) * HD, b, :, c * HD:(c + 1) * HD],
                                 a["state_delta"][0, b, c:DH:2].rearrange("h k v -> k h v")).then_inc(s["state_in"], 16)
            sp.dma_start(kc[:, :, :], a["cache_swa_k"][0].rearrange("b t g d -> t b (g d)")).then_inc(s["cache_in"], 16)
            sp.dma_start(vc[:, :, :], a["cache_swa_v"][0].rearrange("b t g d -> t b (g d)")).then_inc(s["cache_in"], 16)
            for src, dst in (("cache_swa_k", "k_s"), ("cache_swa_v", "v_s")):
                sp.dma_start(out[dst][0][:, 0:WIN - DS], a[src][0][:, DS:WIN]).then_inc(s["out_done"], 16)
            sp.wait_ge(s["kv_sb"], TILES + 1)
            for b in range(DB):
                sp.dma_start(vnew[0:DS, b, :], kv[b * DS:(b + 1) * DS, 1, :]).then_inc(s["vnew_in"], 16)
                sp.dma_start(out["k_s"][0, b, WIN - DS:WIN].rearrange("t g d -> t (g d)"),
                             kv[b * DS:(b + 1) * DS, 0, :]).then_inc(s["out_done"], 16)
                sp.dma_start(out["v_s"][0, b, WIN - DS:WIN].rearrange("t g d -> t (g d)"),
                             kv[b * DS:(b + 1) * DS, 1, :]).then_inc(s["out_done"], 16)
            sp.wait_ge(s["conv_sb"], 2)
            for b in range(DB):
                sp.dma_start(out["c_s"][0, b], crow[b * DS + DS - 3:(b + 1) * DS, :]).then_inc(s["out_done"], 16)
            sp.wait_ge(s["gram_ps"], TILES + 1)
            sp.dma_start(x_res[0:NS, :], a["x_sample"].rearrange("b t d -> (b t) d")).then_inc(s["xres_in"], 16)
            sp.wait_ge(s["supd_done"], DB)
            for b in range(DB):
                for hh in range(DH):
                    q, c = divmod(hh, 2)
                    sp.dma_start(out["s_s"][0, b, hh], s2s[c * HD:(c + 1) * HD, b, q, c * HD:(c + 1) * HD]).then_inc(s["out_done"], 16)
            sp.wait_ge(s["h_ready"], TILES + 1)
            sp.dma_start(h_rows[SEQ:SEQ + P, :], h[:, :]).then_inc(s["h_out"], 16)
            sp.wait_ge(s["h_out"], 16 * (TILES + 2))
            sp.wait_ge(s["state_out"], 16 * (2 + DH))
            sp.wait_ge(s["out_done"], 16 * (2 + 2 * DB + DB + DB * DH))

        @block.gpsimd
        def _(pool):
            g = nc.gpsimd
            row = lambda ap, n: ap.rearrange("(o n) -> o n", o=1).to_broadcast([P, n])
            pool.dma_start(sinks[:, :], row(a["attn_sinks"][0], AH)).then_inc(s["const_in"], 16)
            pool.dma_start(neg_a[:, :], row(a["dn_a_log"][0], DH)).then_inc(s["const_in"], 16)
            pool.dma_start(dtb[:, :], row(a["dn_dt_bias"][0], DH)).then_inc(s["const_in"], 16)
            pool.dma_start(dnn[:, :], row(a["dn_norm"][0], HD)).then_inc(s["const_in"], 16)
            pool.dma_start(dist_s[:, :], a["c_dist"]).then_inc(s["const_in"], 16)
            pool.dma_start(slope_s[:, :], a["c_slope"]).then_inc(s["const_in"], 16)
            with nc.allow_non_contiguous_dma(reason="small weights onto the partitions"):
                pool.dma_start(g_mix[:, :], a["norm_mix"][0].rearrange("(k p) -> p k", p=P)).then_inc(s["const_in"], 16)
                for j in range(TAPS):
                    pool.dma_start(cw[:, j, :], a["conv_w"][0, j].rearrange("(c p) -> p c", p=P)).then_inc(s["const_in"], 16)
                for hh in range(AH):
                    gg, p = divmod(hh, GRP)
                    pool.dma_start(sink_s[p * DS:(p + 1) * DS, gg:gg + 1],
                                   a["attn_sinks"][0:1, hh:hh + 1].to_broadcast([DS, 1])).then_inc(s["const_in"], 16)
            g.memset(eps[:, :], EPS)
            g.memset(one[:, :], 1.0)
            g.memset(ones[:, :], 1.0)
            g.memset(ident[:, :], 0.0)
            g.memset(tri[:, :], 1.0)
            g.memset(pair_diag[:, :], 1.0)
            g.memset(seq_of[:, :], 1.0)
            g.memset(same8[:, :], 1.0)
            g.memset(level[:, :, :], 1.0)
            g.memset(cin[:, :, 0:TAPS - 1], 0.0)
            g.memset(kT[:, :], 0.0)
            g.memset(v_old[:, :], 0.0)
            g.memset(s2[:, :, :], 0.0)
            pool.drain()
            g.affine_select(out=ident[:, :], in_=ident[:, :], compare_op=ALU.not_equal, fill=1.0,
                            base=0, pattern=[[-1, P]], channel_multiplier=1)
            g.affine_select(out=tri[:, :], in_=tri[:, :], compare_op=ALU.is_ge, fill=0.0,
                            base=0, pattern=[[1, P]], channel_multiplier=-1)
            g.affine_select(out=pair_diag[:, 0:HD], in_=pair_diag[:, 0:HD], compare_op=ALU.is_gt, fill=0.0,
                            base=HD, pattern=[[0, HD]], channel_multiplier=-1)
            g.affine_select(out=pair_diag[:, HD:P], in_=pair_diag[:, HD:P], compare_op=ALU.is_ge, fill=0.0,
                            base=-HD, pattern=[[0, HD]], channel_multiplier=1)
            for n, w in enumerate(LEVELS):
                v = level[:, n, :].rearrange("p (a c) -> p a c", c=2 * w)
                g.affine_select(out=v, in_=v, compare_op=ALU.is_ge, fill=0.0, base=0,
                                pattern=[[-2 * w, P // (2 * w)], [0, 2 * w]], channel_multiplier=1)
            sv = same8[:, :].rearrange("p (b t) -> p b t", t=DS)
            g.affine_select(out=sv, in_=sv, compare_op=ALU.is_ge, fill=0.0, base=0,
                            pattern=[[-DS, DB], [0, DS]], channel_multiplier=1)
            g.affine_select(out=seq_of[:, :], in_=seq_of[:, :], compare_op=ALU.is_ge, fill=0.0, base=0,
                            pattern=[[-DS, DB]], channel_multiplier=1)
            pool.drain()
            for n, w in enumerate(LEVELS):
                v = level[:, n, :].rearrange("p (a c) -> p a c", c=2 * w)
                g.affine_select(out=v, in_=v, compare_op=ALU.is_gt, fill=0.0, base=w,
                                pattern=[[2 * w, P // (2 * w)], [0, 2 * w]], channel_multiplier=-1)
            g.affine_select(out=sv, in_=sv, compare_op=ALU.is_gt, fill=0.0, base=DS,
                            pattern=[[DS, DB], [0, DS]], channel_multiplier=-1)
            g.affine_select(out=seq_of[:, :], in_=seq_of[:, :], compare_op=ALU.is_gt, fill=0.0, base=DS,
                            pattern=[[DS, DB]], channel_multiplier=-1)
            pool.drain()
            for n, w in enumerate(LEVELS):
                v = level[:, n, :].rearrange("p (a c) -> p a c", c=2 * w)
                g.affine_select(out=v, in_=v, compare_op=ALU.is_ge, fill=0.0, base=-w,
                                pattern=[[0, P // (2 * w)], [1, 2 * w]], channel_multiplier=0)
            g.tensor_tensor(tri8[:, :], tri[:, 0:NS], same8[:, :], ALU.mult)
            d_int = sc[:, 0, :].bitcast(I32)
            g.iota(d_int, pattern=[[-1, 2 * WIN]], base=WIN, channel_multiplier=1)
            pool.drain()
            g.tensor_copy(dist[:, :], d_int)
            pool.drain()
            g.affine_select(out=dist[:, :], in_=dist[:, :], compare_op=ALU.is_ge, fill=FAR,
                            base=WIN, pattern=[[-1, 2 * WIN]], channel_multiplier=1)
            pool.drain()
            g.affine_select(out=dist[:, :], in_=dist[:, :], compare_op=ALU.is_ge, fill=FAR,
                            base=0, pattern=[[1, 2 * WIN]], channel_multiplier=-1)
            pool.drain()
            g.tensor_copy(dist_old[:, :], dist[:, 0:WIN])
            pool.drain()
            g.memset(dist[:, 0:WIN], FAR)
            pool.drain()
            pool.sem_inc(s["consts"], 1)
            pool.sem_inc(s["h_out"], 16)
            pool.wait_ge(s["conv_ps"], 4)
            g.memset(s2s[:, :, :, :], 0.0)
            g.memset(kgm[:, :, :, :], 0.0)
            g.memset(qgm[:, :, :, :], 0.0)
            pool.drain()
            pool.sem_inc(s["over_clear"], 1)

        @block.tensor
        def _(pe):
            t = nc.tensor
            pe.wait_ge(s["consts"], 1)
            pe.wait_ge(s["w_in_in"], 16 * (KD + 2 * GRP + 1))

            def x_T(i, r):
                pe.wait_ge(s["xn_ready"], i + 1)
                for k in range(KD):
                    m = t.transpose(bank[6 + k // 4][:, (k % 4) * P:(k % 4) * P + r], xn[0:r, k * P:(k + 1) * P], ident[0:r, 0:r])
                m.then_inc(s["xT_ps"], 1)

            def dqkv(i, r, blocks):
                for n in blocks:
                    b, c = divmod(n, 4)
                    if n == 0:
                        pe.wait_ge(s["aT_ready"], i + 1)
                    if n == 8:
                        pe.wait_ge(s["cin_ready"], 3 * i + 1)
                    w = C_DN + n * P
                    for k in range(KD):
                        m = t.matmul(bank[6 + b % 2][:, c * P:c * P + r], w_in[:, k, w:w + P], aT[:, k, 0:r],
                                     start=(k == 0), stop=(k == KD - 1))
                    if c == 3:
                        m.then_inc(s["dqkv_ps"], 1)

            def queries(i, r, blocks):
                for c in blocks:
                    for k in range(KD):
                        m = t.matmul(bank[2][:, c * P:c * P + r], w_in[:, k, c * P:(c + 1) * P], aT[:, k, 0:r],
                                     start=(k == 0), stop=(k == KD - 1))
                    if c == GRP - 1:
                        m.then_inc(s["q_ps"], 1)

            def keys_values(i, r):
                for k in range(KD):
                    t.matmul(bank[3][0:r, 384:400], aT[:, k, 0:r], w_in[:, k, C_AB:INW],
                             start=(k == 0), stop=(k == KD - 1))
                for k in range(KD):
                    t.matmul(bank[3][0:r, 0:256], aT[:, k, 0:r], w_in[:, k, C_K:C_DN],
                             start=(k == 0), stop=(k == KD - 1))
                for k in range(KD):
                    m = t.matmul(bank[3][:, 256:256 + r], w_in[:, k, C_K:C_K + P], aT[:, k, 0:r],
                                 start=(k == 0), stop=(k == KD - 1))
                m.then_inc(s["kv_ps"], 1)

            def z_rows(i, r):
                pe.wait_ge(s["cin_ready"], 3 * i + 2)
                for k in range(KD):
                    m = t.matmul(bank[7][0:r, :], aT[:, k, 0:r], w_in[:, k, C_Z:C_AB],
                                 start=(k == 0), stop=(k == KD - 1))
                m.then_inc(s["z_ps"], 1)

            def front(i, r):
                x_T(i, r)
                dqkv(i, r, range(CB))
                queries(i, r, range(GRP))
                keys_values(i, r)
                z_rows(i, r)

            def tile(i, r, sampled, ahead):
                pe.wait_ge(s["q_sb"], i + 1)
                pe.wait_ge(s["kv_sb"], i + 1)
                if not sampled:
                    for hh in range(AH):
                        g, p = divmod(hh, GRP)
                        m = t.matmul(bank[hh // 2][:, (hh % 2) * 256:(hh % 2) * 256 + 256],
                                     qT[g * HD:(g + 1) * HD, p, :], kT[g * HD:(g + 1) * HD, :], start=True, stop=True)
                    m.then_inc(s["score_ps"], 1)
                else:
                    for b in range(3):
                        for k in range(KD):
                            m = t.matmul(bank[b][0:r, :], aT[:, k, 0:r], w_in[:, k, C_DN + b * 512:C_DN + (b + 1) * 512],
                                         start=(k == 0), stop=(k == KD - 1))
                        m.then_inc(s["conv_ps"], 1)
                    pe.wait_ge(s["stc_in"], 16)
                    for c in range(CB):
                        m = t.transpose(bank[3][:, c * 24:(c + 1) * 24], stconv[:, c * P:(c + 1) * P], ident[0:24, 0:24])
                    m.then_inc(s["stc_ps"], 1)
                pe.wait_ge(s["silu_done"], i + 1)
                pe.wait_ge(s["soft_in"], i + 1)
                for c in range(CB):
                    m = t.transpose(bank[4 + c // 4][0:r, (c % 4) * P:(c % 4 + 1) * P], cs[:, c, 0:r], ident[:, :])
                m.then_inc(s["rows_ps"], 1)
                pe.wait_ge(s["gate_ready"], i + 1)
                pe.wait_ge(s["z_sb"], i + 1)
                cum = tri8 if sampled else tri
                same = same8 if sampled else ones
                t.matmul(bank[7][0:r, 0:DH], cum[0:r, 0:r], gt[0:r, 5, :], start=True, stop=True)
                t.matmul(bank[7][0:r, DH:2 * DH], same[0:r, 0:r], gt[0:r, 5, :], start=True, stop=True)
                if sampled:
                    pe.wait_ge(s["mm_masked"], 1)
                    m = t.matmul(bank[7][:, 64:128], ones[0:r, :], gmb[0:r, :, :], start=True, stop=True)
                    pe.wait_ge(s["conv_sb"], 2)
                else:
                    m = t.matmul(bank[7][:, 64:64 + DH], ones[0:r, :], gt[0:r, 5, :], start=True, stop=True)
                    pe.wait_ge(s["sc_ready"], i + 1)
                for hh in range(DH):
                    m = t.matmul(bank[hh // 4][0:r, (hh % 4) * P:(hh % 4) * P + r],
                                 gt[0:r, 5, hh:hh + 1].to_broadcast([r, r]), cum[0:r, 0:r], start=True, stop=True)
                m.then_inc(s["gsum_ps"], 1)
                if not sampled:
                    pe.wait_ge(s["probs_ready"], i + 1)
                    pe.wait_ge(s["e_in"], i + 1)
                    for hh in range(AH):
                        for b in range(2):
                            m = t.transpose(bank[hh // 2][:, ((hh % 2) * 2 + b) * P:((hh % 2) * 2 + b + 1) * P],
                                            sc[:, hh, b * P:(b + 1) * P], ident[:, :])
                    m.then_inc(s["pT_ps"], 1)
                pe.wait_ge(s["drow_ready"], i + 1)
                for n, b in ((1, 4), (2, 5), (0, 6), (3, 7)):
                    for c in range(4):
                        m = t.transpose(bank[b][:, c * P:c * P + r], rows[0:r, n, c * P:(c + 1) * P], ident[0:r, 0:r])
                m.then_inc(s["rT_ps"], 1)
                if not sampled:
                    pe.wait_ge(s["pT_sb"], i + 1)
                for c in range(4):
                    m = t.transpose(bank[0][:, c * P:c * P + r], rows[0:r, 4, c * P:(c + 1) * P], ident[0:r, 0:r])
                m.then_inc(s["rT_ps"], 1)
                if not sampled:
                    for hh in range(AH):
                        g, p = divmod(hh, GRP)
                        for b, v in enumerate((v_old[:, :], kv[:, 1, :])):
                            m = t.matmul(bank[1][g * HD:(g + 1) * HD, p * P:(p + 1) * P],
                                         v[:, g * HD:(g + 1) * HD], pT[:, hh, b, :], start=(b == 0), stop=(b == 1))
                    m.then_inc(s["att_ps"], 1)
                pe.wait_ge(s["rT_a"], i + 1)
                pe.wait_ge(s["rT_v"], i + 1)
                for hh in range(DH):
                    c, o = hh // 2, (hh % 2) * HD
                    t.matmul(bank[2 + hh % 2][0:r, c * P:c * P + r],
                             rT[o:o + HD, 1, c, 0:r], rT[o:o + HD, 2, c, 0:r], start=True, stop=True)
                    m = t.matmul(bank[4 + hh % 2][0:r, c * P:c * P + r],
                                 rT[o:o + HD, 1, c, 0:r], rT[o:o + HD, 0, c, 0:r], start=True, stop=True)
                m.then_inc(s["gram_ps"], 1)
                if sampled:
                    pe.wait_ge(s["kmask_ready"], 1)
                    pe.wait_ge(s["state_in"], 16 * 2 * DB)
                    for c in range(PAIRS):
                        for b in range(DB):
                            m = t.matmul(bank[6][0:r, c * P:(c + 1) * P], kgm[:, b, c, :], s2s[:, b, c, :],
                                         start=(b == 0), stop=(b == DB - 1))
                else:
                    for c in range(PAIRS):
                        m = t.matmul(bank[6][0:r, c * P:(c + 1) * P], rT[:, 3, c, 0:r], s2[:, c, :], start=True, stop=True)
                m.then_inc(s["kgs_ps"], 1)
                n_lv = 3 if sampled else len(LEVELS) - 1
                if not sampled:
                    pe.wait_ge(s["att_sb"], i + 1)
                gaps = {2: ((0, 1), (2,)), 3: ((3, 4), (5,)), 4: ((6, 7), (8,)), 5: ((9, 10), (11,))}
                for n in range(n_lv):
                    if ahead and n in gaps:
                        dqkv(i + 1, P, gaps[n][0])
                    pe.wait_ge(s["b_ready"], NB * i + n + 1)
                    if n:
                        pe.wait_ge(s["xx_ready"], NX * i + n)
                    for hh in range(DH):
                        rhs = xx[0:r, hh, 0, 0:r] if n else ident[0:r, 0:r]
                        m = t.matmul(bank[hh // 4][0:r, (hh % 4) * P:(hh % 4) * P + r], bt[0:r, hh, 0:r], rhs,
                                     start=True, stop=True)
                    m.then_inc(s["t_ps"], 1)
                    if ahead and n == 1:
                        pe.wait_ge(s["y0_ready"], i + 1)
                        x_T(i + 1, P)
                    if ahead and n in gaps:
                        dqkv(i + 1, P, gaps[n][1])
                    if n:
                        pe.wait_ge(s["t_sb"], (NX - 1) * i + n)
                        for hh in range(DH):
                            b, o = 2 + hh // 2, (hh % 2) * 256
                            t.matmul(bank[b][0:r, o:o + r], xx[0:r, hh, 1, 0:r], t1[0:r, hh, 0:r], start=True, stop=True)
                            m = t.matmul(bank[b][0:r, o + P:o + P + r], t1[0:r, hh, 0:r], xx[0:r, hh, 1, 0:r], start=True, stop=True)
                        m.then_inc(s["zz_ps"], 1)
                pe.wait_ge(s["y0_ready"], i + 1)
                pe.wait_ge(s["xx_ready"], NX * i + n_lv)

                def heads(b, lhs, rhs, done):
                    for hh in range(DH):
                        m = t.matmul(bank[b][0:r, hh * HD:(hh + 1) * HD], lhs(hh), rhs[0:r, hh * HD:(hh + 1) * HD],
                                     start=True, stop=True)
                    m.then_inc(done, 1)

                if ahead:
                    pe.wait_ge(s["cin_ready"], 3 * i + 6)
                heads(6, lambda hh: xx[0:r, hh, 1, 0:r], y0, s["y1_ps"])
                if ahead:
                    queries(i + 1, P, (0,))
                if not sampled:
                    pe.wait_ge(s["b_ready"], NB * i + NB)
                    pe.wait_ge(s["y1_sb"], i + 1)
                    heads(7, lambda hh: bt[0:r, hh, 0:r], y1, s["ty_ps"])
                    if ahead:
                        queries(i + 1, P, (1,))
                    pe.wait_ge(s["ty_sb"], i + 1)
                    heads(6, lambda hh: xx[0:r, hh, 1, 0:r], ty, s["yz_ps"])
                    if ahead:
                        queries(i + 1, P, (2, 3))
                pe.wait_ge(s["vn_ready"], i + 1)
                for c in range(PAIRS):
                    o = bank[0][0:r, c * P:(c + 1) * P]
                    if sampled:
                        for b in range(DB):
                            t.matmul(o, qgm[:, b, c, :], s2s[:, b, c, :], start=(b == 0), stop=False)
                    else:
                        t.matmul(o, rT[:, 4, c, 0:r], s2[:, c, :], start=True, stop=False)
                    for e in range(2):
                        hh = 2 * c + e
                        m = t.matmul(bank[0][0:r, hh * HD:(hh + 1) * HD], qk[0:r, hh, 0:r],
                                     vn[0:r, hh * HD:(hh + 1) * HD], start=False, stop=(e == 1))
                m.then_inc(s["o_ps"], 1)
                if sampled:
                    for b in range(DB):
                        pe.wait_ge(s["ktm_ready"], b + 1)
                        if b >= 2:
                            pe.wait_ge(s["supd_done"], b - 1)
                        for c in range(PAIRS):
                            m = t.matmul(bank[1 + b % 2][:, c * P:(c + 1) * P], ktm[0:r, b % 2, c * P:(c + 1) * P],
                                         vn[0:r, c * P:(c + 1) * P], start=True, stop=True)
                        m.then_inc(s["supd_ps"], 1)
                else:
                    for c in range(PAIRS):
                        m = t.matmul(bank[1][:, c * P:(c + 1) * P], rows[0:r, 5, c * P:(c + 1) * P],
                                     vn[0:r, c * P:(c + 1) * P], start=True, stop=True)
                    m.then_inc(s["upd_ps"], 1)
                if ahead:
                    keys_values(i + 1, P)
                    z_rows(i + 1, P)
                    pe.wait_ge(s["kv_sb"], i + 2)
                pe.wait_ge(s["dn_ready"], i + 1)
                if sampled:
                    sampled_attention()
                for c in range(4):
                    m = t.transpose(bank[3][:, c * P:c * P + r], dn[0:r, c * P:(c + 1) * P], ident[0:r, 0:r])
                m.then_inc(s["dnT_ps"], 1)
                pe.wait_ge(s["dnT_sb"], i + 1)
                pe.wait_ge(s["w_out_in"], 16 * 9)
                for n in range(2):
                    for k in range(KD):
                        m = t.matmul(bank[4 + n][0:r, :], (attT if k < 4 else dnT)[:, k % 4, 0:r], w_out[:, k, n * 512:(n + 1) * 512],
                                     start=(k == 0), stop=(k == KD - 1))
                m.then_inc(s["proj_ps"], 1)

            def sampled_attention():
                pe.wait_ge(s["cache_in"], 32)
                for b in range(DB):
                    m = t.transpose(bank[1 + b // 4][:, (b % 4) * P:(b % 4 + 1) * P], kc[:, b, :], ident[:, :])
                m.then_inc(s["kcT_ps"], 1)
                pe.wait_ge(s["kcT_sb"], 1)
                for b in range(DB):
                    for g in range(2):
                        o = (b % 3) * SKEYS
                        q = qT[:, :, :].rearrange("p c t -> p (c t)")[g * HD:(g + 1) * HD, b * GRP * DS:(b + 1) * GRP * DS]
                        bk = bank[1 + 3 * g + b // 3]
                        t.matmul(bk[0:GRP * DS, o:o + WIN], q, kcT[g * HD:(g + 1) * HD, b, :], start=True, stop=True)
                        m = t.matmul(bk[0:GRP * DS, o + WIN:o + SKEYS], q,
                                     kT[g * HD:(g + 1) * HD, P + b * DS:P + (b + 1) * DS], start=True, stop=True)
                m.then_inc(s["score_ps"], 1)
                pe.wait_ge(s["sprobs"], 1)
                for n in range(2 * DB):
                    t.transpose(bank[1][:, n * 32:(n + 1) * 32], ssc[0:32, n, 0:WIN], ident[0:32, 0:32])
                    m = t.transpose(bank[2][0:DS, n * 32:(n + 1) * 32], ssc[0:32, n, WIN:SKEYS], ident[0:32, 0:32])
                m.then_inc(s["pT_ps"], 1)
                pe.wait_ge(s["pT_sb"], TILES + 1)
                pe.wait_ge(s["vnew_in"], 16 * DB)
                for b in range(DB):
                    for g in range(2):
                        n = b * 2 + g
                        o = bank[3][g * HD:(g + 1) * HD, n * 32 % 512 - g * 32:n * 32 % 512 - g * 32 + 32]
                        t.matmul(o, vc[:, b, g * HD:(g + 1) * HD], spT[:, n, :], start=True, stop=False)
                        m = t.matmul(o, vnew[0:DS, b, g * HD:(g + 1) * HD], spTn[0:DS, n, :], start=False, stop=True)
                m.then_inc(s["att_ps"], 1)
                pe.wait_ge(s["att_sb"], TILES + 1)

            NB = len(LEVELS)
            NX = len(LEVELS) - 1
            front(0, P)
            with pe.Fori(0, TILES - 1) as i:
                tile(i, P, False, True)
            tile(TILES - 1, P, False, False)
            for b in range(3):
                for k in range(KD):
                    m = t.matmul(bank[b][0:3, :], aT[:, k, P - TAPS + 1:P], w_in[:, k, C_DN + b * 512:C_DN + (b + 1) * 512],
                                 start=(k == 0), stop=(k == KD - 1))
            m.then_inc(s["conv_ps"], 1)
            front(TILES, NS)
            tile(TILES, NS, True, False)

        @block.scalar
        def _(act):
            ac = nc.scalar
            act.wait_ge(s["consts"], 1)
            act.wait_ge(s["const_in"], 16 * (6 + 1 + TAPS + AH))
            ac.activation(neg_a[:, :], neg_a[:, :], ACT.Exp)
            act.drain()
            ac.mul(neg_a[:, :], neg_a[:, :], -1.0)

            def x_rms(i, r):
                act.wait_ge(s["x_in"], 16 * (i + 1))
                ac.activation(aT[0:r, :, :].rearrange("p k t -> p (k t)"), x[0:r, :], ACT.Square, accum_out=st[0:r, 0:1])
                act.drain()
                ac.activation(st[0:r, 1:2], st[0:r, 0:1], ACT.Sqrt, scale=1.0 / D, bias=eps[0:r, :]).then_inc(s["rms"], 1)

            def conv_in(i, r, sampled, b):
                act.wait_ge(s["dqkv_ps"], 3 * i + b + 1)
                if sampled:
                    src = bank[6 + b % 2][:, :].rearrange("p (c t) -> p c t", c=4)[:, :, 0:r].rearrange("p c (q t) -> p c q t", t=DS)
                    for c in range(4):
                        dst = cin[:, b * 4 + c, 0:DB * 11].rearrange("p (q t) -> p q t", t=11)[:, :, 3:11]
                        m = ac.activation(dst, src[:, c], ACT.Copy)
                else:
                    m = ac.activation(cin[:, b * 4:b * 4 + 4, 3:3 + P],
                                      bank[6 + b % 2][:, :].rearrange("p (c t) -> p c t", c=4), ACT.Copy)
                m.then_inc(s["cin_ready"], 1)

            def queries(i, r, sampled):
                act.wait_ge(s["q_ps"], i + 1)
                if sampled:
                    for p in range(GRP):
                        m = ac.activation(qT_s[:, :, p, :], bank[2][:, p * P:p * P + NS].rearrange("p (b t) -> p b t", b=DB), ACT.Copy, scale=HD ** -0.5)
                else:
                    m = ac.activation(qT[:, :, 0:r], bank[2][:, :].rearrange("p (c t) -> p c t", c=GRP)[:, :, 0:r], ACT.Copy, scale=HD ** -0.5)
                m.then_inc(s["q_sb"], 1)

            def keys_values_z(i, r, sampled):
                act.wait_ge(s["kv_ps"], i + 1)
                if sampled:
                    act.wait_ge(s["state_out"], 16 * (2 + DH))
                ac.activation(kT[:, P:P + r], bank[3][:, 256:256 + r], ACT.Copy)
                ac.activation(ab_raw[0:r, :], bank[3][0:r, 384:400], ACT.Copy)
                ac.activation(kv[0:r, :, :], bank[3][0:r, 0:256].rearrange("p (c t) -> p c t", c=2), ACT.Copy).then_inc(s["kv_sb"], 1)
                act.wait_ge(s["z_ps"], i + 1)
                ac.activation(z_raw[0:r, :], bank[7][0:r, :], ACT.Copy).then_inc(s["z_sb"], 1)

            def front(i, r, sampled):
                x_rms(i, r)
                for b in range(3):
                    conv_in(i, r, sampled, b)
                queries(i, r, sampled)
                keys_values_z(i, r, sampled)

            def tile(i, r, sampled, ahead):
                if sampled:
                    act.wait_ge(s["over_clear"], 1)
                    act.wait_ge(s["conv_ps"], 4)
                    for b in range(3):
                        m = ac.activation(crow[0:r, b * 512:(b + 1) * 512], bank[b][0:r, :], ACT.Copy)
                    m.then_inc(s["conv_sb"], 1)
                    act.wait_ge(s["stc_ps"], 1)
                    for c in range(CB):
                        m = ac.activation(cin[:, c, 0:DB * 11].rearrange("p (q t) -> p q t", t=11)[:, :, 0:3],
                                          bank[3][:, c * 24:(c + 1) * 24].rearrange("p (q t) -> p q t", t=3), ACT.Copy)
                    m.then_inc(s["stc_sb"], 1)
                act.wait_ge(s["conv_done"], i + 1)
                ac.activation(cs[:, :, 0:r], cacc[:, :, 0:r], ACT.Silu).then_inc(s["silu_done"], 1)
                act.wait_ge(s["z_sb"], i + 1)
                ac.activation(zs[0:r, :], z_raw[0:r, :], ACT.Silu)
                act.wait_ge(s["soft_in"], i + 1)
                ac.activation(gt[0:r, 2, :], gt[0:r, 1, :], ACT.Exp, scale=-1.0)
                ac.activation(gt[0:r, 3, :], ab_raw[0:r, DH:2 * DH], ACT.Exp, scale=-1.0)
                act.drain()
                ac.activation(gt[0:r, 2, :], gt[0:r, 2, :], ACT.Ln, bias=one[0:r, :]).then_inc(s["soft_out"], 1)
                act.wait_ge(s["rows_ps"], i + 1)
                for n in range(2):
                    m = ac.activation(sq[0:r, n * 512:(n + 1) * 512], bank[4 + n][0:r, :], ACT.Square)
                m.then_inc(s["sq_done"], 1)
                act.wait_ge(s["ssq_done"], i + 1)
                ac.activation(rn[0:r, 1, :], rn[0:r, 0, :], ACT.Sqrt, bias=eps[0:r, :]).then_inc(s["rn_sqrt"], 1)
                if not sampled:
                    act.wait_ge(s["nm_ready"], i + 1)
                    for hh in range(AH):
                        ac.activation(sc[:, hh, :], sc[:, hh, :], ACT.Exp, bias=am[:, 2, hh:hh + 1], accum_out=am[:, 4, hh:hh + 1])
                    act.drain()
                    ac.activation(am[:, 3, :], am[:, 3, :], ACT.Exp).then_inc(s["prob_done"], 1)
                act.wait_ge(s["e_in"], i + 1)
                ac.activation(gt[0:r, 8, :], gt[0:r, 6, :], ACT.Exp)
                ac.activation(gt[0:r, 9, :], gt[0:r, 7, :], ACT.Exp)
                if sampled:
                    ac.activation(egb[:, :, :], egb[:, :, :], ACT.Exp)
                else:
                    ac.activation(eg[:, :], eg[:, :], ACT.Exp)
                ac.activation(dt_[0:r, :, 0:r], dt_[0:r, :, 0:r], ACT.Exp).then_inc(s["exp_ready"], 1)
                if not sampled:
                    act.wait_ge(s["pT_ps"], i + 1)
                    for b in range(4):
                        m = ac.activation(pT[:, 2 * b:2 * b + 2, :, :], bank[b][:, :].rearrange("p (h c t) -> p h c t", h=2, c=2), ACT.Copy)
                    m.then_inc(s["pT_sb"], 1)
                act.wait_ge(s["rT_ps"], 2 * i + 2)
                for n, b in ((1, 4), (2, 5), (4, 0)):
                    m = ac.activation(rT[:, n, :, 0:r], bank[b][:, :].rearrange("p (c t) -> p c t", c=4)[:, :, 0:r], ACT.Copy)
                m.then_inc(s["rT_a"], 1)
                if not sampled:
                    act.wait_ge(s["att_ps"], i + 1)
                    ac.activation(attT[:, :, :], bank[1][:, :].rearrange("p (c t) -> p c t", c=4), ACT.Copy)
                    ac.activation(kT[:, 0:P], kT[:, P:2 * P], ACT.Copy)
                    ac.activation(v_old[:, :], kv[:, 1, :], ACT.Copy)
                    ac.activation(dist[:, 0:WIN], dist_old[:, :], ACT.Copy).then_inc(s["att_sb"], 1)
                if ahead:
                    x_rms(i + 1, P)
                n_lv = 3 if sampled else len(LEVELS) - 1
                for n in range(1, n_lv):
                    act.wait_ge(s["t_ps"], NX * i + n + 1)
                    for b in range(2):
                        m = ac.activation(t1[0:r, 4 * b:4 * b + 4, 0:r],
                                          bank[b][0:r, :].rearrange("p (c t) -> p c t", c=4)[:, :, 0:r], ACT.Copy)
                    m.then_inc(s["t_sb"], 1)
                    if ahead and n in (3, 4, 5):
                        conv_in(i + 1, P, False, n - 3)
                if not sampled:
                    act.wait_ge(s["y1_ps"], i + 1)
                    ac.activation(y1[0:r, :], bank[6][0:r, :], ACT.Copy).then_inc(s["y1_sb"], 1)
                    act.wait_ge(s["ty_ps"], i + 1)
                    ac.activation(ty[0:r, :], bank[7][0:r, :], ACT.Copy).then_inc(s["ty_sb"], 1)
                if ahead:
                    queries(i + 1, P, False)
                act.wait_ge(s["o_ps"], i + 1)
                ac.activation(sq[0:r, 0:512], bank[0][0:r, :], ACT.Square).then_inc(s["osq_done"], 1)
                act.wait_ge(s["ossq"], i + 1)
                ac.activation(rn[0:r, 1, 0:DH], rn[0:r, 0, 0:DH], ACT.Sqrt, scale=1.0 / HD, bias=eps[0:r, :]).then_inc(s["orms"], 1)
                if ahead:
                    keys_values_z(i + 1, P, False)
                if sampled:
                    act.wait_ge(s["kcT_ps"], 1)
                    for b in range(2):
                        m = ac.activation(kcT[:, 4 * b:4 * b + 4, :], bank[1 + b][:, :].rearrange("p (c t) -> p c t", c=4), ACT.Copy)
                    m.then_inc(s["kcT_sb"], 1)
                    act.wait_ge(s["nm_ready"], TILES + 1)
                    ac.activation(ssc[0:32, :, :], ssc[0:32, :, :], ACT.Exp)
                    ac.activation(sm[0:32, 3, :], sm[0:32, 3, :], ACT.Exp).then_inc(s["sexp"], 1)
                    act.wait_ge(s["pT_ps"], TILES + 1)
                    ac.activation(spT[:, :, :], bank[1][:, :].rearrange("p (n r) -> p n r", r=32), ACT.Copy)
                    ac.activation(spTn[0:DS, :, :], bank[2][0:DS, :].rearrange("p (n r) -> p n r", r=32), ACT.Copy).then_inc(s["pT_sb"], 1)
                    act.wait_ge(s["att_ps"], TILES + 1)
                    for p in range(GRP):
                        src = bank[3][:, :].rearrange("p (b g r) -> p b g r", b=DB, g=2)[:, :, 0, p * DS:(p + 1) * DS]
                        m = ac.activation(attT[:, p, 0:NS].rearrange("p (b t) -> p b t", b=DB), src, ACT.Copy)
                    m.then_inc(s["att_sb"], 1)
                act.wait_ge(s["dnT_ps"], i + 1)
                ac.activation(dnT[:, :, 0:r], bank[3][:, :].rearrange("p (c t) -> p c t", c=4)[:, :, 0:r], ACT.Copy).then_inc(s["dnT_sb"], 1)

            NX = len(LEVELS) - 1
            front(0, P, False)
            with act.Fori(0, TILES - 1) as i:
                tile(i, P, False, True)
            tile(TILES - 1, P, False, False)
            act.wait_ge(s["conv_ps"], 1)
            for b in range(3):
                m = ac.activation(stage3[0:3, b * 512:(b + 1) * 512], bank[b][0:3, :], ACT.Copy)
            m.then_inc(s["conv_sb"], 1)
            act.wait_ge(s["conv_sb"], 1)
            act.dma_start(out["c_p"][0, 0], stage3[0:3, :]).then_inc(s["misc_in"], 16)
            act.wait_ge(s["misc_in"], 16)
            front(TILES, NS, True)
            tile(TILES, NS, True, False)

        @block.vector
        def _(dve):
            v = nc.vector

            def bc(ap, n):
                sh = list(ap.shape)
                return ap.rearrange("p (h o) -> p h o", o=1).to_broadcast([sh[0], sh[1], n])

            def hd(ap):
                return ap.rearrange("p (h d) -> p h d", d=HD)

            dve.wait_ge(s["consts"], 1)
            dve.wait_ge(s["const_in"], 16 * (6 + 1 + TAPS + AH))

            def x_norm(i, r):
                dve.wait_ge(s["rms"], i + 1)
                v.reciprocal(st[0:r, 2:3], st[0:r, 1:2])
                dve.drain()
                v.tensor_scalar(xn[0:r, :], x[0:r, :], st[0:r, 2:3], None, ALU.mult).then_inc(s["xn_ready"], 1)

            def x_T(i, r):
                dve.wait_ge(s["xT_ps"], i + 1)
                for b in range(2):
                    m = v.tensor_tensor(aT[:, 4 * b:4 * b + 4, 0:r], bank[6 + b][:, :].rearrange("p (k t) -> p k t", k=4)[:, :, 0:r],
                                        bc(g_mix[:, 4 * b:4 * b + 4], r), ALU.mult)
                m.then_inc(s["aT_ready"], 1)

            def conv(i, sampled, b, taps):
                if taps[0] == 0:
                    dve.wait_ge(s["cin_ready"], 3 * i + b + 1)
                for j in taps:
                    for c in range(4 * b, 4 * b + 4):
                        if sampled:
                            src = cin[:, c, 0:DB * 11].rearrange("p (q t) -> p q t", t=11)[:, :, j:j + DS]
                            dst = cacc[:, c, 0:NS].rearrange("p (q t) -> p q t", t=DS)
                        else:
                            src, dst = cin[:, c, j:j + P], cacc[:, c, :]
                        if j == 0:
                            m = v.tensor_scalar(dst, src, cw[:, j, c:c + 1], None, ALU.mult)
                        else:
                            m = v.scalar_tensor_tensor(dst, src, cw[:, j, c:c + 1], dst, ALU.mult, ALU.add)
                    if j < TAPS - 1:
                        dve.drain()
                if b == 2 and taps[-1] == TAPS - 1:
                    m.then_inc(s["conv_done"], 1)
                    if not sampled:
                        dve.drain()
                        v.tensor_copy(cin[:, :, 0:TAPS - 1], cin[:, :, P:P + TAPS - 1])

            def front(i, r, sampled):
                x_norm(i, r)
                x_T(i, r)
                if sampled:
                    dve.wait_ge(s["stc_sb"], 1)
                for b in range(3):
                    conv(i, sampled, b, range(TAPS))

            def tile(i, r, sampled, ahead):
                dve.wait_ge(s["kv_sb"], i + 1)
                v.tensor_tensor(gt[0:r, 0, :], ab_raw[0:r, 0:DH], dtb[0:r, :], ALU.add)
                dve.drain()
                v.tensor_scalar(gt[0:r, 1, :], gt[0:r, 0, :], -1.0, None, ALU.mult)
                dve.drain()
                v.tensor_tensor(gt[0:r, 1, :], gt[0:r, 0, :], gt[0:r, 1, :], ALU.max).then_inc(s["soft_in"], 1)
                dve.wait_ge(s["soft_out"], i + 1)
                v.tensor_scalar(gt[0:r, 0, :], gt[0:r, 0, :], 0.0, None, ALU.max)
                v.tensor_scalar(gt[0:r, 3, :], gt[0:r, 3, :], 1.0, None, ALU.add)
                dve.drain()
                v.tensor_tensor(gt[0:r, 0, :], gt[0:r, 0, :], gt[0:r, 2, :], ALU.add)
                v.reciprocal(gt[0:r, 4, :], gt[0:r, 3, :])
                dve.drain()
                v.tensor_tensor(gt[0:r, 5, :], gt[0:r, 0, :], neg_a[0:r, :], ALU.mult).then_inc(s["gate_ready"], 1)
                if sampled:
                    dve.drain()
                    dve.wait_ge(s["over_clear"], 1)
                    v.tensor_tensor(gmb[0:r, :, :], gt[0:r, 5, :].rearrange("p (o h) -> p o h", o=1).to_broadcast([r, DB, DH]),
                                    bc(seq_of[0:r, :], DH), ALU.mult).then_inc(s["mm_masked"], 1)
                if not sampled:
                    dve.wait_ge(s["score_ps"], i + 1)
                    for hh in range(AH):
                        m = v.scalar_tensor_tensor(sc[:, hh, :], dist[:, :], SLOPE[hh],
                                                   bank[hh // 2][:, (hh % 2) * 256:(hh % 2 + 1) * 256], ALU.mult, ALU.add)
                    m.then_inc(s["sc_ready"], 1)
                    dve.drain()
                    v.tensor_reduce(am[:, 0, :], sc[:, :, :], AXX, ALU.max)
                    dve.drain()
                    v.tensor_tensor(am[:, 1, :], am[:, 0, :], sinks[:, :], ALU.max)
                    dve.drain()
                    v.tensor_tensor(am[:, 3, :], sinks[:, :], am[:, 1, :], ALU.subtract)
                    v.tensor_scalar(am[:, 2, :], am[:, 1, :], -1.0, None, ALU.mult).then_inc(s["nm_ready"], 1)
                dve.wait_ge(s["sq_done"], i + 1)
                v.tensor_reduce(rn[0:r, 0, :], hd(sq[0:r, :]), AXX, ALU.add).then_inc(s["ssq_done"], 1)
                dve.wait_ge(s["gsum_ps"], i + 1)
                v.tensor_copy(gt[0:r, 6, :], bank[7][0:r, 0:DH])
                dve.drain()
                v.tensor_tensor(gt[0:r, 7, :], bank[7][0:r, DH:2 * DH], gt[0:r, 6, :], ALU.subtract)
                for c in range(2):
                    if sampled:
                        v.tensor_copy(egb[c * HD:(c + 1) * HD, :, :],
                                      bank[7][c * HD:(c + 1) * HD, 64:128].rearrange("p (b h e) -> p b h e", b=DB, e=2)[:, :, :, c])
                    else:
                        v.tensor_copy(eg[c * HD:(c + 1) * HD, :],
                                      bank[7][c * HD:(c + 1) * HD, 64:64 + DH].rearrange("p (h e) -> p h e", e=2)[:, :, c])
                for hh in range(DH):
                    m = v.tensor_scalar(dt_[0:r, hh, 0:r], bank[hh // 4][0:r, (hh % 4) * P:(hh % 4) * P + r],
                                        gt[0:r, 6, hh:hh + 1], 0.0, ALU.subtract, ALU.min)
                m.then_inc(s["e_in"], 1)
                if not sampled:
                    dve.wait_ge(s["prob_done"], i + 1)
                    v.tensor_tensor(am[:, 5, :], am[:, 4, :], am[:, 3, :], ALU.add)
                    dve.drain()
                    v.reciprocal(am[:, 0, :], am[:, 5, :])
                    dve.drain()
                    v.tensor_tensor(sc[:, :, :], sc[:, :, :], bc(am[:, 0, :], 2 * WIN), ALU.mult).then_inc(s["probs_ready"], 1)
                dve.wait_ge(s["rn_sqrt"], i + 1)
                v.reciprocal(rn[0:r, 2, :], rn[0:r, 1, :])
                dve.drain()
                dve.wait_ge(s["exp_ready"], i + 1)
                v.tensor_scalar(gt[0:r, 10, :], rn[0:r, 2, 0:DH], HD ** -0.5, None, ALU.mult)
                v.tensor_tensor(gt[0:r, 11, :], rn[0:r, 2, DH:16], gt[0:r, 4, :], ALU.mult)
                v.tensor_tensor(gt[0:r, 7, :], rn[0:r, 2, DH:16], gt[0:r, 9, :], ALU.mult)
                dve.drain()
                v.tensor_tensor(gt[0:r, 0, :], gt[0:r, 11, :], gt[0:r, 8, :], ALU.mult)
                v.tensor_tensor(gt[0:r, 1, :], gt[0:r, 10, :], gt[0:r, 8, :], ALU.mult)
                dve.drain()
                for n, b, f in ((1, 5, rn[0:r, 2, DH:16]), (2, 5, gt[0:r, 11, :]), (0, 4, gt[0:r, 10, :]),
                                (3, 5, gt[0:r, 0, :]), (4, 4, gt[0:r, 1, :]), (5, 5, gt[0:r, 7, :])):
                    v.tensor_tensor(hd(rows[0:r, n, :]), hd(bank[b][0:r, :]), bc(f, HD), ALU.mult)
                v.tensor_tensor(hd(vb[0:r, :]), hd(bank[6][0:r, :]), bc(gt[0:r, 4, :], HD), ALU.mult).then_inc(s["drow_ready"], 1)
                cum = tri8 if sampled else tri
                v.tensor_tensor(dt_[0:r, :, 0:r], dt_[0:r, :, 0:r],
                                cum[0:r, 0:r].rearrange("p (o t) -> p o t", o=1).to_broadcast([r, DH, r]), ALU.mult)
                dve.wait_ge(s["rT_ps"], 2 * i + 1)
                for n, b in ((0, 6), (3, 7)):
                    m = v.tensor_copy(rT[:, n, :, 0:r], bank[b][:, :].rearrange("p (c t) -> p c t", c=4)[:, :, 0:r])
                m.then_inc(s["rT_v"], 1)
                if sampled:
                    dve.drain()
                    dve.wait_ge(s["rT_a"], TILES + 1)
                    for b in range(DB):
                        v.tensor_copy(kgm[:, b, :, b * DS:(b + 1) * DS], rT[:, 3, :, b * DS:(b + 1) * DS])
                        m = v.tensor_copy(qgm[:, b, :, b * DS:(b + 1) * DS], rT[:, 4, :, b * DS:(b + 1) * DS])
                    m.then_inc(s["kmask_ready"], 1)
                dve.wait_ge(s["gram_ps"], i + 1)
                for b in range(2):
                    v.tensor_tensor(lt[0:r, b:DH:2, 0:r], bank[2 + b][0:r, :].rearrange("p (c t) -> p c t", c=4)[:, :, 0:r],
                                    dt_[0:r, b:DH:2, 0:r], ALU.mult)
                    v.tensor_tensor(qk[0:r, b:DH:2, 0:r], bank[4 + b][0:r, :].rearrange("p (c t) -> p c t", c=4)[:, :, 0:r],
                                    dt_[0:r, b:DH:2, 0:r], ALU.mult)
                dve.drain()

                def cut(n):
                    v.tensor_tensor(bt[0:r, :, 0:r], lt[0:r, :, 0:r],
                                    level[0:r, n, 0:r].rearrange("p (o t) -> p o t", o=1).to_broadcast([r, DH, r]),
                                    ALU.mult).then_inc(s["b_ready"], 1)

                cut(0)
                dve.wait_ge(s["kgs_ps"], i + 1)
                v.tensor_tensor(y0[0:r, :], vb[0:r, :], bank[6][0:r, :], ALU.subtract).then_inc(s["y0_ready"], 1)
                ident_b = ident[0:r, 0:r].rearrange("p (o t) -> p o t", o=1)
                n_lv = 3 if sampled else len(LEVELS) - 1
                for n in range(n_lv):
                    dve.wait_ge(s["t_ps"], NX * i + n + 1)
                    if n == 0:
                        for b in range(2):
                            v.tensor_tensor(xx[0:r, 4 * b:4 * b + 4, 0, 0:r], ident_b.to_broadcast([r, 4, r]),
                                            bank[b][0:r, :].rearrange("p (c t) -> p c t", c=4)[:, :, 0:r], ALU.subtract)
                        m = v.tensor_tensor(xx[0:r, :, 1, 0:r], ident_b.to_broadcast([r, DH, r]), bt[0:r, :, 0:r], ALU.subtract)
                        m.then_inc(s["xx_ready"], 1)
                        dve.drain()
                        cut(n + 1)
                        if ahead:
                            x_norm(i + 1, P)
                    else:
                        if n + 1 < (n_lv if sampled else n_lv + 1):
                            cut(n + 1)
                        if ahead and n == 4:
                            conv(i + 1, False, 0, (0, 1))
                        if ahead and n == 5:
                            conv(i + 1, False, 0, (2, 3))
                        dve.wait_ge(s["zz_ps"], (NX - 1) * i + n)
                        for b in range(4):
                            xv = xx[0:r, 2 * b:2 * b + 2, :, 0:r]
                            zv = bank[2 + b][0:r, :].rearrange("p (h c t) -> p h c t", h=2, c=2)[:, :, :, 0:r]
                            m = v.tensor_tensor(xv, xv, zv, ALU.subtract)
                        m.then_inc(s["xx_ready"], 1)
                        if ahead and n == 1:
                            x_T(i + 1, P)
                if sampled:
                    dve.wait_ge(s["y1_ps"], i + 1)
                    v.tensor_copy(vn[0:r, :], bank[6][0:r, :]).then_inc(s["vn_ready"], 1)
                else:
                    if ahead:
                        conv(i + 1, False, 1, (0, 1))
                    dve.wait_ge(s["yz_ps"], i + 1)
                    v.tensor_tensor(vn[0:r, :], y1[0:r, :], bank[6][0:r, :], ALU.subtract).then_inc(s["vn_ready"], 1)
                    v.tensor_tensor(s2n[:, :, :], s2[:, :, :], bc(eg[:, :], P), ALU.mult)
                if sampled:
                    for b in range(DB):
                        if b >= 2:
                            dve.wait_ge(s["supd_ps"], b - 1)
                        v.tensor_scalar(ktm[0:r, b % 2, :], rows[0:r, 5, :], seq_of[0:r, b:b + 1], None, ALU.mult).then_inc(s["ktm_ready"], 1)
                        if b >= 1:
                            state_update(b - 1)
                    state_update(DB - 1)
                dve.wait_ge(s["osq_done"], i + 1)
                v.tensor_reduce(rn[0:r, 0, 0:DH], hd(sq[0:r, 0:512]), AXX, ALU.add).then_inc(s["ossq"], 1)
                if not sampled:
                    dve.drain()
                    dve.wait_ge(s["upd_ps"], i + 1)
                    for c in range(PAIRS):
                        v.tensor_tensor(s2[:, c, :], bank[1][:, c * P:(c + 1) * P], pair_diag[:, :], ALU.mult)
                    dve.drain()
                    v.tensor_tensor(s2[:, :, :], s2[:, :, :], s2n[:, :, :], ALU.add)
                dve.wait_ge(s["orms"], i + 1)
                v.reciprocal(rn[0:r, 2, 0:DH], rn[0:r, 1, 0:DH])
                dve.drain()
                v.tensor_tensor(hd(dn[0:r, :]), hd(bank[0][0:r, :]), bc(rn[0:r, 2, 0:DH], HD), ALU.mult)
                dve.drain()
                v.tensor_tensor(hd(dn[0:r, :]), hd(dn[0:r, :]),
                                dnn[0:r, :].rearrange("p (o d) -> p o d", o=1).to_broadcast([r, DH, HD]), ALU.mult)
                dve.drain()
                v.tensor_tensor(dn[0:r, :], dn[0:r, :], zs[0:r, :], ALU.mult).then_inc(s["dn_ready"], 1)
                if ahead:
                    conv(i + 1, False, 1, (2, 3))
                    conv(i + 1, False, 2, (0, 1, 2, 3))
                if sampled:
                    sampled_softmax()
                    v.memset(h[NS:P, :], 0.0)
                dve.wait_ge(s["proj_ps"], i + 1)
                dve.wait_ge(s["xres_in"], 16 * (i + 1))
                for n in range(2):
                    m = v.tensor_tensor(h[0:r, n * 512:(n + 1) * 512], x_res[0:r, n * 512:(n + 1) * 512], bank[4 + n][0:r, :], ALU.add)
                m.then_inc(s["h_ready"], 1)

            def state_update(b):
                dve.wait_ge(s["supd_ps"], b + 1)
                if b == 0:
                    dve.wait_ge(s["o_ps"], TILES + 1)
                for c in range(PAIRS):
                    v.tensor_scalar(s2s[:, b, c, :], s2s[:, b, c, :], egb[:, b, c:c + 1], None, ALU.mult)
                    v.tensor_tensor(s2n[:, c, :], bank[1 + b % 2][:, c * P:(c + 1) * P], pair_diag[:, :], ALU.mult)
                dve.drain()
                v.tensor_tensor(s2s[:, b, :, :], s2s[:, b, :, :], s2n[:, :, :], ALU.add).then_inc(s["supd_done"], 1)
                dve.drain()

            def sampled_softmax():
                dve.wait_ge(s["score_ps"], TILES + 1)
                for n in range(2 * DB):
                    v.scalar_tensor_tensor(ssc[0:32, n, :], dist_s[:, :], slope_s[:, n % 2:n % 2 + 1],
                                           bank[1 + 3 * (n % 2) + n // 6][0:32, (n // 2 % 3) * SKEYS:(n // 2 % 3 + 1) * SKEYS], ALU.mult, ALU.add)
                dve.drain()
                v.tensor_reduce(sm[0:32, 0, :], ssc[0:32, :, :], AXX, ALU.max)
                dve.drain()
                sk = sink_s[0:32, :].rearrange("p (o g) -> p o g", o=1).to_broadcast([32, DB, 2])
                as_bg = lambda ap: ap.rearrange("p (b g) -> p b g", g=2)
                v.tensor_tensor(as_bg(sm[0:32, 1, :]), as_bg(sm[0:32, 0, :]), sk, ALU.max)
                dve.drain()
                v.tensor_tensor(as_bg(sm[0:32, 3, :]), sk, as_bg(sm[0:32, 1, :]), ALU.subtract)
                v.tensor_tensor(ssc[0:32, :, :], ssc[0:32, :, :], bc(sm[0:32, 1, :], SKEYS), ALU.subtract).then_inc(s["nm_ready"], 1)
                dve.wait_ge(s["sexp"], 1)
                v.tensor_reduce(sm[0:32, 4, :], ssc[0:32, :, :], AXX, ALU.add)
                dve.drain()
                v.tensor_tensor(sm[0:32, 5, :], sm[0:32, 4, :], sm[0:32, 3, :], ALU.add)
                dve.drain()
                v.reciprocal(sm[0:32, 2, :], sm[0:32, 5, :])
                dve.drain()
                v.tensor_tensor(ssc[0:32, :, :], ssc[0:32, :, :], bc(sm[0:32, 2, :], SKEYS), ALU.mult).then_inc(s["sprobs"], 1)

            NX = len(LEVELS) - 1
            front(0, P, False)
            with dve.Fori(0, TILES - 1) as i:
                tile(i, P, False, True)
            tile(TILES - 1, P, False, False)
            front(TILES, NS, True)
            tile(TILES, NS, True, False)


def peer_block(nc, sems, a, out, h_rows):
    RING = 8
    STEP = 16
    ON_PE = (0, 1, 2, 3, 4, 5, 7, 9, 11, 13)
    PB = PLE // P
    NPE = len(ON_PE)
    with ExitStack() as ctx:
        def sb(name, shape, dt=F32):
            return ctx.enter_context(nc.sbuf_tensor(name, shape, dt))

        def sem(name):
            return sems.enter_context(nc.semaphore("peer_" + name))

        bank = [ctx.enter_context(nc.psum_tensor(f"pbank{b}", [P, 512], F32)) for b in range(8)]
        wq = sb("wq_sb", [P, KD, PH * 2 * P])
        keysT = sb("keysT_sb", [P, 16, P])
        ident = sb("p_ident", [P, P])
        g_ffn = sb("g_ffn_sb", [P, D])
        iota16 = sb("iota16", [P, TOPK])
        iota_i = sb("iota16i", [P, TOPK], I32)
        eps = sb("p_eps", [P, 1])
        c_nxt = sb("c_nxt", [P, D])
        h_cur = sb("h_cur", [P, D])
        c_cur = sb("c_cur", [P, D])
        st = sb("p_stats", [P, 4])
        gst = sb("gate_stats", [P, 8])
        wg = sb("ple_gate_sb", [P, KD, D])
        wi = sb("ple_in_sb", [P, PB, D])
        g_ple = sb("g_ple_sb", [P, KD])
        g_fin = sb("g_fin_sb", [P, D])
        ple = sb("p_tile", [P, PLE])
        pleT = sb("pT_tile", [P, PB, P])
        cT = sb("cT_sb", [P, KD, P])
        qT = sb("pqT_sb", [P, 16, P])
        q_flat = qT[:, :, :].rearrange("p n t -> p (n t)")
        y, en = q_flat[:, 0:D], q_flat[:, D:2 * D]
        sco = sb("key_scores", [P, 16, P])
        v1 = sb("top_val", [P, 2, TOPK])
        x1 = sb("top_idx", [P, 2, TOPK], U32)
        x1f = sb("top_idxf", [P, 2, TOPK])
        cand = sb("cand", [P, TOPK, TOPK])
        cand2 = sb("cand_left", [P, TOPK * TOPK])
        sst = cand[:, :, :].rearrange("p a b -> p (a b)").rearrange("p (f n) -> p f n", f=2)
        sst2 = cand2[:, :].rearrange("p (f n) -> p f n", f=2)
        sc16 = sb("best_val", [P, TOPK])
        ci = sb("best_idx", [P, TOPK], U32)
        cab = sb("best_ab", [P, 2, TOPK], U32)
        cabf = sb("best_abf", [P, 2, TOPK])
        eq = sb("onehot", [P, 2, TOPK, TOPK])
        e12 = sb("best_keys", [P, 2, TOPK])
        sc_all = sb("gate_raw", [P, SLOTS])
        gate = sb("gates", [P, SLOTS])
        idx = sb("expert_all", [P, ALLT * SLOTS], I32)
        gs = sb("gate_sum", [P, 2, PH])
        stage = [sb(f"idx_stage{k}", [P, RING], I32) for k in range(2)]
        rows = sb("expert_rows", [P, RING, D])
        keys = rows[:, 0:2, :].rearrange("p k d -> p (k d)").rearrange("p (n d) -> p n d", n=16)
        dot16 = sb("dots_here", [P, STEP])
        dots = sb("dots", [P, SLOTS])
        wgt = sb("weights", [P, SLOTS])
        w16 = sb("weights_here", [P, STEP])
        diag = sb("weight_diag", [P, NPE, P])
        zero = sb("p_zero", [P, P])

        names = ("p_consts w_in2 keysT_ps keysT_sb c_in h_in p_in wg_in g_in rms c_ready cT_ps cT_sb q_ps q_sb "
                 "s_ps s_sb idx_ready gate_sub gate_exp dots_ready gelu_done cur_free cur_ready k_in "
                 "passed passed2 staged diag_ready w_ready act_passed pe_passed dve_passed vacc_ps vacc_free gate_rms "
                 "en_ready enT_ps enT_sb pT_sb gate_ps sig_done sum_ready rms2 y_ready y_out").split()
        s = {n: sem(n) for n in names}
        got = [sem(f"row_in{k}") for k in range(RING)]
        used = [sem(f"row_used{k}") for k in range(RING)]

        def turn(i, part, j, half):
            return (i * 2 + part) * (SLOTS // RING) + j * (STEP // RING) + half

        u_tab, v_tab = a["peer_u"][0], a["peer_v"][0]
        block = ctx.enter_context(nc.Block())

        def y_rows(i):
            return out["y_p"][0, bass.ds(i * P, P), :]

        @block.sync
        def _(sp):
            sp.dma_start(keys[:, 0:16:2, :], a["peer_keys1"][0].rearrange("h n d -> n h d")).then_inc(s["k_in"], 16)
            sp.dma_start(keys[:, 1:16:2, :], a["peer_keys2"][0].rearrange("h n d -> n h d")).then_inc(s["k_in"], 16)
            sp.dma_start(g_ffn[:, :], a["norm_ffn"].to_broadcast([P, D])).then_inc(s["k_in"], 16)
            sp.dma_start(c_nxt[:, :], h_rows[0:P, :]).then_inc(s["c_in"], 16)
            for k in range(KD):
                sp.dma_start(wq[:, k, :], a["peer_wq"][0, k * P:(k + 1) * P, :]).then_inc(s["w_in2"], 16)
            sp.dma_start(h_cur[:, :], h_rows[0:P, :]).then_inc(s["h_in"], 16)
            sp.dma_start(ple[:, :], a["p_prompt"][0, 0, 0:P, :]).then_inc(s["p_in"], 16)
            sp.wait_ge(s["cur_ready"], 1)
            sp.dma_start(c_nxt[:, :], h_rows[P:2 * P, :]).then_inc(s["c_in"], 16)
            sp.dma_start(g_fin[:, :], a["norm_final"].rearrange("(o n) -> o n", o=1).to_broadcast([P, D])).then_inc(s["g_in"], 16)
            with nc.allow_non_contiguous_dma(reason="a weight per channel onto the partitions"):
                sp.dma_start(g_ple[:, :], a["norm_ple"][0].rearrange("(k p) -> p k", p=P)).then_inc(s["g_in"], 16)
            for k in range(KD):
                sp.dma_start(wg[:, k, :], a["ple_gate"][0, k * P:(k + 1) * P, :]).then_inc(s["wg_in"], 16)
            sp.dma_start(wi[:, :, :], a["ple_in"][0].rearrange("(k p) n -> p k n", p=P)).then_inc(s["wg_in"], 16)
            sp.wait_ge(s["cur_ready"], 2)
            sp.dma_start(c_nxt[:, :], h_rows[2 * P:3 * P, :]).then_inc(s["c_in"], 16)

            def gate_io(i, y_dst, p_src, r):
                sp.wait_ge(s["pT_sb"], i + 1)
                sp.dma_start(ple[0:r, :], p_src).then_inc(s["p_in"], 16)
                sp.wait_ge(s["sum_ready"], i + 1)
                sp.dma_start(h_cur[:, :], h_rows[bass.ds(i * P + P, P), :]).then_inc(s["h_in"], 16)
                sp.wait_ge(s["y_ready"], i + 1)
                sp.dma_start(y_dst, y).then_inc(s["y_out"], 16)

            with sp.Fori(1, TILES - 1) as i:
                gate_io(i - 1, y_rows(i - 1), a["p_prompt"][0, 0, bass.ds(i * P, P), :], P)
                sp.wait_ge(s["cur_ready"], i + 2)
                sp.dma_start(c_nxt[:, :], h_rows[bass.ds(i * P + 2 * P, P), :]).then_inc(s["c_in"], 16)
            gate_io(TILES - 2, y_rows(TILES - 2), a["p_prompt"][0, 0, SEQ - P:SEQ, :], P)
            gate_io(TILES - 1, y_rows(TILES - 1), a["p_sample"][0].rearrange("b t d -> (b t) d"), NS)
            sp.wait_ge(s["y_ready"], ALLT)
            sp.dma_start(out["y_s"].rearrange("b t d -> (b t) d"), y[0:NS, :]).then_inc(s["y_out"], 16)
            sp.wait_ge(s["y_out"], 16 * ALLT)

        @block.gpsimd
        def _(pool):
            g = nc.gpsimd
            g.memset(eps[:, :], EPS)
            g.memset(zero[:, :], 0.0)
            g.memset(ident[:, :], 0.0)
            g.iota(iota_i[:, :], pattern=[[1, TOPK]], base=0, channel_multiplier=0)
            pool.drain()
            g.affine_select(out=ident[:, :], in_=ident[:, :], compare_op=ALU.not_equal, fill=1.0,
                            base=0, pattern=[[-1, P]], channel_multiplier=1)
            g.tensor_copy(iota16[:, :], iota_i[:, :])
            pool.drain()
            pool.sem_inc(s["p_consts"], 1)
            pool.sem_inc(s["vacc_free"], 1)
            for k in range(RING):
                pool.sem_inc(used[k], 1)

            def gathers(i, part, r, table):
                with pool.Fori(0, SLOTS // STEP) as j:
                    pool.wait_ge(s["idx_ready"], PH * i + j + 1)
                    pool.sem_inc(s["passed"], 1)
                    for half in range(2):
                        g.tensor_copy(stage[half][:, :], idx[:, bass.ds(i * SLOTS + j * STEP + half * RING, RING)]).then_inc(s["staged"], 1)
                        pool.wait_ge(s["staged"], turn(i, part, j, half) + 1)
                        for k in range(RING):
                            pool.wait_ge(used[k], turn(i, part, j, half) + 1)
                            pool.sem_inc(s["passed"], 1)
                            g.indirect_dma_start(rows[0:r, k, :], None, table,
                                                 bass.IndirectOffsetOnAxis(ap=stage[half][0:r, k:k + 1], axis=0)).then_inc(got[k], 16)

            pool.wait_ge(s["keysT_ps"], 1)
            with pool.Fori(0, TILES) as i:
                gathers(i, 0, P, u_tab)
                gathers(i, 1, P, v_tab)
            gathers(TILES, 0, NS, u_tab)
            gathers(TILES, 1, NS, v_tab)

        @block.tensor
        def _(pe):
            t = nc.tensor
            pe.wait_ge(s["p_consts"], 1)
            pe.wait_ge(s["k_in"], 48)
            for n in range(16):
                m = t.transpose(bank[n // 4][:, (n % 4) * P:(n % 4 + 1) * P], keys[:, n, :], ident[:, :])
            m.then_inc(s["keysT_ps"], 1)
            pe.wait_ge(s["keysT_sb"], 1)
            pe.wait_ge(s["w_in2"], 16 * KD)

            def scores(i):
                pe.wait_ge(s["c_ready"], i + 1)
                for k in range(KD):
                    m = t.transpose(bank[6 + k // 4][:, (k % 4) * P:(k % 4 + 1) * P], c_nxt[:, k * P:(k + 1) * P], ident[:, :])
                m.then_inc(s["cT_ps"], 1)
                pe.wait_ge(s["cT_sb"], i + 1)
                for b in range(4):
                    for c in range(4):
                        n = b * 4 + c
                        for k in range(KD):
                            m = t.matmul(bank[4 + b % 2][:, c * P:(c + 1) * P], wq[:, k, n * P:(n + 1) * P], cT[:, k, :],
                                         start=(k == 0), stop=(k == KD - 1))
                    m.then_inc(s["q_ps"], 1)
                    if b == 0:
                        continue
                    pe.wait_ge(s["q_sb"], 4 * i + b)
                pe.wait_ge(s["q_sb"], 4 * i + 4)
                for n in range(16):
                    m = t.matmul(bank[4 + n // 4][:, (n % 4) * P:(n % 4 + 1) * P], qT[:, n, :], keysT[:, n, :], start=True, stop=True)
                m.then_inc(s["s_ps"], 1)

            def accumulate(i, r):
                pe.wait_ge(s["vacc_free"], i + 1)
                for n in range(2):
                    t.matmul(bank[n][0:r, :], zero[0:r, 0:r], g_ffn[0:r, n * 512:(n + 1) * 512], start=True, stop=False)
                with pe.Fori(0, SLOTS // STEP) as j:
                    for n, k in enumerate(ON_PE):
                        pe.wait_ge(s["diag_ready"], (i * (SLOTS // STEP) + j) * NPE + n + 1)
                        pe.wait_ge(got[k % RING], 16 * (turn(i, 1, j, k // RING) + 1))
                        if r < P:
                            pe.sem_inc(s["pe_passed"], 1)
                        for c in range(2):
                            m = t.matmul(bank[c][0:r, :], diag[0:r, n, 0:r], rows[0:r, k % RING, c * 512:(c + 1) * 512],
                                         start=False, stop=False)
                        m.then_inc(used[k % RING], 1)
                for n in range(2):
                    m = t.matmul(bank[n][0:r, :], zero[0:r, 0:r], g_ffn[0:r, n * 512:(n + 1) * 512], start=False, stop=True)
                m.then_inc(s["vacc_ps"], 1)

            def gate_products(i, r):
                pe.wait_ge(s["en_ready"], i + 1)
                pe.wait_ge(s["p_in"], 16 * i + 16)
                if r < P:
                    pe.sem_inc(s["pe_passed"], 1)
                for k in range(KD):
                    t.transpose(bank[4 + k // 4][:, (k % 4) * P:(k % 4) * P + r], en[0:r, k * P:(k + 1) * P], ident[0:r, 0:r])
                for k in range(PB):
                    m = t.transpose(bank[6][:, k * P:k * P + r], ple[0:r, k * P:(k + 1) * P], ident[0:r, 0:r])
                m.then_inc(s["enT_ps"], 1)
                pe.wait_ge(s["enT_sb"], i + 1)
                pe.wait_ge(s["pT_sb"], i + 1)
                pe.wait_ge(s["wg_in"], 16 * (KD + 1))
                for n in range(2):
                    for k in range(KD):
                        t.matmul(bank[n][0:r, :], cT[:, k, 0:r], wg[:, k, n * 512:(n + 1) * 512], start=(k == 0), stop=(k == KD - 1))
                for n in range(2):
                    for k in range(PB):
                        m = t.matmul(bank[2 + n][0:r, :], pleT[:, k, 0:r], wi[:, k, n * 512:(n + 1) * 512], start=(k == 0), stop=(k == PB - 1))
                m.then_inc(s["gate_ps"], 1)

            scores(0)
            scores(1)
            accumulate(0, P)
            with pe.Fori(1, TILES) as i:
                gate_products(i - 1, P)
                scores(i + 1)
                pe.wait_ge(s["sig_done"], i)
                accumulate(i, P)
            gate_products(TILES - 1, P)
            pe.wait_ge(s["sig_done"], TILES)
            accumulate(TILES, NS)
            gate_products(TILES, NS)

        @block.scalar
        def _(act):
            ac = nc.scalar
            act.wait_ge(s["p_consts"], 1)
            act.wait_ge(s["keysT_ps"], 1)
            for b in range(4):
                m = ac.activation(keysT[:, 4 * b:4 * b + 4, :], bank[b][:, :].rearrange("p (c t) -> p c t", c=4), ACT.Copy)
            m.then_inc(s["keysT_sb"], 1)

            def rms(i):
                act.wait_ge(s["c_in"], 16 * i + 16)
                ac.activation(en, c_nxt[:, :], ACT.Square, accum_out=st[:, 0:1])
                act.drain()
                ac.activation(st[:, 1:2], st[:, 0:1], ACT.Sqrt, scale=1.0 / D, bias=eps[:, :]).then_inc(s["rms"], 1)

            def tokens_T(i):
                act.wait_ge(s["cT_ps"], i + 1)
                for b in range(2):
                    m = ac.activation(cT[:, 4 * b:4 * b + 4, :], bank[6 + b][:, :].rearrange("p (c t) -> p c t", c=4), ACT.Copy)
                m.then_inc(s["cT_sb"], 1)

            def scores(i):
                for b in range(4):
                    act.wait_ge(s["q_ps"], 4 * i + b + 1)
                    ac.activation(qT[:, 4 * b:4 * b + 4, :], bank[4 + b % 2][:, :].rearrange("p (c t) -> p c t", c=4), ACT.Copy).then_inc(s["q_sb"], 1)
                act.wait_ge(s["s_ps"], i + 1)
                for b in range(4):
                    m = ac.activation(sco[:, 4 * b:4 * b + 4, :], bank[4 + b][:, :].rearrange("p (c t) -> p c t", c=4), ACT.Copy)
                m.then_inc(s["s_sb"], 1)

            def gate_rms(i, r):
                act.wait_ge(s["cur_free"], i + 1)
                ac.activation(en[0:r, :], h_cur[0:r, :], ACT.Square, accum_out=gst[0:r, 0:1])
                act.drain()
                ac.activation(gst[0:r, 1:2], gst[0:r, 0:1], ACT.Sqrt, scale=1.0 / D, bias=eps[0:r, :]).then_inc(s["gate_rms"], 1)

            def gate_sigmoid(i, r):
                act.wait_ge(s["enT_ps"], i + 1)
                ac.activation(pleT[:, :, 0:r], bank[6][:, 0:PLE].rearrange("p (k t) -> p k t", k=PB)[:, :, 0:r], ACT.Copy).then_inc(s["pT_sb"], 1)
                act.wait_ge(s["gate_ps"], i + 1)
                for n in range(2):
                    m = ac.activation(y[0:r, n * 512:(n + 1) * 512], bank[n][0:r, :], ACT.Sigmoid)
                m.then_inc(s["sig_done"], 1)

            def last_rms(i, r):
                act.wait_ge(s["sum_ready"], i + 1)
                ac.activation(en[0:r, :], y[0:r, :], ACT.Square, accum_out=gst[0:r, 3:4])
                act.drain()
                ac.activation(gst[0:r, 4:5], gst[0:r, 3:4], ACT.Sqrt, scale=1.0 / D, bias=eps[0:r, :]).then_inc(s["rms2"], 1)

            def take_over(i):
                ac.activation(c_cur[:, :], c_nxt[:, :], ACT.Copy).then_inc(s["cur_ready"], 1)

            def gates(i):
                act.wait_ge(s["gate_sub"], i + 1)
                ac.activation(sc_all[:, :], sc_all[:, :], ACT.Exp).then_inc(s["gate_exp"], 1)

            def diagonals(i, r):
                act.wait_ge(s["w_ready"], i + 1)
                act.sem_inc(s["act_passed"], 1)
                with act.Fori(0, SLOTS // STEP) as j:
                    for n, k in enumerate(ON_PE):
                        act.wait_ge(used[k % RING], turn(i, 1, j, k // RING))
                        act.sem_inc(s["act_passed"], 1)
                        ac.activation(diag[0:r, n, 0:r], ident[0:r, 0:r], ACT.Copy,
                                      scale=wgt[0:r, bass.ds(j * STEP + k, 1)]).then_inc(s["diag_ready"], 1)

            def weights(i, r):
                act.wait_ge(s["dots_ready"], i + 1)
                ac.activation(wgt[0:r, :], dots[0:r, :], ACT.Gelu).then_inc(s["gelu_done"], 1)

            rms(0)
            tokens_T(0)
            scores(0)
            take_over(0)
            rms(1)
            gates(0)
            tokens_T(1)
            scores(1)
            weights(0, P)
            take_over(1)
            diagonals(0, P)
            gates(1)
            with act.Fori(1, TILES) as i:
                rms(i + 1)
                gate_rms(i - 1, P)
                gate_sigmoid(i - 1, P)
                tokens_T(i + 1)
                last_rms(i - 1, P)
                act.wait_ge(s["y_out"], 16 * i)
                scores(i + 1)
                weights(i, P)
                take_over(i + 1)
                diagonals(i, P)
                gates(i + 1)
            gate_rms(TILES - 1, P)
            gate_sigmoid(TILES - 1, P)
            last_rms(TILES - 1, P)
            weights(TILES, NS)
            diagonals(TILES, NS)
            gate_rms(TILES, NS)
            act.wait_ge(s["y_out"], 16 * TILES)
            gate_sigmoid(TILES, NS)
            last_rms(TILES, NS)

        @block.vector
        def _(dve):
            v = nc.vector
            dve.wait_ge(s["p_consts"], 1)
            dve.wait_ge(s["k_in"], 48)

            def norm(i):
                dve.wait_ge(s["rms"], i + 1)
                v.reciprocal(st[:, 2:3], st[:, 1:2])
                dve.drain()
                v.scalar_tensor_tensor(c_nxt[:, :], c_nxt[:, :], st[:, 2:3], g_ffn[:, :], ALU.mult, ALU.mult).then_inc(s["c_ready"], 1)

            def best(i, j):
                v.tensor_copy(sst[:, :, :], sco[:, bass.ds(j * 2, 2), :])
                dve.drain()
                for f in range(2):
                    v.max(v1[:, f, 0:8], sst[:, f, :])
                dve.drain()
                for f in range(2):
                    v.max_index(x1[:, f, 0:8], v1[:, f, 0:8], sst[:, f, :])
                    v.match_replace(sst2[:, f, :], v1[:, f, 0:8], sst[:, f, :], LOW)
                dve.drain()
                for f in range(2):
                    v.max(v1[:, f, 8:16], sst2[:, f, :])
                dve.drain()
                for f in range(2):
                    v.max_index(x1[:, f, 8:16], v1[:, f, 8:16], sst2[:, f, :])
                v.tensor_tensor(cand[:, :, :], v1[:, 0, :].rearrange("p (a o) -> p a o", o=1).to_broadcast([P, TOPK, TOPK]),
                                v1[:, 1, :].rearrange("p (o b) -> p o b", o=1).to_broadcast([P, TOPK, TOPK]), ALU.add)
                dve.drain()
                flat = cand[:, :, :].rearrange("p a b -> p (a b)")
                v.tensor_copy(x1f[:, :, :], x1[:, :, :])
                v.max(sc16[:, 0:8], flat)
                dve.drain()
                v.max_index(ci[:, 0:8], sc16[:, 0:8], flat)
                v.match_replace(cand2[:, :], sc16[:, 0:8], flat, LOW)
                dve.drain()
                v.max(sc16[:, 8:16], cand2[:, :])
                dve.drain()
                v.max_index(ci[:, 8:16], sc16[:, 8:16], cand2[:, :])
                dve.drain()
                v.tensor_scalar(cab[:, 0, :], ci[:, :], 4, None, ALU.logical_shift_right)
                v.tensor_scalar(cab[:, 1, :], ci[:, :], 15, None, ALU.bitwise_and)
                dve.drain()
                v.tensor_copy(cabf[:, :, :], cab[:, :, :])
                dve.drain()
                for f in range(2):
                    v.tensor_tensor(eq[:, f], cabf[:, f, :].rearrange("p (k o) -> p k o", o=1).to_broadcast([P, TOPK, TOPK]),
                                    iota16[:, :].rearrange("p (o a) -> p o a", o=1).to_broadcast([P, TOPK, TOPK]), ALU.is_equal)
                dve.drain()
                for f in range(2):
                    v.tensor_tensor(eq[:, f], eq[:, f],
                                    x1f[:, f, :].rearrange("p (o a) -> p o a", o=1).to_broadcast([P, TOPK, TOPK]), ALU.mult)
                dve.drain()
                v.tensor_reduce(e12[:, :, :], eq[:, :, :, :], AXX, ALU.add)
                dve.drain()
                v.scalar_tensor_tensor(idx[:, bass.ds(i * SLOTS + j * TOPK, TOPK)], e12[:, 0, :], float(NK), e12[:, 1, :],
                                       ALU.mult, ALU.add).then_inc(s["idx_ready"], 1)
                v.tensor_scalar(sc_all[:, bass.ds(j * TOPK, TOPK)], sc16[:, :], sc16[:, 0:1], None, ALU.subtract)
                dve.drain()

            def gates(i):
                dve.wait_ge(s["gate_exp"], i + 1)
                by_head = sc_all[:, :].rearrange("p (h k) -> p h k", k=TOPK)
                v.tensor_reduce(gs[:, 0, :], by_head, AXX, ALU.add)
                dve.drain()
                v.reciprocal(gs[:, 1, :], gs[:, 0, :])
                dve.drain()
                v.tensor_tensor(gate[:, :].rearrange("p (h k) -> p h k", k=TOPK), by_head,
                                gs[:, 1, :].rearrange("p (h o) -> p h o", o=1).to_broadcast([P, PH, TOPK]), ALU.mult)
                dve.drain()

            norm(0)
            dve.wait_ge(s["s_sb"], 1)
            best(0, 0)

            def dots_of(i, r, j):
                for k in range(STEP):
                    dve.wait_ge(got[k % RING], 16 * (turn(i, 0, j, k // RING) + 1))
                    v.tensor_tensor_reduce(out=rows[0:r, k % RING, :], in0=rows[0:r, k % RING, :], in1=c_cur[0:r, :], scale=1.0,
                                           scalar=0.0, op0=ALU.mult, op1=ALU.add,
                                           accum_out=dot16[0:r, k:k + 1]).then_inc(used[k % RING], 1)
                dve.drain()
                v.tensor_copy(dots[0:r, bass.ds(j * STEP, STEP)], dot16[0:r, :])
                dve.drain()

            def dot_products(i, r, steps):
                with dve.Fori(*steps) as j:
                    dots_of(i, r, j)

            def gate_norm(i, r):
                dve.wait_ge(s["gate_rms"], i + 1)
                v.reciprocal(gst[0:r, 2:3], gst[0:r, 1:2])
                dve.drain()
                v.tensor_scalar(en[0:r, :], h_cur[0:r, :], gst[0:r, 2:3], None, ALU.mult).then_inc(s["en_ready"], 1)

            def gate_T(i, r):
                dve.wait_ge(s["enT_ps"], i + 1)
                for b in range(2):
                    m = v.tensor_tensor(cT[:, 4 * b:4 * b + 4, 0:r], bank[4 + b][:, :].rearrange("p (k t) -> p k t", k=4)[:, :, 0:r],
                                        g_ple[:, 4 * b:4 * b + 4].rearrange("p (k o) -> p k o", o=1).to_broadcast([P, 4, r]), ALU.mult)
                m.then_inc(s["enT_sb"], 1)

            def gate_sum(i, r):
                dve.wait_ge(s["sig_done"], i + 1)
                for n in range(2):
                    v.tensor_tensor(y[0:r, n * 512:(n + 1) * 512], y[0:r, n * 512:(n + 1) * 512], bank[2 + n][0:r, :], ALU.mult)
                dve.drain()
                v.tensor_tensor(y[0:r, :], y[0:r, :], h_cur[0:r, :], ALU.add).then_inc(s["sum_ready"], 1)

            def last_norm(i, r):
                dve.wait_ge(s["rms2"], i + 1)
                v.reciprocal(gst[0:r, 5:6], gst[0:r, 4:5])
                dve.drain()
                v.scalar_tensor_tensor(y[0:r, :], y[0:r, :], gst[0:r, 5:6], g_fin[0:r, :], ALU.mult, ALU.mult).then_inc(s["y_ready"], 1)

            def tile(i, r, first, last):
                dve.wait_ge(s["cur_ready"], i + 1)
                dve.sem_inc(s["dve_passed"], 1)
                if first:
                    with dve.Fori(1, PH) as j:
                        best(0, j)
                        dots_of(i, r, j - 1)
                    dve.sem_inc(s["gate_sub"], 1)
                    norm(i + 1)
                    dot_products(i, r, (PH - 1, PH))
                    gates(i)
                else:
                    dot_products(i, r, (0, 1))
                    gates(i)
                    gate_norm(i - 1, P)
                    dot_products(i, r, (1, 2))
                    gate_T(i - 1, P)
                    if not last:
                        norm(i + 1)
                    dot_products(i, r, (2, 4))
                    gate_sum(i - 1, P)
                    dot_products(i, r, (4, 5))
                    last_norm(i - 1, P)
                    dot_products(i, r, (5, SLOTS // STEP))
                dve.sem_inc(s["dots_ready"], 1)
                dve.wait_ge(s["gelu_done"], i + 1)
                v.tensor_tensor(wgt[0:r, :], wgt[0:r, :], gate[0:r, :], ALU.mult).then_inc(s["w_ready"], 1)
                dve.drain()
                if not last:
                    dve.wait_ge(s["s_sb"], i + 2)
                    dve.sem_inc(s["passed2"], 1)
                dve.wait_ge(s["h_in"], 16 * i + 16)
                dve.sem_inc(s["dve_passed"], 1)
                with dve.Fori(0, SLOTS // STEP) as j:
                    v.tensor_copy(w16[0:r, :], wgt[0:r, bass.ds(j * STEP, STEP)])
                    if not last:
                        best(i + 1, j)
                    else:
                        dve.drain()
                    for k in range(STEP):
                        if k in ON_PE:
                            continue
                        dve.wait_ge(got[k % RING], 16 * (turn(i, 1, j, k // RING) + 1))
                        v.scalar_tensor_tensor(h_cur[0:r, :], rows[0:r, k % RING, :], w16[0:r, k:k + 1], h_cur[0:r, :],
                                               ALU.mult, ALU.add).then_inc(used[k % RING], 1)
                        dve.drain()
                if not last:
                    dve.sem_inc(s["gate_sub"], 1)
                dve.wait_ge(s["vacc_ps"], i + 1)
                for n in range(2):
                    m = v.tensor_tensor(h_cur[0:r, n * 512:(n + 1) * 512], h_cur[0:r, n * 512:(n + 1) * 512], bank[n][0:r, :], ALU.add)
                m.then_inc(s["vacc_free"], 1)
                dve.drain()
                dve.sem_inc(s["cur_free"], 1)

            tile(0, P, True, False)
            dve.wait_ge(s["g_in"], 32)
            with dve.Fori(1, TILES) as i:
                tile(i, P, False, False)
            tile(TILES, NS, False, True)
            gate_norm(TILES, NS)
            gate_T(TILES, NS)
            gate_sum(TILES, NS)
            last_norm(TILES, NS)


def program(nc, a, out):
    h_rows = nc.dram_tensor("h_after_mixer", [ALLT * P, D], F32).ap()
    with ExitStack() as sems:
        mixer_block(nc, sems, a, out, h_rows)
        peer_block(nc, sems, a, out, h_rows)


_INS = ['x_prompt', 'x_sample', 'p_prompt', 'p_sample', 'cache_swa_k', 'cache_swa_v', 'state_conv', 'state_delta',
        'norm_mix', 'w_in', 'conv_w', 'attn_sinks', 'dn_a_log', 'dn_dt_bias', 'dn_norm', 'w_out', 'norm_ffn',
        'peer_wq', 'peer_keys1', 'peer_keys2', 'peer_u', 'peer_v', 'norm_ple', 'ple_in', 'ple_gate', 'norm_final']
_OUTS = [('y_p', (1, SEQ, D)), ('y_s', (DB, DS, D)), ('k_p', (1, 1, WIN, KVH, HD)), ('v_p', (1, 1, WIN, KVH, HD)),
         ('c_p', (1, 1, TAPS - 1, DQKV)), ('s_p', (1, 1, DH, HD, HD)), ('k_s', (1, DB, WIN, KVH, HD)),
         ('v_s', (1, DB, WIN, KVH, HD)), ('c_s', (1, DB, TAPS - 1, DQKV)), ('s_s', (1, DB, DH, HD, HD))]


def kernel(**inputs):
    import numpy as _np
    import concourse.bacc as _bacc
    from concourse.bass_utils import run_bass_kernel_spmd as _run

    nc = _bacc.Bacc("TRN2", target_bir_lowering=False, num_devices=1)
    arrays, a, out = {}, {}, {}
    for name in _INS:
        arrays[f"in_{name}_dram"] = _np.ascontiguousarray(inputs[name])
        a[name] = nc.dram_tensor(f"in_{name}_dram", arrays[f"in_{name}_dram"].shape, F32, kind="ExternalInput").ap()
    i, j = _np.arange(GRP * DS)[:, None] % DS, _np.arange(SKEYS)[None]
    far = (WIN + i - j < 0) | (WIN + i - j > WIN)
    consts = {"c_dist": _np.where(far, FAR, WIN + i - j).astype(_np.float32),
              "c_slope": _np.array([[SLOPE[g * GRP + n // DS] for g in range(KVH)] for n in range(GRP * DS)], _np.float32)}
    for name, value in consts.items():
        arrays[f"in_{name}_dram"] = value
        a[name] = nc.dram_tensor(f"in_{name}_dram", value.shape, F32, kind="ExternalInput").ap()
    for name, shape in _OUTS:
        out[name] = nc.dram_tensor(f"out_{name}_dram", shape, F32, kind="ExternalOutput").ap()
    program(nc, a, out)
    r = _run(nc, [arrays], core_ids=[0])
    return tuple(r.results[0][f"out_{name}_dram"] for name, _ in _OUTS)
```

```python
import concourse.bass as bass
from concourse import mybir
from contextlib import ExitStack

F32 = mybir.dt.float32
I32 = mybir.dt.int32
U32 = mybir.dt.uint32
ALU = mybir.AluOpType
ACT = mybir.ActivationFunctionType
AXX = mybir.AxisListType.X

P = 128
D = 1024
KD = D // P
SEQ = 1024
TILES = SEQ // P
DB, DS = 8, 8
NS = DB * DS
ALLT = TILES + 1
HD = 64
AH, KVH, GRP = 8, 2, 4
WIN = 128
DH = 8
PAIRS = DH // 2
DQKV = 3 * DH * HD
CB = DQKV // P
TAPS = 4
C_K, C_V, C_DN = 512, 640, 768
C_Z = C_DN + DQKV
C_AB = C_Z + DH * HD
INW = C_AB + 2 * DH
NK = 128
NEXP = NK * NK
PH, TOPK = 8, 16
SLOTS = PH * TOPK
PLE = 256
EPS = 1e-6
FAR = 1e32
LOW = -3e38
LEVELS = (1, 2, 4, 8, 16, 32, 64)
SKEYS = WIN + DS
SLOPE = [-(2.0 ** (-8.0 * (h + 1) / AH)) for h in range(AH)]


def mixer_block(nc, sems, a, out, h_rows):
    with ExitStack() as ctx:
        def sb(name, shape, dt=F32):
            return ctx.enter_context(nc.sbuf_tensor(name, shape, dt))

        def sem(name):
            return sems.enter_context(nc.semaphore("mixer_" + name))

        bank = [ctx.enter_context(nc.psum_tensor(f"mbank{b}", [P, 512], F32)) for b in range(8)]

        w_in = sb("w_in_sb", [P, KD, INW])
        w_flat = w_in[:, :, :].rearrange("p k n -> p (k n)")
        w_out = sb("w_out_sb", [P, KD, D])
        ident = sb("m_ident", [P, P])
        tri = sb("m_tri", [P, P])
        tri8 = sb("m_tri8", [P, NS])
        level = sb("m_level", [P, len(LEVELS), P])
        ones = sb("m_ones", [P, P])
        same8 = sb("m_same8", [P, NS])
        seq_of = sb("m_seq_of", [P, DB])
        pair_diag = sb("m_pair_diag", [P, P])
        g_mix = sb("g_mix_sb", [P, KD])
        cw = sb("conv_w_sb", [P, TAPS, CB])
        sinks = sb("sinks_sb", [P, AH])
        neg_a = sb("neg_a_sb", [P, DH])
        dtb = sb("dtb_sb", [P, DH])
        dnn = sb("dn_norm_sb", [P, HD])
        dist = sb("att_dist", [P, 2 * WIN])
        dist_old = sb("att_dist_old", [P, WIN])
        dist_s = sb("att_dist_s", [GRP * DS, SKEYS])
        slope_s = sb("att_slope_s", [GRP * DS, KVH])
        eps = sb("m_eps", [P, 1])
        one = sb("m_one", [P, 1])

        xh = sb("x_and_h", [P, D])
        x = xn = h = xh
        st = sb("m_stats", [P, 4])
        aT = sb("aT_sb", [P, KD, P])
        attT = sb("att_T", [P, 4, P])
        cin = sb("cin_sb", [P, CB, TAPS - 1 + P])
        cacc = sb("cacc_sb", [P, CB, P])
        cs = sb("cs_sb", [P, CB, P])
        qT = sb("qT_sb", [P, GRP, P])
        kT = sb("kT_sb", [P, 2 * P])
        kv = sb("kv_sb", [P, 2, P])
        v_old = sb("v_old_sb", [P, P])
        zs = sb("zs_sb", [P, 512])
        ab_raw = sb("ab_raw_sb", [P, 2 * DH])
        sc = sb("att_sc", [P, AH, 2 * WIN])
        am = sb("att_m", [P, 6, AH])
        pT = sb("att_pT", [P, AH, 2, P])
        gt = sb("gate_small", [P, 12, DH])
        rn = sb("m_rn", [P, 3, 16])
        rows = sb("dn_rows", [P, 6, 512])
        vb = sb("dn_vb", [P, 512])
        rT = sb("dn_rT", [P, 5, 4, P])
        s2 = sb("dn_s2", [P, PAIRS, P])
        eg = sb("dn_eg", [P, PAIRS])
        qT_s = qT[:, :, :].rearrange("p c t -> p (c t)")[:, 0:DB * GRP * DS].rearrange("p (b h t) -> p b h t", b=DB, h=GRP)
        x_res = rT[:, 0:2, :, :].rearrange("p a c t -> p (a c t)")
        dt_ = cacc[:, 0:DH, :]
        cs_flat = cs[:, :, :].rearrange("p c t -> p (c t)")
        crow = cs_flat
        sq = cs_flat[:, 0:1024]
        y0, y1, ty = (cs_flat[:, n * 512:(n + 1) * 512] for n in range(3))
        rows_flat = rows[:, :, :].rearrange("p c t -> p (c t)")
        lt = rows_flat[:, 0:1024].rearrange("p (h t) -> p h t", h=DH)
        qk = rows_flat[:, 1024:2048].rearrange("p (h t) -> p h t", h=DH)
        vn = rows[:, 4, :]
        stconv = rows_flat[0:24, 0:DQKV]
        pT_flat = pT[:, :, :, :].rearrange("p h c t -> p (h c t)")
        bt = pT_flat[:, 0:1024].rearrange("p (h t) -> p h t", h=DH)
        t1 = pT_flat[:, 1024:2048].rearrange("p (h t) -> p h t", h=DH)
        xx = sc[:, :, :].rearrange("p h (c t) -> p h c t", c=2)
        sc_flat = sc[:, :, :].rearrange("p h t -> p (h t)")
        dn = sc_flat[:, 0:512]
        dnT = xh[:, 512:1024].rearrange("p (c t) -> p c t", c=4)
        s2n = vb[:, :].rearrange("p (c t) -> p c t", c=PAIRS)
        stage3 = cin[:, :, :].rearrange("p c t -> p (c t)")[:, 0:DQKV]

        at = [0]

        def over(n):
            at[0] += n
            assert at[0] <= KD * INW
            return w_flat[:, at[0] - n:at[0]]

        s2s = over(DB * PAIRS * P).rearrange("p (b c v) -> p b c v", b=DB, c=PAIRS)
        kgm = over(DB * PAIRS * NS).rearrange("p (b c t) -> p b c t", b=DB, c=PAIRS)
        qgm = over(DB * PAIRS * NS).rearrange("p (b c t) -> p b c t", b=DB, c=PAIRS)
        ktm = over(2 * 512).rearrange("p (r n) -> p r n", r=2)
        kc = over(DB * P).rearrange("p (b n) -> p b n", b=DB)
        vc = over(DB * P).rearrange("p (b n) -> p b n", b=DB)
        kcT = over(DB * P).rearrange("p (b n) -> p b n", b=DB)
        vnew = over(DB * P).rearrange("p (b n) -> p b n", b=DB)
        ssc = over(2 * DB * SKEYS).rearrange("p (b k) -> p b k", k=SKEYS)
        sm = over(6 * 2 * DB).rearrange("p (r n) -> p r n", r=6)
        spT = over(512).rearrange("p (b r) -> p b r", b=2 * DB)
        spTn = over(512).rearrange("p (b r) -> p b r", b=2 * DB)
        egb = over(DB * PAIRS).rearrange("p (b c) -> p b c", b=DB)
        gmb = over(DB * DH).rearrange("p (b c) -> p b c", b=DB)
        sink_s = sb("sink_s", [P, 2])

        names = ("const_in w_dn_in w_in_in w_out_in misc_in consts x_in rms xn_ready xT_ps aT_ready dqkv_ps "
                 "cin_ready kv_ps kv_sb q_ps q_sb z_ps z_sb silu_done conv_done rows_ps sq_done ssq_done rn_sqrt "
                 "soft_in soft_out gate_ready gsum_ps e_in exp_ready drow_ready rT_ps rT_a rT_v gram_ps "
                 "kgs_ps y0_ready b_ready t_ps t_sb zz_ps xx_ready y1_ps y1_sb ty_ps ty_sb yz_ps vn_ready "
                 "o_ps upd_ps osq_done ossq orms dn_ready dnT_ps dnT_sb score_ps sc_ready nm_ready "
                 "prob_done probs_ready pT_ps pT_sb att_ps att_sb proj_ps h_ready h_out sp_passed "
                 "state_out stc_in stc_ps stc_sb cache_in state_in vnew_in kcT_ps kcT_sb over_clear "
                 "ktm_ready supd_ps supd_done conv_ps conv_sb crow_out out_done mm_masked sexp sprobs "
                 "xres_in").split()
        s = {n: sem(n) for n in names}
        block = ctx.enter_context(nc.Block())

        @block.sync
        def _(sp):
            sp.dma_start(x[:, :], a["x_prompt"][0, 0:P, :]).then_inc(s["x_in"], 16)
            wv = a["w_in"][0].rearrange("(k p) n -> p k n", p=P)
            for k in range(KD):
                sp.dma_start(w_in[:, k, C_DN:C_Z], wv[:, k, C_DN:C_Z]).then_inc(s["w_dn_in"], 16)
            sp.dma_start(w_in[:, :, C_Z:INW], wv[:, :, C_Z:INW]).then_inc(s["w_in_in"], 16)
            for b in range(GRP):
                for g in range(KVH):
                    c = (g * GRP + b) * HD
                    sp.dma_start(w_in[:, :, b * P + g * HD:b * P + (g + 1) * HD],
                                 wv[:, :, c:c + HD]).then_inc(s["w_in_in"], 16)
            sp.dma_start(w_in[:, :, C_K:C_DN], wv[:, :, C_K:C_DN]).then_inc(s["w_in_in"], 16)
            wo = a["w_out"][0]
            for b in range(GRP):
                for g in range(KVH):
                    r = (g * GRP + b) * HD
                    sp.dma_start(w_out[g * HD:(g + 1) * HD, b, :], wo[r:r + HD, :]).then_inc(s["w_out_in"], 16)
            sp.dma_start(w_out[:, 4:8, :], wo[512:1024, :].rearrange("(k p) n -> p k n", p=P)).then_inc(s["w_out_in"], 16)

            def tile(i):
                sp.wait_ge(s["gram_ps"], i + 1)
                sp.sem_inc(s["sp_passed"], 1)
                sp.dma_start(x_res[:, :], a["x_prompt"][0, bass.ds(i * P, P), :]).then_inc(s["xres_in"], 16)

            def store(i):
                sp.wait_ge(s["h_ready"], i + 1)
                sp.sem_inc(s["sp_passed"], 1)
                sp.dma_start(h_rows[bass.ds(i * P, P), :], h[:, :]).then_inc(s["h_out"], 16)

            def next_x(i):
                sp.dma_start(x[:, :], a["x_prompt"][0, bass.ds(i * P + P, P), :]).then_inc(s["x_in"], 16)

            sp.wait_ge(s["xT_ps"], 1)
            next_x(0)
            tile(0)
            with sp.Fori(1, TILES - 1) as i:
                store(i - 1)
                sp.wait_ge(s["h_out"], 16 * i)
                sp.sem_inc(s["sp_passed"], 1)
                next_x(i)
                tile(i)
            store(TILES - 2)
            tile(TILES - 1)
            store(TILES - 1)
            sp.wait_ge(s["h_ready"], TILES)
            sp.wait_ge(s["h_out"], 16 * TILES)
            sp.dma_start(out["k_p"][0, 0].rearrange("t g d -> t (g d)"), kv[:, 0, :]).then_inc(s["state_out"], 16)
            sp.dma_start(out["v_p"][0, 0].rearrange("t g d -> t (g d)"), kv[:, 1, :]).then_inc(s["state_out"], 16)
            for hh in range(DH):
                q, c = divmod(hh, 2)
                sp.dma_start(out["s_p"][0, 0, hh], s2[c * HD:(c + 1) * HD, q, c * HD:(c + 1) * HD]).then_inc(s["state_out"], 16)
            sp.dma_start(x[0:NS, :], a["x_sample"].rearrange("b t d -> (b t) d")).then_inc(s["x_in"], 16)
            sp.dma_start(stconv[:, :], a["state_conv"][0].rearrange("b t c -> (b t) c")).then_inc(s["stc_in"], 16)
            sp.wait_ge(s["conv_sb"], 2)
            for b in range(DB):
                sp.dma_start(out["c_s"][0, b], crow[b * DS + DS - 3:(b + 1) * DS, :]).then_inc(s["crow_out"], 16)
            sp.wait_ge(s["over_clear"], 1)
            for c in range(2):
                for b in range(DB):
                    sp.dma_start(s2s[c * HD:(c + 1) * HD, b, :, c * HD:(c + 1) * HD],
                                 a["state_delta"][0, b, c:DH:2].rearrange("h k v -> k h v")).then_inc(s["state_in"], 16)
            sp.dma_start(kc[:, :, :], a["cache_swa_k"][0].rearrange("b t g d -> t b (g d)")).then_inc(s["cache_in"], 16)
            sp.dma_start(vc[:, :, :], a["cache_swa_v"][0].rearrange("b t g d -> t b (g d)")).then_inc(s["cache_in"], 16)
            for src, dst in (("cache_swa_k", "k_s"), ("cache_swa_v", "v_s")):
                sp.dma_start(out[dst][0][:, 0:WIN - DS], a[src][0][:, DS:WIN]).then_inc(s["out_done"], 16)
            sp.wait_ge(s["kv_sb"], TILES + 1)
            for b in range(DB):
                sp.dma_start(vnew[0:DS, b, :], kv[b * DS:(b + 1) * DS, 1, :]).then_inc(s["vnew_in"], 16)
                sp.dma_start(out["k_s"][0, b, WIN - DS:WIN].rearrange("t g d -> t (g d)"),
                             kv[b * DS:(b + 1) * DS, 0, :]).then_inc(s["out_done"], 16)
                sp.dma_start(out["v_s"][0, b, WIN - DS:WIN].rearrange("t g d -> t (g d)"),
                             kv[b * DS:(b + 1) * DS, 1, :]).then_inc(s["out_done"], 16)
            sp.wait_ge(s["gram_ps"], TILES + 1)
            sp.dma_start(x_res[0:NS, :], a["x_sample"].rearrange("b t d -> (b t) d")).then_inc(s["xres_in"], 16)
            sp.wait_ge(s["supd_done"], DB)
            for b in range(DB):
                for hh in range(DH):
                    q, c = divmod(hh, 2)
                    sp.dma_start(out["s_s"][0, b, hh], s2s[c * HD:(c + 1) * HD, b, q, c * HD:(c + 1) * HD]).then_inc(s["out_done"], 16)
            sp.wait_ge(s["h_ready"], TILES + 1)
            for n in range(P // NS):
                sp.dma_start(h_rows[SEQ + n * NS:SEQ + (n + 1) * NS, :], h[0:NS, :]).then_inc(s["h_out"], 16)
            sp.wait_ge(s["h_out"], 16 * (TILES + P // NS))
            sp.wait_ge(s["state_out"], 16 * (2 + DH))
            sp.wait_ge(s["out_done"], 16 * (2 + 2 * DB + DB * DH))
            sp.wait_ge(s["crow_out"], 16 * DB)

        @block.gpsimd
        def _(pool):
            g = nc.gpsimd
            g.memset(eps[:, :], EPS)
            g.memset(one[:, :], 1.0)
            g.memset(ident[:, :], 0.0)
            g.memset(cin[:, :, 0:TAPS - 1], 0.0)
            g.memset(kT[:, :], 0.0)
            g.memset(v_old[:, :], 0.0)
            pool.drain()
            g.affine_select(out=ident[:, :], in_=ident[:, :], compare_op=ALU.not_equal, fill=1.0,
                            base=0, pattern=[[-1, P]], channel_multiplier=1)
            pool.drain()
            pool.sem_inc(s["consts"], 1)
            g.memset(s2[:, :, :], 0.0)
            g.memset(ones[:, :], 1.0)
            g.memset(tri[:, :], 1.0)
            g.memset(pair_diag[:, :], 1.0)
            g.memset(seq_of[:, :], 1.0)
            g.memset(same8[:, :], 1.0)
            g.memset(level[:, :, :], 1.0)
            pool.drain()
            g.affine_select(out=tri[:, :], in_=tri[:, :], compare_op=ALU.is_ge, fill=0.0,
                            base=0, pattern=[[1, P]], channel_multiplier=-1)
            g.affine_select(out=pair_diag[:, 0:HD], in_=pair_diag[:, 0:HD], compare_op=ALU.is_gt, fill=0.0,
                            base=HD, pattern=[[0, HD]], channel_multiplier=-1)
            g.affine_select(out=pair_diag[:, HD:P], in_=pair_diag[:, HD:P], compare_op=ALU.is_ge, fill=0.0,
                            base=-HD, pattern=[[0, HD]], channel_multiplier=1)
            for n, w in enumerate(LEVELS):
                v = level[:, n, :].rearrange("p (a c) -> p a c", c=2 * w)
                g.affine_select(out=v, in_=v, compare_op=ALU.is_ge, fill=0.0, base=0,
                                pattern=[[-2 * w, P // (2 * w)], [0, 2 * w]], channel_multiplier=1)
            sv = same8[:, :].rearrange("p (b t) -> p b t", t=DS)
            g.affine_select(out=sv, in_=sv, compare_op=ALU.is_ge, fill=0.0, base=0,
                            pattern=[[-DS, DB], [0, DS]], channel_multiplier=1)
            g.affine_select(out=seq_of[:, :], in_=seq_of[:, :], compare_op=ALU.is_ge, fill=0.0, base=0,
                            pattern=[[-DS, DB]], channel_multiplier=1)
            pool.drain()
            for n, w in enumerate(LEVELS):
                v = level[:, n, :].rearrange("p (a c) -> p a c", c=2 * w)
                g.affine_select(out=v, in_=v, compare_op=ALU.is_gt, fill=0.0, base=w,
                                pattern=[[2 * w, P // (2 * w)], [0, 2 * w]], channel_multiplier=-1)
            g.affine_select(out=sv, in_=sv, compare_op=ALU.is_gt, fill=0.0, base=DS,
                            pattern=[[DS, DB], [0, DS]], channel_multiplier=-1)
            g.affine_select(out=seq_of[:, :], in_=seq_of[:, :], compare_op=ALU.is_gt, fill=0.0, base=DS,
                            pattern=[[DS, DB]], channel_multiplier=-1)
            pool.drain()
            for n, w in enumerate(LEVELS):
                v = level[:, n, :].rearrange("p (a c) -> p a c", c=2 * w)
                g.affine_select(out=v, in_=v, compare_op=ALU.is_ge, fill=0.0, base=-w,
                                pattern=[[0, P // (2 * w)], [1, 2 * w]], channel_multiplier=0)
            g.tensor_tensor(tri8[:, :], tri[:, 0:NS], same8[:, :], ALU.mult)
            d_int = vb[:, 0:2 * WIN].bitcast(I32)
            g.iota(d_int, pattern=[[-1, 2 * WIN]], base=WIN, channel_multiplier=1)
            pool.drain()
            g.tensor_copy(dist[:, :], d_int)
            pool.drain()
            g.affine_select(out=dist[:, :], in_=dist[:, :], compare_op=ALU.is_ge, fill=FAR,
                            base=WIN, pattern=[[-1, 2 * WIN]], channel_multiplier=1)
            pool.drain()
            g.affine_select(out=dist[:, :], in_=dist[:, :], compare_op=ALU.is_ge, fill=FAR,
                            base=0, pattern=[[1, 2 * WIN]], channel_multiplier=-1)
            pool.drain()
            g.tensor_copy(dist_old[:, :], dist[:, 0:WIN])
            pool.drain()
            g.memset(dist[:, 0:WIN], FAR)
            pool.drain()
            pool.sem_inc(s["consts"], 1)
            pool.wait_ge(s["z_ps"], TILES + 1)
            g.memset(s2s[:, :, :, :], 0.0)
            g.memset(kgm[:, :, :, :], 0.0)
            g.memset(qgm[:, :, :, :], 0.0)
            pool.drain()
            pool.sem_inc(s["over_clear"], 1)

        @block.tensor
        def _(pe):
            t = nc.tensor
            pe.wait_ge(s["consts"], 1)

            def x_T(i, r):
                pe.wait_ge(s["xn_ready"], i + 1)
                for k in range(KD):
                    m = t.transpose(bank[6 + k // 4][:, (k % 4) * P:(k % 4) * P + r], xn[0:r, k * P:(k + 1) * P], ident[0:r, 0:r])
                m.then_inc(s["xT_ps"], 1)

            def dqkv(i, r, blocks):
                for n in blocks:
                    b, c = divmod(n, 4)
                    if n == 0:
                        pe.wait_ge(s["aT_ready"], i + 1)
                    if n == 8:
                        pe.wait_ge(s["cin_ready"], 3 * i + 1)
                    w = C_DN + n * P
                    for k in range(KD):
                        m = t.matmul(bank[6 + b % 2][:, c * P:c * P + r], w_in[:, k, w:w + P], aT[:, k, 0:r],
                                     start=(k == 0), stop=(k == KD - 1))
                    if c == 3:
                        m.then_inc(s["dqkv_ps"], 1)

            def queries(i, r, blocks):
                for c in blocks:
                    for k in range(KD):
                        m = t.matmul(bank[2][:, c * P:c * P + r], w_in[:, k, c * P:(c + 1) * P], aT[:, k, 0:r],
                                     start=(k == 0), stop=(k == KD - 1))
                    if c == GRP - 1:
                        m.then_inc(s["q_ps"], 1)

            def keys_values(i, r):
                for k in range(KD):
                    t.matmul(bank[3][0:r, 384:400], aT[:, k, 0:r], w_in[:, k, C_AB:INW],
                             start=(k == 0), stop=(k == KD - 1))
                for k in range(KD):
                    t.matmul(bank[3][0:r, 0:256], aT[:, k, 0:r], w_in[:, k, C_K:C_DN],
                             start=(k == 0), stop=(k == KD - 1))
                for k in range(KD):
                    m = t.matmul(bank[3][:, 256:256 + r], w_in[:, k, C_K:C_K + P], aT[:, k, 0:r],
                                 start=(k == 0), stop=(k == KD - 1))
                m.then_inc(s["kv_ps"], 1)

            def z_rows(i, r):
                pe.wait_ge(s["cin_ready"], 3 * i + 2)
                for k in range(KD):
                    m = t.matmul(bank[7][0:r, :], aT[:, k, 0:r], w_in[:, k, C_Z:C_AB],
                                 start=(k == 0), stop=(k == KD - 1))
                m.then_inc(s["z_ps"], 1)

            def front(i):
                x_T(i, P)
                pe.wait_ge(s["w_dn_in"], 16 * KD)
                dqkv(i, P, range(CB))
                pe.wait_ge(s["w_in_in"], 16 * (1 + 2 * GRP + 1))
                queries(i, P, range(GRP))
                keys_values(i, P)
                z_rows(i, P)

            def front_sampled(i, r):
                x_T(i, r)
                pe.wait_ge(s["aT_ready"], i + 1)
                pe.wait_ge(s["conv_sb"], 1)
                for n, b in enumerate((0, 1, 4)):
                    for k in range(KD):
                        m = t.matmul(bank[b][0:r, :], aT[:, k, 0:r], w_in[:, k, C_DN + n * 512:C_DN + (n + 1) * 512],
                                     start=(k == 0), stop=(k == KD - 1))
                    m.then_inc(s["conv_ps"], 1)
                queries(i, r, range(GRP))
                keys_values(i, r)
                pe.wait_ge(s["conv_sb"], 2)
                for c in range(CB):
                    if c == 8:
                        pe.wait_ge(s["cin_ready"], 3 * i + 1)
                    m = t.transpose(bank[6 + c // 4 % 2][:, (c % 4) * P:(c % 4) * P + r], crow[0:r, c * P:(c + 1) * P], ident[0:r, 0:r])
                    if c % 4 == 3:
                        m.then_inc(s["dqkv_ps"], 1)
                z_rows(i, r)

            def out_products(i, r):
                pe.wait_ge(s["dnT_sb"], i + 1)
                for n in range(2):
                    for k in range(KD):
                        m = t.matmul(bank[2 + n][0:r, :], (attT if k < 4 else dnT)[:, k % 4, 0:r], w_out[:, k, n * 512:(n + 1) * 512],
                                     start=(k == 0), stop=(k == KD - 1))
                    m.then_inc(s["proj_ps"], 1)

            def tile(i, r, sampled, ahead, before):
                pe.wait_ge(s["q_sb"], i + 1)
                pe.wait_ge(s["kv_sb"], i + 1)
                if not sampled:
                    for hh in range(AH):
                        g, p = divmod(hh, GRP)
                        m = t.matmul(bank[hh // 2][:, (hh % 2) * 256:(hh % 2) * 256 + 256],
                                     qT[g * HD:(g + 1) * HD, p, :], kT[g * HD:(g + 1) * HD, :], start=True, stop=True)
                    m.then_inc(s["score_ps"], 1)
                else:
                    pe.wait_ge(s["stc_in"], 16)
                    for c in range(CB):
                        m = t.transpose(bank[3][:, c * 24:(c + 1) * 24], stconv[:, c * P:(c + 1) * P], ident[0:24, 0:24])
                    m.then_inc(s["stc_ps"], 1)
                pe.wait_ge(s["silu_done"], i + 1)
                if before:
                    pe.wait_ge(s["dnT_sb"], i)
                for c in range(CB):
                    m = t.transpose(bank[4 + c // 4][0:r, (c % 4) * P:(c % 4 + 1) * P], cs[:, c, 0:r], ident[:, :])
                m.then_inc(s["rows_ps"], 1)
                pe.wait_ge(s["gate_ready"], i + 1)
                pe.wait_ge(s["z_sb"], i + 1)
                cum = tri8 if sampled else tri
                same = same8 if sampled else ones
                t.matmul(bank[7][0:r, 0:DH], cum[0:r, 0:r], gt[0:r, 5, :], start=True, stop=True)
                t.matmul(bank[7][0:r, DH:2 * DH], same[0:r, 0:r], gt[0:r, 5, :], start=True, stop=True)
                if sampled:
                    pe.wait_ge(s["mm_masked"], 1)
                    m = t.matmul(bank[7][:, 64:128], ones[0:r, :], gmb[0:r, :, :], start=True, stop=True)
                else:
                    m = t.matmul(bank[7][:, 64:64 + DH], ones[0:r, :], gt[0:r, 5, :], start=True, stop=True)
                    pe.wait_ge(s["sc_ready"], i + 1)
                for hh in range(DH):
                    m = t.matmul(bank[hh // 4][0:r, (hh % 4) * P:(hh % 4) * P + r],
                                 gt[0:r, 5, hh:hh + 1].to_broadcast([r, r]), cum[0:r, 0:r], start=True, stop=True)
                m.then_inc(s["gsum_ps"], 1)
                if before:
                    out_products(i - 1, P)
                    pe.wait_ge(s["h_ready"], i)
                if not sampled:
                    pe.wait_ge(s["probs_ready"], i + 1)
                    pe.wait_ge(s["e_in"], i + 1)
                    for hh in range(AH):
                        for b in range(2):
                            m = t.transpose(bank[hh // 2][:, ((hh % 2) * 2 + b) * P:((hh % 2) * 2 + b + 1) * P],
                                            sc[:, hh, b * P:(b + 1) * P], ident[:, :])
                    m.then_inc(s["pT_ps"], 1)
                pe.wait_ge(s["drow_ready"], i + 1)
                for n, b in ((1, 4), (2, 5), (0, 6), (3, 7)):
                    for c in range(4):
                        m = t.transpose(bank[b][:, c * P:c * P + r], rows[0:r, n, c * P:(c + 1) * P], ident[0:r, 0:r])
                m.then_inc(s["rT_ps"], 1)
                if not sampled:
                    pe.wait_ge(s["pT_sb"], i + 1)
                for c in range(4):
                    m = t.transpose(bank[0][:, c * P:c * P + r], rows[0:r, 4, c * P:(c + 1) * P], ident[0:r, 0:r])
                m.then_inc(s["rT_ps"], 1)
                if not sampled:
                    for hh in range(AH):
                        g, p = divmod(hh, GRP)
                        for b, v in enumerate((v_old[:, :], kv[:, 1, :])):
                            m = t.matmul(bank[1][g * HD:(g + 1) * HD, p * P:(p + 1) * P],
                                         v[:, g * HD:(g + 1) * HD], pT[:, hh, b, :], start=(b == 0), stop=(b == 1))
                    m.then_inc(s["att_ps"], 1)
                pe.wait_ge(s["rT_a"], i + 1)
                pe.wait_ge(s["rT_v"], i + 1)
                for hh in range(DH):
                    c, o = hh // 2, (hh % 2) * HD
                    t.matmul(bank[2 + hh % 2][0:r, c * P:c * P + r],
                             rT[o:o + HD, 1, c, 0:r], rT[o:o + HD, 2, c, 0:r], start=True, stop=True)
                    m = t.matmul(bank[4 + hh % 2][0:r, c * P:c * P + r],
                                 rT[o:o + HD, 1, c, 0:r], rT[o:o + HD, 0, c, 0:r], start=True, stop=True)
                m.then_inc(s["gram_ps"], 1)
                if sampled:
                    pe.wait_ge(s["mm_masked"], 2)
                    pe.wait_ge(s["state_in"], 16 * 2 * DB)
                    for c in range(PAIRS):
                        for b in range(DB):
                            m = t.matmul(bank[6][0:r, c * P:(c + 1) * P], kgm[:, b, c, :], s2s[:, b, c, :],
                                         start=(b == 0), stop=(b == DB - 1))
                else:
                    for c in range(PAIRS):
                        m = t.matmul(bank[6][0:r, c * P:(c + 1) * P], rT[:, 3, c, 0:r], s2[:, c, :], start=True, stop=True)
                m.then_inc(s["kgs_ps"], 1)
                n_lv = 3 if sampled else len(LEVELS) - 1
                if not sampled:
                    pe.wait_ge(s["att_sb"], i + 1)
                gaps = {2: ((), (0, 1, 2)), 3: ((3, 4), (5,)), 4: ((6, 7), (8,)), 5: ((9, 10), (11,))}
                for n in range(n_lv):
                    if ahead and n in gaps:
                        dqkv(i + 1, P, gaps[n][0])
                    pe.wait_ge(s["b_ready"], NB * i + n + 1)
                    if n:
                        pe.wait_ge(s["xx_ready"], NX * i + n)
                    for hh in range(DH):
                        rhs = xx[0:r, hh, 0, 0:r] if n else ident[0:r, 0:r]
                        m = t.matmul(bank[hh // 4][0:r, (hh % 4) * P:(hh % 4) * P + r], bt[0:r, hh, 0:r], rhs,
                                     start=True, stop=True)
                    m.then_inc(s["t_ps"], 1)
                    if ahead and n == 1:
                        pe.wait_ge(s["y0_ready"], i + 1)
                        x_T(i + 1, P)
                    if ahead and n in gaps:
                        dqkv(i + 1, P, gaps[n][1])
                    if n:
                        pe.wait_ge(s["t_sb"], (NX - 1) * i + n)
                        for hh in range(DH):
                            b, o = 2 + hh // 2, (hh % 2) * 256
                            t.matmul(bank[b][0:r, o:o + r], xx[0:r, hh, 1, 0:r], t1[0:r, hh, 0:r], start=True, stop=True)
                            m = t.matmul(bank[b][0:r, o + P:o + P + r], t1[0:r, hh, 0:r], xx[0:r, hh, 1, 0:r], start=True, stop=True)
                        m.then_inc(s["zz_ps"], 1)
                pe.wait_ge(s["y0_ready"], i + 1)
                pe.wait_ge(s["xx_ready"], NX * i + n_lv)

                def heads(b, lhs, rhs, done):
                    for hh in range(DH):
                        m = t.matmul(bank[b][0:r, hh * HD:(hh + 1) * HD], lhs(hh), rhs[0:r, hh * HD:(hh + 1) * HD],
                                     start=True, stop=True)
                    m.then_inc(done, 1)

                if ahead:
                    pe.wait_ge(s["cin_ready"], 3 * i + 6)
                heads(6, lambda hh: xx[0:r, hh, 1, 0:r], y0, s["y1_ps"])
                if ahead:
                    queries(i + 1, P, (0,))
                if not sampled:
                    pe.wait_ge(s["b_ready"], NB * i + NB)
                    pe.wait_ge(s["y1_sb"], i + 1)
                    heads(7, lambda hh: bt[0:r, hh, 0:r], y1, s["ty_ps"])
                    if ahead:
                        queries(i + 1, P, (1,))
                    pe.wait_ge(s["ty_sb"], i + 1)
                    heads(6, lambda hh: xx[0:r, hh, 1, 0:r], ty, s["yz_ps"])
                    if ahead:
                        queries(i + 1, P, (2, 3))
                pe.wait_ge(s["vn_ready"], i + 1)
                for c in range(PAIRS):
                    o = bank[0][0:r, c * P:(c + 1) * P]
                    if sampled:
                        for b in range(DB):
                            t.matmul(o, qgm[:, b, c, :], s2s[:, b, c, :], start=(b == 0), stop=False)
                    else:
                        t.matmul(o, rT[:, 4, c, 0:r], s2[:, c, :], start=True, stop=False)
                    for e in range(2):
                        hh = 2 * c + e
                        m = t.matmul(bank[0][0:r, hh * HD:(hh + 1) * HD], qk[0:r, hh, 0:r],
                                     vn[0:r, hh * HD:(hh + 1) * HD], start=False, stop=(e == 1))
                m.then_inc(s["o_ps"], 1)
                if sampled:
                    for b in range(DB):
                        pe.wait_ge(s["ktm_ready"], b + 1)
                        if b >= 2:
                            pe.wait_ge(s["supd_done"], b - 1)
                        for c in range(PAIRS):
                            m = t.matmul(bank[1 + b % 2][:, c * P:(c + 1) * P], ktm[0:r, b % 2, c * P:(c + 1) * P],
                                         vn[0:r, c * P:(c + 1) * P], start=True, stop=True)
                        m.then_inc(s["supd_ps"], 1)
                else:
                    for c in range(PAIRS):
                        m = t.matmul(bank[1][:, c * P:(c + 1) * P], rows[0:r, 5, c * P:(c + 1) * P],
                                     vn[0:r, c * P:(c + 1) * P], start=True, stop=True)
                    m.then_inc(s["upd_ps"], 1)
                if ahead:
                    keys_values(i + 1, P)
                pe.wait_ge(s["dn_ready"], i + 1)
                if sampled:
                    sampled_attention()
                for c in range(4):
                    m = t.transpose(bank[5][:, c * P:c * P + r], dn[0:r, c * P:(c + 1) * P], ident[0:r, 0:r])
                m.then_inc(s["dnT_ps"], 1)
                if ahead:
                    z_rows(i + 1, P)

            def sampled_attention():
                pe.wait_ge(s["cache_in"], 32)
                for b in range(DB):
                    m = t.transpose(bank[1 + b // 4][:, (b % 4) * P:(b % 4 + 1) * P], kc[:, b, :], ident[:, :])
                m.then_inc(s["kcT_ps"], 1)
                pe.wait_ge(s["kcT_sb"], 1)
                for b in range(DB):
                    for g in range(2):
                        o = (b % 3) * SKEYS
                        q = qT[:, :, :].rearrange("p c t -> p (c t)")[g * HD:(g + 1) * HD, b * GRP * DS:(b + 1) * GRP * DS]
                        bk = bank[1 + 3 * g + b // 3]
                        t.matmul(bk[0:GRP * DS, o:o + WIN], q, kcT[g * HD:(g + 1) * HD, b, :], start=True, stop=True)
                        m = t.matmul(bk[0:GRP * DS, o + WIN:o + SKEYS], q,
                                     kT[g * HD:(g + 1) * HD, P + b * DS:P + (b + 1) * DS], start=True, stop=True)
                m.then_inc(s["score_ps"], 1)
                pe.wait_ge(s["sprobs"], 1)
                for n in range(2 * DB):
                    t.transpose(bank[1][:, n * 32:(n + 1) * 32], ssc[0:32, n, 0:WIN], ident[0:32, 0:32])
                    m = t.transpose(bank[2][0:DS, n * 32:(n + 1) * 32], ssc[0:32, n, WIN:SKEYS], ident[0:32, 0:32])
                m.then_inc(s["pT_ps"], 1)
                pe.wait_ge(s["pT_sb"], TILES + 1)
                pe.wait_ge(s["vnew_in"], 16 * DB)
                for b in range(DB):
                    for g in range(2):
                        n = b * 2 + g
                        o = bank[3][g * HD:(g + 1) * HD, n * 32 % 512 - g * 32:n * 32 % 512 - g * 32 + 32]
                        t.matmul(o, vc[:, b, g * HD:(g + 1) * HD], spT[:, n, :], start=True, stop=False)
                        m = t.matmul(o, vnew[0:DS, b, g * HD:(g + 1) * HD], spTn[0:DS, n, :], start=False, stop=True)
                m.then_inc(s["att_ps"], 1)
                pe.wait_ge(s["att_sb"], TILES + 1)

            NB = len(LEVELS)
            NX = len(LEVELS) - 1
            front(0)
            pe.wait_ge(s["consts"], 2)
            pe.wait_ge(s["w_out_in"], 16 * 9)
            tile(0, P, False, True, False)
            with pe.Fori(1, TILES - 1) as i:
                tile(i, P, False, True, True)
            tile(TILES - 1, P, False, False, True)
            out_products(TILES - 1, P)
            pe.wait_ge(s["h_ready"], TILES)
            for c in range(CB):
                m = t.transpose(bank[c // 4][0:3, (c % 4) * P:(c % 4 + 1) * P], cin[:, c, P:P + TAPS - 1], ident[:, :])
            m.then_inc(s["conv_ps"], 1)
            front_sampled(TILES, NS)
            tile(TILES, NS, True, False, False)
            out_products(TILES, NS)

        @block.scalar
        def _(act):
            ac = nc.scalar
            row = lambda ap, n: ap.rearrange("(o n) -> o n", o=1).to_broadcast([P, n])
            act.dma_start(sinks[:, :], row(a["attn_sinks"][0], AH)).then_inc(s["const_in"], 16)
            act.dma_start(neg_a[:, :], row(a["dn_a_log"][0], DH)).then_inc(s["const_in"], 16)
            act.dma_start(dtb[:, :], row(a["dn_dt_bias"][0], DH)).then_inc(s["const_in"], 16)
            act.dma_start(dnn[:, :], row(a["dn_norm"][0], HD)).then_inc(s["const_in"], 16)
            act.dma_start(dist_s[:, :], a["c_dist"]).then_inc(s["const_in"], 16)
            act.dma_start(slope_s[:, :], a["c_slope"]).then_inc(s["const_in"], 16)
            with nc.allow_non_contiguous_dma(reason="small weights onto the partitions"):
                act.dma_start(g_mix[:, :], a["norm_mix"][0].rearrange("(k p) -> p k", p=P)).then_inc(s["const_in"], 16)
                for j in range(TAPS):
                    act.dma_start(cw[:, j, :], a["conv_w"][0, j].rearrange("(c p) -> p c", p=P)).then_inc(s["const_in"], 16)
                for hh in range(AH):
                    gg, p = divmod(hh, GRP)
                    act.dma_start(sink_s[p * DS:(p + 1) * DS, gg:gg + 1],
                                   a["attn_sinks"][0:1, hh:hh + 1].to_broadcast([DS, 1])).then_inc(s["const_in"], 16)
            act.wait_ge(s["consts"], 1)
            act.wait_ge(s["const_in"], 16 * (6 + 1 + TAPS + AH))
            ac.activation(neg_a[:, :], neg_a[:, :], ACT.Exp)
            act.drain()
            ac.mul(neg_a[:, :], neg_a[:, :], -1.0)

            def x_rms(i, r):
                act.wait_ge(s["x_in"], 16 * (i + 1))
                ac.activation(aT[0:r, :, :].rearrange("p k t -> p (k t)"), x[0:r, :], ACT.Square, accum_out=st[0:r, 0:1])
                act.drain()
                ac.activation(st[0:r, 1:2], st[0:r, 0:1], ACT.Sqrt, scale=1.0 / D, bias=eps[0:r, :]).then_inc(s["rms"], 1)

            def conv_in(i, r, sampled, b):
                act.wait_ge(s["dqkv_ps"], 3 * i + b + 1)
                if sampled:
                    src = bank[6 + b % 2][:, :].rearrange("p (c t) -> p c t", c=4)[:, :, 0:r].rearrange("p c (q t) -> p c q t", t=DS)
                    for c in range(4):
                        dst = cin[:, b * 4 + c, 0:DB * 11].rearrange("p (q t) -> p q t", t=11)[:, :, 3:11]
                        m = ac.activation(dst, src[:, c], ACT.Copy)
                else:
                    m = ac.activation(cin[:, b * 4:b * 4 + 4, 3:3 + P],
                                      bank[6 + b % 2][:, :].rearrange("p (c t) -> p c t", c=4), ACT.Copy)
                m.then_inc(s["cin_ready"], 1)

            def queries(i, r, sampled):
                act.wait_ge(s["q_ps"], i + 1)
                if sampled:
                    for p in range(GRP):
                        m = ac.activation(qT_s[:, :, p, :], bank[2][:, p * P:p * P + NS].rearrange("p (b t) -> p b t", b=DB), ACT.Copy, scale=HD ** -0.5)
                else:
                    m = ac.activation(qT[:, :, 0:r], bank[2][:, :].rearrange("p (c t) -> p c t", c=GRP)[:, :, 0:r], ACT.Copy, scale=HD ** -0.5)
                m.then_inc(s["q_sb"], 1)

            def keys_values(i, r, sampled):
                act.wait_ge(s["kv_ps"], i + 1)
                if sampled:
                    act.wait_ge(s["state_out"], 16 * (2 + DH))
                ac.activation(kT[:, P:P + r], bank[3][:, 256:256 + r], ACT.Copy)
                ac.activation(ab_raw[0:r, :], bank[3][0:r, 384:400], ACT.Copy)
                ac.activation(kv[0:r, :, :], bank[3][0:r, 0:256].rearrange("p (c t) -> p c t", c=2), ACT.Copy).then_inc(s["kv_sb"], 1)

            def z_gate(i, r):
                act.wait_ge(s["z_ps"], i + 1)
                ac.activation(zs[0:r, :], bank[7][0:r, :], ACT.Silu).then_inc(s["z_sb"], 1)

            def after_conv(i, r):
                act.wait_ge(s["conv_done"], i + 1)
                ac.activation(cs[:, :, 0:r], cacc[:, :, 0:r], ACT.Silu).then_inc(s["silu_done"], 1)

            def front(i, r, sampled):
                x_rms(i, r)
                if sampled:
                    for n, b in enumerate((0, 1, 4)):
                        act.wait_ge(s["conv_ps"], 2 + n)
                        m = ac.activation(crow[0:r, n * 512:(n + 1) * 512], bank[b][0:r, :], ACT.Copy)
                    m.then_inc(s["conv_sb"], 1)
                for b in range(3):
                    conv_in(i, r, sampled, b)
                queries(i, r, sampled)
                keys_values(i, r, sampled)
                z_gate(i, r)

            def tile(i, r, sampled, ahead):
                if sampled:
                    act.wait_ge(s["stc_ps"], 1)
                    for c in range(CB):
                        m = ac.activation(cin[:, c, 0:DB * 11].rearrange("p (q t) -> p q t", t=11)[:, :, 0:3],
                                          bank[3][:, c * 24:(c + 1) * 24].rearrange("p (q t) -> p q t", t=3), ACT.Copy)
                    m.then_inc(s["stc_sb"], 1)
                    act.wait_ge(s["crow_out"], 16 * DB)
                    after_conv(i, r)
                act.wait_ge(s["soft_in"], i + 1)
                ac.activation(gt[0:r, 2, :], gt[0:r, 1, :], ACT.Exp, scale=-1.0)
                ac.activation(gt[0:r, 3, :], ab_raw[0:r, DH:2 * DH], ACT.Exp, scale=-1.0)
                act.drain()
                ac.activation(gt[0:r, 2, :], gt[0:r, 2, :], ACT.Ln, bias=one[0:r, :]).then_inc(s["soft_out"], 1)
                act.wait_ge(s["rows_ps"], i + 1)
                for n in range(2):
                    m = ac.activation(sq[0:r, n * 512:(n + 1) * 512], bank[4 + n][0:r, :], ACT.Square)
                m.then_inc(s["sq_done"], 1)
                act.wait_ge(s["ssq_done"], i + 1)
                ac.activation(rn[0:r, 1, :], rn[0:r, 0, :], ACT.Sqrt, bias=eps[0:r, :]).then_inc(s["rn_sqrt"], 1)
                if not sampled:
                    act.wait_ge(s["nm_ready"], i + 1)
                    for hh in range(AH):
                        ac.activation(sc[:, hh, :], sc[:, hh, :], ACT.Exp, bias=am[:, 2, hh:hh + 1], accum_out=am[:, 4, hh:hh + 1])
                    act.drain()
                    ac.activation(am[:, 3, :], am[:, 3, :], ACT.Exp).then_inc(s["prob_done"], 1)
                act.wait_ge(s["e_in"], i + 1)
                ac.activation(gt[0:r, 8, :], gt[0:r, 6, :], ACT.Exp)
                ac.activation(gt[0:r, 9, :], gt[0:r, 7, :], ACT.Exp)
                if sampled:
                    ac.activation(egb[:, :, :], egb[:, :, :], ACT.Exp)
                else:
                    ac.activation(eg[:, :], eg[:, :], ACT.Exp)
                ac.activation(dt_[0:r, :, 0:r], dt_[0:r, :, 0:r], ACT.Exp).then_inc(s["exp_ready"], 1)
                if not sampled:
                    act.wait_ge(s["pT_ps"], i + 1)
                    for b in range(4):
                        m = ac.activation(pT[:, 2 * b:2 * b + 2, :, :], bank[b][:, :].rearrange("p (h c t) -> p h c t", h=2, c=2), ACT.Copy)
                    m.then_inc(s["pT_sb"], 1)
                act.wait_ge(s["rT_ps"], 2 * i + 2)
                for n, b in ((1, 4), (2, 5), (4, 0)):
                    m = ac.activation(rT[:, n, :, 0:r], bank[b][:, :].rearrange("p (c t) -> p c t", c=4)[:, :, 0:r], ACT.Copy)
                m.then_inc(s["rT_a"], 1)
                if not sampled:
                    act.wait_ge(s["att_ps"], i + 1)
                    ac.activation(attT[:, :, :], bank[1][:, :].rearrange("p (c t) -> p c t", c=4), ACT.Copy)
                    ac.activation(kT[:, 0:P], kT[:, P:2 * P], ACT.Copy)
                    ac.activation(v_old[:, :], kv[:, 1, :], ACT.Copy)
                    ac.activation(dist[:, 0:WIN], dist_old[:, :], ACT.Copy).then_inc(s["att_sb"], 1)
                if ahead:
                    x_rms(i + 1, P)
                n_lv = 3 if sampled else len(LEVELS) - 1
                for n in range(1, n_lv):
                    act.wait_ge(s["t_ps"], NX * i + n + 1)
                    for b in range(2):
                        m = ac.activation(t1[0:r, 4 * b:4 * b + 4, 0:r],
                                          bank[b][0:r, :].rearrange("p (c t) -> p c t", c=4)[:, :, 0:r], ACT.Copy)
                    m.then_inc(s["t_sb"], 1)
                    if ahead and n in (3, 4, 5):
                        conv_in(i + 1, P, False, n - 3)
                if not sampled:
                    act.wait_ge(s["y1_ps"], i + 1)
                    ac.activation(y1[0:r, :], bank[6][0:r, :], ACT.Copy).then_inc(s["y1_sb"], 1)
                    act.wait_ge(s["ty_ps"], i + 1)
                    ac.activation(ty[0:r, :], bank[7][0:r, :], ACT.Copy).then_inc(s["ty_sb"], 1)
                if ahead:
                    queries(i + 1, P, False)
                act.wait_ge(s["o_ps"], i + 1)
                ac.activation(sq[0:r, 0:512], bank[0][0:r, :], ACT.Square).then_inc(s["osq_done"], 1)
                act.wait_ge(s["ossq"], i + 1)
                ac.activation(rn[0:r, 1, 0:DH], rn[0:r, 0, 0:DH], ACT.Sqrt, scale=1.0 / HD, bias=eps[0:r, :]).then_inc(s["orms"], 1)
                if ahead:
                    keys_values(i + 1, P, False)
                    after_conv(i + 1, P)
                if sampled:
                    act.wait_ge(s["kcT_ps"], 1)
                    for b in range(2):
                        m = ac.activation(kcT[:, 4 * b:4 * b + 4, :], bank[1 + b][:, :].rearrange("p (c t) -> p c t", c=4), ACT.Copy)
                    m.then_inc(s["kcT_sb"], 1)
                    act.wait_ge(s["nm_ready"], TILES + 1)
                    ac.activation(ssc[0:32, :, :], ssc[0:32, :, :], ACT.Exp)
                    ac.activation(sm[0:32, 3, :], sm[0:32, 3, :], ACT.Exp).then_inc(s["sexp"], 1)
                    act.wait_ge(s["pT_ps"], TILES + 1)
                    ac.activation(spT[:, :, :], bank[1][:, :].rearrange("p (n r) -> p n r", r=32), ACT.Copy)
                    ac.activation(spTn[0:DS, :, :], bank[2][0:DS, :].rearrange("p (n r) -> p n r", r=32), ACT.Copy).then_inc(s["pT_sb"], 1)
                    act.wait_ge(s["att_ps"], TILES + 1)
                    for p in range(GRP):
                        src = bank[3][:, :].rearrange("p (b g r) -> p b g r", b=DB, g=2)[:, :, 0, p * DS:(p + 1) * DS]
                        m = ac.activation(attT[:, p, 0:NS].rearrange("p (b t) -> p b t", b=DB), src, ACT.Copy)
                    m.then_inc(s["att_sb"], 1)
                if not sampled and not ahead:
                    act.wait_ge(s["h_out"], 16 * i)
                act.wait_ge(s["dnT_ps"], i + 1)
                ac.activation(dnT[:, :, 0:r], bank[5][:, :].rearrange("p (c t) -> p c t", c=4)[:, :, 0:r], ACT.Copy).then_inc(s["dnT_sb"], 1)
                if ahead:
                    z_gate(i + 1, P)

            NX = len(LEVELS) - 1
            front(0, P, False)
            after_conv(0, P)
            act.wait_ge(s["consts"], 2)
            with act.Fori(0, TILES - 1) as i:
                tile(i, P, False, True)
            tile(TILES - 1, P, False, False)
            act.wait_ge(s["conv_ps"], 1)
            for b in range(3):
                m = ac.activation(stage3[0:3, b * 512:(b + 1) * 512], bank[b][0:3, :], ACT.Copy)
            m.then_inc(s["conv_sb"], 1)
            act.wait_ge(s["conv_sb"], 1)
            act.dma_start(out["c_p"][0, 0], stage3[0:3, :]).then_inc(s["misc_in"], 16)
            act.wait_ge(s["misc_in"], 16)
            front(TILES, NS, True)
            tile(TILES, NS, True, False)

        @block.vector
        def _(dve):
            v = nc.vector

            def bc(ap, n):
                sh = list(ap.shape)
                return ap.rearrange("p (h o) -> p h o", o=1).to_broadcast([sh[0], sh[1], n])

            def hd(ap):
                return ap.rearrange("p (h d) -> p h d", d=HD)

            dve.wait_ge(s["consts"], 1)
            dve.wait_ge(s["const_in"], 16 * (6 + 1 + TAPS + AH))

            def x_norm(i, r):
                dve.wait_ge(s["rms"], i + 1)
                v.reciprocal(st[0:r, 2:3], st[0:r, 1:2])
                dve.drain()
                v.tensor_scalar(xn[0:r, :], x[0:r, :], st[0:r, 2:3], None, ALU.mult).then_inc(s["xn_ready"], 1)

            def x_T(i, r):
                dve.wait_ge(s["xT_ps"], i + 1)
                for b in range(2):
                    m = v.tensor_tensor(aT[:, 4 * b:4 * b + 4, 0:r], bank[6 + b][:, :].rearrange("p (k t) -> p k t", k=4)[:, :, 0:r],
                                        bc(g_mix[:, 4 * b:4 * b + 4], r), ALU.mult)
                m.then_inc(s["aT_ready"], 1)

            def conv(i, sampled, b, taps):
                if taps[0] == 0:
                    dve.wait_ge(s["cin_ready"], 3 * i + b + 1)
                for j in taps:
                    for c in range(4 * b, 4 * b + 4):
                        if sampled:
                            src = cin[:, c, 0:DB * 11].rearrange("p (q t) -> p q t", t=11)[:, :, j:j + DS]
                            dst = cacc[:, c, 0:NS].rearrange("p (q t) -> p q t", t=DS)
                        else:
                            src, dst = cin[:, c, j:j + P], cacc[:, c, :]
                        if j == 0:
                            m = v.tensor_scalar(dst, src, cw[:, j, c:c + 1], None, ALU.mult)
                        else:
                            m = v.scalar_tensor_tensor(dst, src, cw[:, j, c:c + 1], dst, ALU.mult, ALU.add)
                    if j < TAPS - 1:
                        dve.drain()
                if b == 2 and taps[-1] == TAPS - 1:
                    m.then_inc(s["conv_done"], 1)
                    if not sampled:
                        dve.drain()
                        v.tensor_copy(cin[:, :, 0:TAPS - 1], cin[:, :, P:P + TAPS - 1])

            def front(i, r, sampled):
                x_norm(i, r)
                x_T(i, r)
                if sampled:
                    dve.wait_ge(s["stc_sb"], 1)
                for b in range(3):
                    conv(i, sampled, b, range(TAPS))

            def residual(i, r, n):
                dve.wait_ge(s["proj_ps"], 2 * i + n + 1)
                if n == 0:
                    dve.wait_ge(s["xres_in"], 16 * (i + 1))
                m = v.tensor_tensor(h[0:r, n * 512:(n + 1) * 512], x_res[0:r, n * 512:(n + 1) * 512], bank[2 + n][0:r, :], ALU.add)
                if n == 1:
                    m.then_inc(s["h_ready"], 1)

            def tile(i, r, sampled, ahead, before):
                dve.wait_ge(s["kv_sb"], i + 1)
                v.tensor_tensor(gt[0:r, 0, :], ab_raw[0:r, 0:DH], dtb[0:r, :], ALU.add)
                dve.drain()
                v.tensor_scalar(gt[0:r, 1, :], gt[0:r, 0, :], -1.0, None, ALU.mult)
                dve.drain()
                v.tensor_tensor(gt[0:r, 1, :], gt[0:r, 0, :], gt[0:r, 1, :], ALU.max).then_inc(s["soft_in"], 1)
                dve.wait_ge(s["soft_out"], i + 1)
                v.tensor_scalar(gt[0:r, 0, :], gt[0:r, 0, :], 0.0, None, ALU.max)
                v.tensor_scalar(gt[0:r, 3, :], gt[0:r, 3, :], 1.0, None, ALU.add)
                dve.drain()
                v.tensor_tensor(gt[0:r, 0, :], gt[0:r, 0, :], gt[0:r, 2, :], ALU.add)
                v.reciprocal(gt[0:r, 4, :], gt[0:r, 3, :])
                dve.drain()
                v.tensor_tensor(gt[0:r, 5, :], gt[0:r, 0, :], neg_a[0:r, :], ALU.mult).then_inc(s["gate_ready"], 1)
                if sampled:
                    dve.drain()
                    dve.wait_ge(s["over_clear"], 1)
                    v.tensor_tensor(gmb[0:r, :, :], gt[0:r, 5, :].rearrange("p (o h) -> p o h", o=1).to_broadcast([r, DB, DH]),
                                    bc(seq_of[0:r, :], DH), ALU.mult).then_inc(s["mm_masked"], 1)
                if not sampled:
                    dve.wait_ge(s["score_ps"], i + 1)
                    for hh in range(AH):
                        m = v.scalar_tensor_tensor(sc[:, hh, :], dist[:, :], SLOPE[hh],
                                                   bank[hh // 2][:, (hh % 2) * 256:(hh % 2 + 1) * 256], ALU.mult, ALU.add)
                    m.then_inc(s["sc_ready"], 1)
                    dve.drain()
                    v.tensor_reduce(am[:, 0, :], sc[:, :, :], AXX, ALU.max)
                    dve.drain()
                    v.tensor_tensor(am[:, 1, :], am[:, 0, :], sinks[:, :], ALU.max)
                    dve.drain()
                    v.tensor_tensor(am[:, 3, :], sinks[:, :], am[:, 1, :], ALU.subtract)
                    v.tensor_scalar(am[:, 2, :], am[:, 1, :], -1.0, None, ALU.mult).then_inc(s["nm_ready"], 1)
                dve.wait_ge(s["sq_done"], i + 1)
                v.tensor_reduce(rn[0:r, 0, :], hd(sq[0:r, :]), AXX, ALU.add).then_inc(s["ssq_done"], 1)
                dve.wait_ge(s["gsum_ps"], i + 1)
                v.tensor_copy(gt[0:r, 6, :], bank[7][0:r, 0:DH])
                dve.drain()
                v.tensor_tensor(gt[0:r, 7, :], bank[7][0:r, DH:2 * DH], gt[0:r, 6, :], ALU.subtract)
                for c in range(2):
                    if sampled:
                        v.tensor_copy(egb[c * HD:(c + 1) * HD, :, :],
                                      bank[7][c * HD:(c + 1) * HD, 64:128].rearrange("p (b h e) -> p b h e", b=DB, e=2)[:, :, :, c])
                    else:
                        v.tensor_copy(eg[c * HD:(c + 1) * HD, :],
                                      bank[7][c * HD:(c + 1) * HD, 64:64 + DH].rearrange("p (h e) -> p h e", e=2)[:, :, c])
                for hh in range(DH):
                    m = v.tensor_scalar(dt_[0:r, hh, 0:r], bank[hh // 4][0:r, (hh % 4) * P:(hh % 4) * P + r],
                                        gt[0:r, 6, hh:hh + 1], 0.0, ALU.subtract, ALU.min)
                m.then_inc(s["e_in"], 1)
                if not sampled:
                    dve.wait_ge(s["prob_done"], i + 1)
                    v.tensor_tensor(am[:, 5, :], am[:, 4, :], am[:, 3, :], ALU.add)
                    dve.drain()
                    v.reciprocal(am[:, 0, :], am[:, 5, :])
                    dve.drain()
                    v.tensor_tensor(sc[:, :, :], sc[:, :, :], bc(am[:, 0, :], 2 * WIN), ALU.mult).then_inc(s["probs_ready"], 1)
                dve.wait_ge(s["rn_sqrt"], i + 1)
                v.reciprocal(rn[0:r, 2, :], rn[0:r, 1, :])
                dve.drain()
                dve.wait_ge(s["exp_ready"], i + 1)
                v.tensor_scalar(gt[0:r, 10, :], rn[0:r, 2, 0:DH], HD ** -0.5, None, ALU.mult)
                v.tensor_tensor(gt[0:r, 11, :], rn[0:r, 2, DH:16], gt[0:r, 4, :], ALU.mult)
                v.tensor_tensor(gt[0:r, 7, :], rn[0:r, 2, DH:16], gt[0:r, 9, :], ALU.mult)
                dve.drain()
                v.tensor_tensor(gt[0:r, 0, :], gt[0:r, 11, :], gt[0:r, 8, :], ALU.mult)
                v.tensor_tensor(gt[0:r, 1, :], gt[0:r, 10, :], gt[0:r, 8, :], ALU.mult)
                dve.drain()
                if before:
                    residual(i - 1, P, 0)
                for n, b, f in ((1, 5, rn[0:r, 2, DH:16]), (2, 5, gt[0:r, 11, :]), (0, 4, gt[0:r, 10, :]),
                                (3, 5, gt[0:r, 0, :]), (4, 4, gt[0:r, 1, :]), (5, 5, gt[0:r, 7, :])):
                    v.tensor_tensor(hd(rows[0:r, n, :]), hd(bank[b][0:r, :]), bc(f, HD), ALU.mult)
                    if before and n == 0:
                        residual(i - 1, P, 1)
                v.tensor_tensor(hd(vb[0:r, :]), hd(bank[6][0:r, :]), bc(gt[0:r, 4, :], HD), ALU.mult).then_inc(s["drow_ready"], 1)
                cum = tri8 if sampled else tri
                v.tensor_tensor(dt_[0:r, :, 0:r], dt_[0:r, :, 0:r],
                                cum[0:r, 0:r].rearrange("p (o t) -> p o t", o=1).to_broadcast([r, DH, r]), ALU.mult)
                dve.wait_ge(s["rT_ps"], 2 * i + 1)
                for n, b in ((0, 6), (3, 7)):
                    m = v.tensor_copy(rT[:, n, :, 0:r], bank[b][:, :].rearrange("p (c t) -> p c t", c=4)[:, :, 0:r])
                m.then_inc(s["rT_v"], 1)
                if sampled:
                    dve.drain()
                    dve.wait_ge(s["rT_a"], TILES + 1)
                    for b in range(DB):
                        v.tensor_copy(kgm[:, b, :, b * DS:(b + 1) * DS], rT[:, 3, :, b * DS:(b + 1) * DS])
                        m = v.tensor_copy(qgm[:, b, :, b * DS:(b + 1) * DS], rT[:, 4, :, b * DS:(b + 1) * DS])
                    m.then_inc(s["mm_masked"], 1)
                dve.wait_ge(s["gram_ps"], i + 1)
                for b in range(2):
                    v.tensor_tensor(lt[0:r, b:DH:2, 0:r], bank[2 + b][0:r, :].rearrange("p (c t) -> p c t", c=4)[:, :, 0:r],
                                    dt_[0:r, b:DH:2, 0:r], ALU.mult)
                    v.tensor_tensor(qk[0:r, b:DH:2, 0:r], bank[4 + b][0:r, :].rearrange("p (c t) -> p c t", c=4)[:, :, 0:r],
                                    dt_[0:r, b:DH:2, 0:r], ALU.mult)
                dve.drain()

                def cut(n):
                    v.tensor_tensor(bt[0:r, :, 0:r], lt[0:r, :, 0:r],
                                    level[0:r, n, 0:r].rearrange("p (o t) -> p o t", o=1).to_broadcast([r, DH, r]),
                                    ALU.mult).then_inc(s["b_ready"], 1)

                cut(0)
                dve.wait_ge(s["kgs_ps"], i + 1)
                v.tensor_tensor(y0[0:r, :], vb[0:r, :], bank[6][0:r, :], ALU.subtract).then_inc(s["y0_ready"], 1)
                ident_b = ident[0:r, 0:r].rearrange("p (o t) -> p o t", o=1)
                n_lv = 3 if sampled else len(LEVELS) - 1
                dve.drain()
                v.tensor_tensor(xx[0:r, :, 1, 0:r], ident_b.to_broadcast([r, DH, r]), bt[0:r, :, 0:r], ALU.subtract)
                for n in range(n_lv):
                    dve.wait_ge(s["t_ps"], NX * i + n + 1)
                    if n == 0:
                        for b in range(2):
                            m = v.tensor_tensor(xx[0:r, 4 * b:4 * b + 4, 0, 0:r], ident_b.to_broadcast([r, 4, r]),
                                            bank[b][0:r, :].rearrange("p (c t) -> p c t", c=4)[:, :, 0:r], ALU.subtract)
                        m.then_inc(s["xx_ready"], 1)
                        dve.drain()
                        cut(n + 1)
                        if ahead:
                            x_norm(i + 1, P)
                    else:
                        if n + 1 < (n_lv if sampled else n_lv + 1):
                            cut(n + 1)
                        if ahead and n == 4:
                            conv(i + 1, False, 0, (0, 1, 2))
                        if ahead and n == 5:
                            conv(i + 1, False, 0, (3,))
                            conv(i + 1, False, 1, (0, 1))
                        dve.wait_ge(s["zz_ps"], (NX - 1) * i + n)
                        for b in range(4):
                            xv = xx[0:r, 2 * b:2 * b + 2, :, 0:r]
                            zv = bank[2 + b][0:r, :].rearrange("p (h c t) -> p h c t", h=2, c=2)[:, :, :, 0:r]
                            m = v.tensor_tensor(xv, xv, zv, ALU.subtract)
                        m.then_inc(s["xx_ready"], 1)
                        if ahead and n == 1:
                            x_T(i + 1, P)
                if sampled:
                    dve.wait_ge(s["y1_ps"], i + 1)
                    v.tensor_copy(vn[0:r, :], bank[6][0:r, :]).then_inc(s["vn_ready"], 1)
                else:
                    if ahead:
                        conv(i + 1, False, 1, (2, 3))
                    dve.wait_ge(s["yz_ps"], i + 1)
                    v.tensor_tensor(vn[0:r, :], y1[0:r, :], bank[6][0:r, :], ALU.subtract).then_inc(s["vn_ready"], 1)
                    v.tensor_tensor(s2n[:, :, :], s2[:, :, :], bc(eg[:, :], P), ALU.mult)
                    if ahead:
                        conv(i + 1, False, 2, (0, 1))
                if sampled:
                    for b in range(DB):
                        if b >= 2:
                            dve.wait_ge(s["supd_ps"], b - 1)
                        v.tensor_scalar(ktm[0:r, b % 2, :], rows[0:r, 5, :], seq_of[0:r, b:b + 1], None, ALU.mult).then_inc(s["ktm_ready"], 1)
                        if b >= 1:
                            state_update(b - 1)
                    state_update(DB - 1)
                dve.wait_ge(s["osq_done"], i + 1)
                v.tensor_reduce(rn[0:r, 0, 0:DH], hd(sq[0:r, 0:512]), AXX, ALU.add).then_inc(s["ossq"], 1)
                if not sampled:
                    dve.drain()
                    dve.wait_ge(s["upd_ps"], i + 1)
                    for c in range(PAIRS):
                        v.tensor_tensor(s2[:, c, :], bank[1][:, c * P:(c + 1) * P], pair_diag[:, :], ALU.mult)
                    dve.drain()
                    v.tensor_tensor(s2[:, :, :], s2[:, :, :], s2n[:, :, :], ALU.add)
                dve.wait_ge(s["orms"], i + 1)
                v.reciprocal(rn[0:r, 2, 0:DH], rn[0:r, 1, 0:DH])
                dve.drain()
                v.tensor_tensor(hd(dn[0:r, :]), hd(bank[0][0:r, :]), bc(rn[0:r, 2, 0:DH], HD), ALU.mult)
                dve.drain()
                v.tensor_tensor(hd(dn[0:r, :]), hd(dn[0:r, :]),
                                dnn[0:r, :].rearrange("p (o d) -> p o d", o=1).to_broadcast([r, DH, HD]), ALU.mult)
                dve.drain()
                v.tensor_tensor(dn[0:r, :], dn[0:r, :], zs[0:r, :], ALU.mult).then_inc(s["dn_ready"], 1)
                if ahead:
                    conv(i + 1, False, 2, (2, 3))
                if sampled:
                    sampled_softmax()

            def state_update(b):
                dve.wait_ge(s["supd_ps"], b + 1)
                if b == 0:
                    dve.wait_ge(s["o_ps"], TILES + 1)
                for c in range(PAIRS):
                    v.tensor_scalar(s2s[:, b, c, :], s2s[:, b, c, :], egb[:, b, c:c + 1], None, ALU.mult)
                    v.tensor_tensor(s2n[:, c, :], bank[1 + b % 2][:, c * P:(c + 1) * P], pair_diag[:, :], ALU.mult)
                dve.drain()
                v.tensor_tensor(s2s[:, b, :, :], s2s[:, b, :, :], s2n[:, :, :], ALU.add).then_inc(s["supd_done"], 1)
                dve.drain()

            def sampled_softmax():
                dve.wait_ge(s["score_ps"], TILES + 1)
                for n in range(2 * DB):
                    v.scalar_tensor_tensor(ssc[0:32, n, :], dist_s[:, :], slope_s[:, n % 2:n % 2 + 1],
                                           bank[1 + 3 * (n % 2) + n // 6][0:32, (n // 2 % 3) * SKEYS:(n // 2 % 3 + 1) * SKEYS], ALU.mult, ALU.add)
                dve.drain()
                v.tensor_reduce(sm[0:32, 0, :], ssc[0:32, :, :], AXX, ALU.max)
                dve.drain()
                sk = sink_s[0:32, :].rearrange("p (o g) -> p o g", o=1).to_broadcast([32, DB, 2])
                as_bg = lambda ap: ap.rearrange("p (b g) -> p b g", g=2)
                v.tensor_tensor(as_bg(sm[0:32, 1, :]), as_bg(sm[0:32, 0, :]), sk, ALU.max)
                dve.drain()
                v.tensor_tensor(as_bg(sm[0:32, 3, :]), sk, as_bg(sm[0:32, 1, :]), ALU.subtract)
                v.tensor_tensor(ssc[0:32, :, :], ssc[0:32, :, :], bc(sm[0:32, 1, :], SKEYS), ALU.subtract).then_inc(s["nm_ready"], 1)
                dve.wait_ge(s["sexp"], 1)
                v.tensor_reduce(sm[0:32, 4, :], ssc[0:32, :, :], AXX, ALU.add)
                dve.drain()
                v.tensor_tensor(sm[0:32, 5, :], sm[0:32, 4, :], sm[0:32, 3, :], ALU.add)
                dve.drain()
                v.reciprocal(sm[0:32, 2, :], sm[0:32, 5, :])
                dve.drain()
                v.tensor_tensor(ssc[0:32, :, :], ssc[0:32, :, :], bc(sm[0:32, 2, :], SKEYS), ALU.mult).then_inc(s["sprobs"], 1)

            NX = len(LEVELS) - 1
            front(0, P, False)
            dve.wait_ge(s["consts"], 2)
            tile(0, P, False, True, False)
            with dve.Fori(1, TILES - 1) as i:
                tile(i, P, False, True, True)
            tile(TILES - 1, P, False, False, True)
            for n in range(2):
                residual(TILES - 1, P, n)
            front(TILES, NS, True)
            tile(TILES, NS, True, False, False)
            for n in range(2):
                residual(TILES, NS, n)


def peer_block(nc, sems, a, out, h_rows):
    RING = 8
    STEP = 16
    ON_PE = (0, 1, 2, 3, 4, 5, 7, 9, 11, 13)
    PB = PLE // P
    NPE = len(ON_PE)
    with ExitStack() as ctx:
        def sb(name, shape, dt=F32):
            return ctx.enter_context(nc.sbuf_tensor(name, shape, dt))

        def sem(name):
            return sems.enter_context(nc.semaphore("peer_" + name))

        bank = [ctx.enter_context(nc.psum_tensor(f"pbank{b}", [P, 512], F32)) for b in range(8)]
        wq = sb("wq_sb", [P, KD, PH * 2 * P])
        keysT = sb("keysT_sb", [P, 16, P])
        ident = sb("p_ident", [P, P])
        g_ffn = sb("g_ffn_sb", [P, D])
        iota16 = sb("iota16", [P, TOPK])
        iota_i = sb("iota16i", [P, TOPK], I32)
        eps = sb("p_eps", [P, 1])
        c_nxt = sb("c_nxt", [P, D])
        h_cur = sb("h_cur", [P, D])
        c_cur = sb("c_cur", [P, D])
        st = sb("p_stats", [P, 4])
        gst = sb("gate_stats", [P, 8])
        wg = sb("ple_gate_sb", [P, KD, D])
        wi = sb("ple_in_sb", [P, PB, D])
        g_ple = sb("g_ple_sb", [P, KD])
        g_fin = sb("g_fin_sb", [P, D])
        ple = sb("p_tile", [P, PLE])
        pleT = sb("pT_tile", [P, PB, P])
        cT = sb("cT_sb", [P, KD, P])
        qT = sb("pqT_sb", [P, 16, P])
        q_flat = qT[:, :, :].rearrange("p n t -> p (n t)")
        y, en = q_flat[:, 0:D], q_flat[:, D:2 * D]
        sco = sb("key_scores", [P, 16, P])
        v1 = sb("top_val", [P, 2, TOPK])
        x1 = sb("top_idx", [P, 2, TOPK], U32)
        x1f = sb("top_idxf", [P, 2, TOPK])
        cand = sb("cand", [P, TOPK, TOPK])
        cand2 = sb("cand_left", [P, TOPK * TOPK])
        sst = cand[:, :, :].rearrange("p a b -> p (a b)").rearrange("p (f n) -> p f n", f=2)
        sst2 = cand2[:, :].rearrange("p (f n) -> p f n", f=2)
        sc16 = sb("best_val", [P, TOPK])
        ci = sb("best_idx", [P, TOPK], U32)
        cab = sb("best_ab", [P, 2, TOPK], U32)
        cabf = sb("best_abf", [P, 2, TOPK])
        eq = sb("onehot", [P, 2, TOPK, TOPK])
        e12 = sb("best_keys", [P, 2, TOPK])
        sc_all = sb("gate_raw", [P, SLOTS])
        gate = sb("gates", [P, SLOTS])
        idx = sb("expert_all", [P, ALLT * SLOTS], I32)
        gs = sb("gate_sum", [P, 2, PH])
        stage = [sb(f"idx_stage{k}", [P, RING], I32) for k in range(2)]
        rows = sb("expert_rows", [P, RING, D])
        keys = rows[:, 0:2, :].rearrange("p k d -> p (k d)").rearrange("p (n d) -> p n d", n=16)
        dot16 = sb("dots_here", [P, STEP])
        dots = sb("dots", [P, SLOTS])
        wgt = sb("weights", [P, SLOTS])
        w16 = sb("weights_here", [P, STEP])
        diag = sb("weight_diag", [P, NPE, P])
        zero = sb("p_zero", [P, P])
        fold = sb("p_fold", [P, NS])
        HALF = SLOTS // 2

        names = ("p_consts wq_in0 wq_in1 keysT_ps keysT_sb c_in h_in p_in wg_in g_in rms c_ready cT_ps cT_sb q_ps q_sb "
                 "s_ps s_sb idx_ready gate_sub gate_exp dots_ready gelu_done cur_free cur_ready k_in "
                 "passed staged diag_ready w_ready act_passed pe_passed dve_passed vacc_ps vacc_free gate_rms "
                 "en_ready enT_ps enT_sb pT_sb gate_ps sig_done sum_ready rms2 y_ready y_out").split()
        s = {n: sem(n) for n in names}
        got = [sem(f"row_in{k}") for k in range(RING)]
        used = [sem(f"row_used{k}") for k in range(RING)]

        def turn(i, part, j, half):
            return (i * 2 + part) * (SLOTS // RING) + j * (STEP // RING) + half

        def turn_last(i, part, j, half):
            return TILES * 2 * (SLOTS // RING) + part * (HALF // RING) + j * (STEP // RING) + half

        u_tab, v_tab = a["peer_u"][0], a["peer_v"][0]
        block = ctx.enter_context(nc.Block())

        def y_rows(i):
            return out["y_p"][0, bass.ds(i * P, P), :]

        @block.sync
        def _(sp):
            sp.dma_start(keys[:, 0:16:2, :], a["peer_keys1"][0].rearrange("h n d -> n h d")).then_inc(s["k_in"], 16)
            sp.dma_start(keys[:, 1:16:2, :], a["peer_keys2"][0].rearrange("h n d -> n h d")).then_inc(s["k_in"], 16)
            sp.dma_start(g_ffn[:, :], a["norm_ffn"].to_broadcast([P, D])).then_inc(s["k_in"], 16)
            sp.dma_start(c_nxt[:, :], h_rows[0:P, :]).then_inc(s["c_in"], 16)
            for b in range(2):
                sp.dma_start(wq[:, :, b * D:(b + 1) * D],
                             a["peer_wq"][0, :, b * D:(b + 1) * D].rearrange("(k p) n -> p k n", p=P)).then_inc(s[f"wq_in{b}"], 16)
            sp.dma_start(h_cur[:, :], h_rows[0:P, :]).then_inc(s["h_in"], 16)
            sp.dma_start(ple[:, :], a["p_prompt"][0, 0, 0:P, :]).then_inc(s["p_in"], 16)
            sp.wait_ge(s["cur_ready"], 1)
            sp.dma_start(c_nxt[:, :], h_rows[P:2 * P, :]).then_inc(s["c_in"], 16)
            sp.dma_start(g_fin[:, :], a["norm_final"].rearrange("(o n) -> o n", o=1).to_broadcast([P, D])).then_inc(s["g_in"], 16)
            with nc.allow_non_contiguous_dma(reason="a weight per channel onto the partitions"):
                sp.dma_start(g_ple[:, :], a["norm_ple"][0].rearrange("(k p) -> p k", p=P)).then_inc(s["g_in"], 16)
            for k in range(KD):
                sp.dma_start(wg[:, k, :], a["ple_gate"][0, k * P:(k + 1) * P, :]).then_inc(s["wg_in"], 16)
            sp.dma_start(wi[:, :, :], a["ple_in"][0].rearrange("(k p) n -> p k n", p=P)).then_inc(s["wg_in"], 16)
            sp.wait_ge(s["cur_ready"], 2)
            sp.dma_start(c_nxt[:, :], h_rows[2 * P:3 * P, :]).then_inc(s["c_in"], 16)

            def gate_io(i, y_dst, p_src, r):
                sp.wait_ge(s["pT_sb"], i + 1)
                sp.dma_start(ple[0:r, :], p_src).then_inc(s["p_in"], 16)
                sp.wait_ge(s["sum_ready"], i + 1)
                sp.dma_start(h_cur[:, :], h_rows[bass.ds(i * P + P, P), :]).then_inc(s["h_in"], 16)
                sp.wait_ge(s["y_ready"], i + 1)
                sp.dma_start(y_dst, y).then_inc(s["y_out"], 16)

            with sp.Fori(1, TILES - 1) as i:
                gate_io(i - 1, y_rows(i - 1), a["p_prompt"][0, 0, bass.ds(i * P, P), :], P)
                sp.wait_ge(s["cur_ready"], i + 2)
                sp.dma_start(c_nxt[:, :], h_rows[bass.ds(i * P + 2 * P, P), :]).then_inc(s["c_in"], 16)
            gate_io(TILES - 2, y_rows(TILES - 2), a["p_prompt"][0, 0, SEQ - P:SEQ, :], P)
            gate_io(TILES - 1, y_rows(TILES - 1), a["p_sample"][0].rearrange("b t d -> (b t) d"), NS)
            sp.wait_ge(s["y_ready"], ALLT)
            sp.dma_start(out["y_s"].rearrange("b t d -> (b t) d"), y[0:NS, :]).then_inc(s["y_out"], 16)
            sp.wait_ge(s["y_out"], 16 * ALLT)

        @block.gpsimd
        def _(pool):
            g = nc.gpsimd
            g.memset(eps[:, :], EPS)
            g.memset(zero[:, :], 0.0)
            g.memset(ident[:, :], 0.0)
            g.iota(iota_i[:, :], pattern=[[1, TOPK]], base=0, channel_multiplier=0)
            pool.drain()
            g.affine_select(out=ident[:, :], in_=ident[:, :], compare_op=ALU.not_equal, fill=1.0,
                            base=0, pattern=[[-1, P]], channel_multiplier=1)
            g.tensor_copy(iota16[:, :], iota_i[:, :])
            pool.drain()
            g.tensor_tensor(fold[:, :], ident[:, 0:NS], ident[:, NS:P], ALU.add)
            pool.drain()
            pool.sem_inc(s["p_consts"], 1)
            pool.sem_inc(s["vacc_free"], 1)
            for k in range(RING):
                pool.sem_inc(used[k], 1)

            def gather_step(i, part, j, half, table, at):
                pool.wait_ge(s["staged"], at(i, part, j, half) + 1)
                for k in range(RING):
                    pool.wait_ge(used[k], at(i, part, j, half) + 1)
                    pool.sem_inc(s["passed"], 1)
                    g.indirect_dma_start(rows[:, k, :], None, table,
                                         bass.IndirectOffsetOnAxis(ap=stage[half][:, k:k + 1], axis=0)).then_inc(got[k], 16)

            def gathers(i, part, table):
                with pool.Fori(0, SLOTS // STEP) as j:
                    pool.wait_ge(s["idx_ready"], PH * i + j + 1)
                    pool.sem_inc(s["passed"], 1)
                    for half in range(2):
                        g.tensor_copy(stage[half][:, :], idx[:, bass.ds(i * SLOTS + j * STEP + half * RING, RING)]).then_inc(s["staged"], 1)
                        gather_step(i, part, j, half, table, turn)

            def gathers_last(part, table):
                with pool.Fori(0, HALF // STEP) as j:
                    for half in range(2):
                        g.tensor_copy(stage[half][:, :], idx[:, bass.ds(TILES * SLOTS + j * STEP + half * RING, RING)]).then_inc(s["staged"], 1)
                        gather_step(TILES, part, j, half, table, turn_last)

            pool.wait_ge(s["keysT_ps"], 1)
            with pool.Fori(0, TILES) as i:
                gathers(i, 0, u_tab)
                gathers(i, 1, v_tab)
            pool.wait_ge(s["idx_ready"], PH * ALLT + 1)
            gathers_last(0, u_tab)
            gathers_last(1, v_tab)

        @block.tensor
        def _(pe):
            t = nc.tensor
            pe.wait_ge(s["p_consts"], 1)
            pe.wait_ge(s["k_in"], 48)
            for n in range(16):
                m = t.transpose(bank[n // 4][:, (n % 4) * P:(n % 4 + 1) * P], keys[:, n, :], ident[:, :])
            m.then_inc(s["keysT_ps"], 1)
            pe.wait_ge(s["keysT_sb"], 1)

            def scores(i, first=False):
                pe.wait_ge(s["c_ready"], i + 1)
                for k in range(KD):
                    m = t.transpose(bank[6 + k // 4][:, (k % 4) * P:(k % 4 + 1) * P], c_nxt[:, k * P:(k + 1) * P], ident[:, :])
                m.then_inc(s["cT_ps"], 1)
                pe.wait_ge(s["cT_sb"], i + 1)
                for b in range(4):
                    if first and b % 2 == 0:
                        pe.wait_ge(s[f"wq_in{b // 2}"], 16)
                    for c in range(4):
                        n = b * 4 + c
                        for k in range(KD):
                            m = t.matmul(bank[4 + b % 2][:, c * P:(c + 1) * P], wq[:, k, n * P:(n + 1) * P], cT[:, k, :],
                                         start=(k == 0), stop=(k == KD - 1))
                    m.then_inc(s["q_ps"], 1)
                    if b == 0:
                        continue
                    pe.wait_ge(s["q_sb"], 4 * i + b)
                pe.wait_ge(s["q_sb"], 4 * i + 4)
                for n in range(16):
                    m = t.matmul(bank[4 + n // 4][:, (n % 4) * P:(n % 4 + 1) * P], qT[:, n, :], keysT[:, n, :], start=True, stop=True)
                m.then_inc(s["s_ps"], 1)

            def accumulate(i, last):
                r, at, steps = (NS, turn_last, HALF // STEP) if last else (P, turn, SLOTS // STEP)
                pe.wait_ge(s["vacc_free"], i + 1)
                for n in range(2):
                    t.matmul(bank[n][0:r, :], zero[:, 0:r], g_ffn[:, n * 512:(n + 1) * 512], start=True, stop=False)
                with pe.Fori(0, steps) as j:
                    for n, k in enumerate(ON_PE):
                        pe.wait_ge(s["diag_ready"], (i * (SLOTS // STEP) + j) * NPE + n + 1)
                        pe.wait_ge(got[k % RING], 16 * (at(i, 1, j, k // RING) + 1))
                        for c in range(2):
                            m = t.matmul(bank[c][0:r, :], diag[:, n, 0:r], rows[:, k % RING, c * 512:(c + 1) * 512],
                                         start=False, stop=False)
                        m.then_inc(used[k % RING], 1)
                if last:
                    pe.wait_ge(s["gate_sub"], ALLT + 1)
                for n in range(2):
                    lhs, rhs = (fold, h_cur) if last else (zero, g_ffn)
                    m = t.matmul(bank[n][0:r, :], lhs[:, 0:r], rhs[:, n * 512:(n + 1) * 512], start=False, stop=True)
                m.then_inc(s["vacc_ps"], 1)

            def gate_products(i, r):
                pe.wait_ge(s["en_ready"], i + 1)
                pe.wait_ge(s["p_in"], 16 * i + 16)
                if r < P:
                    pe.sem_inc(s["pe_passed"], 1)
                for k in range(KD):
                    t.transpose(bank[4 + k // 4][:, (k % 4) * P:(k % 4) * P + r], en[0:r, k * P:(k + 1) * P], ident[0:r, 0:r])
                for k in range(PB):
                    m = t.transpose(bank[6][:, k * P:k * P + r], ple[0:r, k * P:(k + 1) * P], ident[0:r, 0:r])
                m.then_inc(s["enT_ps"], 1)
                pe.wait_ge(s["wg_in"], 16 * (KD + 1))
                pe.wait_ge(s["pT_sb"], i + 1)
                for n in range(2):
                    for k in range(PB):
                        t.matmul(bank[2 + n][0:r, :], pleT[:, k, 0:r], wi[:, k, n * 512:(n + 1) * 512], start=(k == 0), stop=(k == PB - 1))
                pe.wait_ge(s["enT_sb"], i + 1)
                for n in range(2):
                    for k in range(KD):
                        m = t.matmul(bank[n][0:r, :], cT[:, k, 0:r], wg[:, k, n * 512:(n + 1) * 512], start=(k == 0), stop=(k == KD - 1))
                m.then_inc(s["gate_ps"], 1)

            scores(0, first=True)
            scores(1)
            accumulate(0, False)
            with pe.Fori(1, TILES) as i:
                gate_products(i - 1, P)
                scores(i + 1)
                pe.wait_ge(s["sig_done"], i)
                accumulate(i, False)
            gate_products(TILES - 1, P)
            pe.wait_ge(s["sig_done"], TILES)
            accumulate(TILES, True)
            gate_products(TILES, NS)

        @block.scalar
        def _(act):
            ac = nc.scalar
            act.wait_ge(s["p_consts"], 1)
            act.wait_ge(s["keysT_ps"], 1)
            for b in range(4):
                m = ac.activation(keysT[:, 4 * b:4 * b + 4, :], bank[b][:, :].rearrange("p (c t) -> p c t", c=4), ACT.Copy)
            m.then_inc(s["keysT_sb"], 1)

            def rms(i):
                act.wait_ge(s["c_in"], 16 * i + 16)
                ac.activation(en, c_nxt[:, :], ACT.Square, accum_out=st[:, 0:1])
                act.drain()
                ac.activation(st[:, 1:2], st[:, 0:1], ACT.Sqrt, scale=1.0 / D, bias=eps[:, :]).then_inc(s["rms"], 1)

            def tokens_T(i):
                act.wait_ge(s["cT_ps"], i + 1)
                for b in range(2):
                    m = ac.activation(cT[:, 4 * b:4 * b + 4, :], bank[6 + b][:, :].rearrange("p (c t) -> p c t", c=4), ACT.Copy)
                m.then_inc(s["cT_sb"], 1)

            def queries(i):
                for b in range(4):
                    act.wait_ge(s["q_ps"], 4 * i + b + 1)
                    ac.activation(qT[:, 4 * b:4 * b + 4, :], bank[4 + b % 2][:, :].rearrange("p (c t) -> p c t", c=4), ACT.Copy).then_inc(s["q_sb"], 1)

            def scores(i):
                act.wait_ge(s["s_ps"], i + 1)
                for b in range(4):
                    m = ac.activation(sco[:, 4 * b:4 * b + 4, :], bank[4 + b][:, :].rearrange("p (c t) -> p c t", c=4), ACT.Copy)
                m.then_inc(s["s_sb"], 1)

            def gate_rms(i, r):
                act.wait_ge(s["cur_free"], i + 1)
                ac.activation(en[0:r, :], h_cur[0:r, :], ACT.Square, accum_out=gst[0:r, 0:1])
                act.drain()
                ac.activation(gst[0:r, 1:2], gst[0:r, 0:1], ACT.Sqrt, scale=1.0 / D, bias=eps[0:r, :]).then_inc(s["gate_rms"], 1)

            def gate_sigmoid(i, r):
                act.wait_ge(s["enT_ps"], i + 1)
                ac.activation(pleT[:, :, 0:r], bank[6][:, 0:PLE].rearrange("p (k t) -> p k t", k=PB)[:, :, 0:r], ACT.Copy).then_inc(s["pT_sb"], 1)
                act.wait_ge(s["gate_ps"], i + 1)
                for n in range(2):
                    m = ac.activation(y[0:r, n * 512:(n + 1) * 512], bank[n][0:r, :], ACT.Sigmoid)
                m.then_inc(s["sig_done"], 1)

            def last_rms(i, r):
                act.wait_ge(s["sum_ready"], i + 1)
                ac.activation(en[0:r, :], y[0:r, :], ACT.Square, accum_out=gst[0:r, 3:4])
                act.drain()
                ac.activation(gst[0:r, 4:5], gst[0:r, 3:4], ACT.Sqrt, scale=1.0 / D, bias=eps[0:r, :]).then_inc(s["rms2"], 1)

            def take_over(i):
                ac.activation(c_cur[:, :], c_nxt[:, :], ACT.Copy).then_inc(s["cur_ready"], 1)

            def gates(i):
                act.wait_ge(s["gate_sub"], i + 1)
                ac.activation(sc_all[:, :], sc_all[:, :], ACT.Exp).then_inc(s["gate_exp"], 1)

            def diagonals(i, last):
                r, at, steps = (NS, turn_last, HALF // STEP) if last else (P, turn, SLOTS // STEP)
                act.wait_ge(s["w_ready"], i + 1)
                act.sem_inc(s["act_passed"], 1)
                with act.Fori(0, steps) as j:
                    for n, k in enumerate(ON_PE):
                        act.wait_ge(used[k % RING], at(i, 1, j, k // RING))
                        act.sem_inc(s["act_passed"], 1)
                        ac.activation(diag[:, n, 0:r], (fold if last else ident)[:, :], ACT.Copy,
                                      scale=wgt[:, bass.ds(j * STEP + k, 1)]).then_inc(s["diag_ready"], 1)

            def weights(i, n):
                act.wait_ge(s["dots_ready"], i + 1)
                ac.activation(wgt[:, 0:n], dots[:, 0:n], ACT.Gelu).then_inc(s["gelu_done"], 1)

            rms(0)
            tokens_T(0)
            queries(0)
            scores(0)
            take_over(0)
            rms(1)
            tokens_T(1)
            queries(1)
            gates(0)
            scores(1)
            weights(0, SLOTS)
            take_over(1)
            diagonals(0, False)
            gates(1)
            with act.Fori(1, TILES) as i:
                rms(i + 1)
                gate_rms(i - 1, P)
                gate_sigmoid(i - 1, P)
                tokens_T(i + 1)
                last_rms(i - 1, P)
                act.wait_ge(s["y_out"], 16 * i)
                queries(i + 1)
                scores(i + 1)
                weights(i, SLOTS)
                take_over(i + 1)
                diagonals(i, False)
                gates(i + 1)
            gate_rms(TILES - 1, P)
            gate_sigmoid(TILES - 1, P)
            last_rms(TILES - 1, P)
            weights(TILES, HALF)
            diagonals(TILES, True)
            gate_rms(TILES, NS)
            act.wait_ge(s["y_out"], 16 * TILES)
            gate_sigmoid(TILES, NS)
            last_rms(TILES, NS)

        @block.vector
        def _(dve):
            v = nc.vector
            dve.wait_ge(s["p_consts"], 1)
            dve.wait_ge(s["k_in"], 48)

            def norm(i):
                dve.wait_ge(s["rms"], i + 1)
                v.reciprocal(st[:, 2:3], st[:, 1:2])
                dve.drain()
                v.scalar_tensor_tensor(c_nxt[:, :], c_nxt[:, :], st[:, 2:3], g_ffn[:, :], ALU.mult, ALU.mult).then_inc(s["c_ready"], 1)

            def best(i, j):
                v.tensor_copy(sst[:, :, :], sco[:, bass.ds(j * 2, 2), :])
                dve.drain()
                for f in range(2):
                    v.max(v1[:, f, 0:8], sst[:, f, :])
                dve.drain()
                for f in range(2):
                    v.max_index(x1[:, f, 0:8], v1[:, f, 0:8], sst[:, f, :])
                    v.match_replace(sst2[:, f, :], v1[:, f, 0:8], sst[:, f, :], LOW)
                dve.drain()
                for f in range(2):
                    v.max(v1[:, f, 8:16], sst2[:, f, :])
                dve.drain()
                for f in range(2):
                    v.max_index(x1[:, f, 8:16], v1[:, f, 8:16], sst2[:, f, :])
                v.tensor_tensor(cand[:, :, :], v1[:, 0, :].rearrange("p (a o) -> p a o", o=1).to_broadcast([P, TOPK, TOPK]),
                                v1[:, 1, :].rearrange("p (o b) -> p o b", o=1).to_broadcast([P, TOPK, TOPK]), ALU.add)
                dve.drain()
                flat = cand[:, :, :].rearrange("p a b -> p (a b)")
                v.tensor_copy(x1f[:, :, :], x1[:, :, :])
                v.max(sc16[:, 0:8], flat)
                dve.drain()
                v.max_index(ci[:, 0:8], sc16[:, 0:8], flat)
                v.match_replace(cand2[:, :], sc16[:, 0:8], flat, LOW)
                dve.drain()
                v.max(sc16[:, 8:16], cand2[:, :])
                dve.drain()
                v.max_index(ci[:, 8:16], sc16[:, 8:16], cand2[:, :])
                dve.drain()
                v.tensor_scalar(cab[:, 0, :], ci[:, :], 4, None, ALU.logical_shift_right)
                v.tensor_scalar(cab[:, 1, :], ci[:, :], 15, None, ALU.bitwise_and)
                dve.drain()
                v.tensor_copy(cabf[:, :, :], cab[:, :, :])
                dve.drain()
                for f in range(2):
                    v.tensor_tensor(eq[:, f], cabf[:, f, :].rearrange("p (k o) -> p k o", o=1).to_broadcast([P, TOPK, TOPK]),
                                    iota16[:, :].rearrange("p (o a) -> p o a", o=1).to_broadcast([P, TOPK, TOPK]), ALU.is_equal)
                dve.drain()
                for f in range(2):
                    v.tensor_tensor(eq[:, f], eq[:, f],
                                    x1f[:, f, :].rearrange("p (o a) -> p o a", o=1).to_broadcast([P, TOPK, TOPK]), ALU.mult)
                dve.drain()
                v.tensor_reduce(e12[:, :, :], eq[:, :, :, :], AXX, ALU.add)
                dve.drain()
                v.scalar_tensor_tensor(idx[:, bass.ds(i * SLOTS + j * TOPK, TOPK)], e12[:, 0, :], float(NK), e12[:, 1, :],
                                       ALU.mult, ALU.add).then_inc(s["idx_ready"], 1)
                v.tensor_scalar(sc_all[:, bass.ds(j * TOPK, TOPK)], sc16[:, :], sc16[:, 0:1], None, ALU.subtract)
                dve.drain()

            def gates(i):
                dve.wait_ge(s["gate_exp"], i + 1)
                by_head = sc_all[:, :].rearrange("p (h k) -> p h k", k=TOPK)
                v.tensor_reduce(gs[:, 0, :], by_head, AXX, ALU.add)
                dve.drain()
                v.reciprocal(gs[:, 1, :], gs[:, 0, :])
                dve.drain()
                v.tensor_tensor(gate[:, :].rearrange("p (h k) -> p h k", k=TOPK), by_head,
                                gs[:, 1, :].rearrange("p (h o) -> p h o", o=1).to_broadcast([P, PH, TOPK]), ALU.mult)
                dve.drain()

            norm(0)
            dve.wait_ge(s["s_sb"], 1)
            best(0, 0)

            def dots_of(i, j, at=turn):
                for k in range(STEP):
                    dve.wait_ge(got[k % RING], 16 * (at(i, 0, j, k // RING) + 1))
                    v.tensor_tensor_reduce(out=rows[:, k % RING, :], in0=rows[:, k % RING, :], in1=c_cur[:, :], scale=1.0,
                                           scalar=0.0, op0=ALU.mult, op1=ALU.add,
                                           accum_out=dot16[:, k:k + 1]).then_inc(used[k % RING], 1)
                dve.drain()
                v.tensor_copy(dots[:, bass.ds(j * STEP, STEP)], dot16[:, :])
                dve.drain()

            def dot_products(i, steps, at=turn):
                with dve.Fori(*steps) as j:
                    dots_of(i, j, at)

            def gate_norm(i, r):
                dve.wait_ge(s["gate_rms"], i + 1)
                v.reciprocal(gst[0:r, 2:3], gst[0:r, 1:2])
                dve.drain()
                v.tensor_scalar(en[0:r, :], h_cur[0:r, :], gst[0:r, 2:3], None, ALU.mult).then_inc(s["en_ready"], 1)

            def gate_T(i, r):
                dve.wait_ge(s["enT_ps"], i + 1)
                for b in range(2):
                    m = v.tensor_tensor(cT[:, 4 * b:4 * b + 4, 0:r], bank[4 + b][:, :].rearrange("p (k t) -> p k t", k=4)[:, :, 0:r],
                                        g_ple[:, 4 * b:4 * b + 4].rearrange("p (k o) -> p k o", o=1).to_broadcast([P, 4, r]), ALU.mult)
                m.then_inc(s["enT_sb"], 1)

            def gate_sum(i, r):
                dve.wait_ge(s["sig_done"], i + 1)
                for n in range(2):
                    v.tensor_tensor(y[0:r, n * 512:(n + 1) * 512], y[0:r, n * 512:(n + 1) * 512], bank[2 + n][0:r, :], ALU.mult)
                dve.drain()
                v.tensor_tensor(y[0:r, :], y[0:r, :], h_cur[0:r, :], ALU.add).then_inc(s["sum_ready"], 1)

            def last_norm(i, r):
                dve.wait_ge(s["rms2"], i + 1)
                v.reciprocal(gst[0:r, 5:6], gst[0:r, 4:5])
                dve.drain()
                v.scalar_tensor_tensor(y[0:r, :], y[0:r, :], gst[0:r, 5:6], g_fin[0:r, :], ALU.mult, ALU.mult).then_inc(s["y_ready"], 1)

            def tile(i, first, last):
                dve.wait_ge(s["cur_ready"], i + 1)
                dve.sem_inc(s["dve_passed"], 1)
                if first:
                    def head(j):
                        best(0, j)
                        dots_of(i, j - 1)

                    head(1)
                    norm(i + 1)
                    with dve.Fori(2, PH) as j:
                        head(j)
                    dve.sem_inc(s["gate_sub"], 1)
                    dot_products(i, (PH - 1, PH))
                    gates(i)
                else:
                    at = turn_last if last else turn
                    dot_products(i, (0, 1), at)
                    gates(i)
                    gate_norm(i - 1, P)
                    dot_products(i, (1, 2), at)
                    gate_T(i - 1, P)
                    if not last:
                        norm(i + 1)
                    summed, normed = (3, 4) if last else (4, 5)
                    dot_products(i, (2, summed), at)
                    gate_sum(i - 1, P)
                    dot_products(i, (summed, normed), at)
                    last_norm(i - 1, P)
                    if not last:
                        dot_products(i, (normed, SLOTS // STEP))
                dve.sem_inc(s["dots_ready"], 1)
                dve.wait_ge(s["gelu_done"], i + 1)
                if last:
                    for n in range(2):
                        q = slice(n * NS, (n + 1) * NS)
                        m = v.tensor_tensor(wgt[q, 0:HALF], wgt[q, 0:HALF], gate[q, n * HALF:(n + 1) * HALF], ALU.mult)
                    m.then_inc(s["w_ready"], 1)
                else:
                    v.tensor_tensor(wgt[:, :], wgt[:, :], gate[:, :], ALU.mult).then_inc(s["w_ready"], 1)
                dve.drain()
                if not last:
                    dve.wait_ge(s["s_sb"], i + 2)
                    dve.sem_inc(s["dve_passed"], 1)
                dve.wait_ge(s["h_in"], 16 * i + 16)
                dve.sem_inc(s["dve_passed"], 1)
                if last:
                    v.memset(h_cur[NS:P, :], 0.0)
                    dve.drain()
                at, steps = (turn_last, HALF // STEP) if last else (turn, SLOTS // STEP)
                with dve.Fori(0, steps) as j:
                    v.tensor_copy(w16[:, :], wgt[:, bass.ds(j * STEP, STEP)])
                    if not last:
                        best(i + 1, j)
                    else:
                        dve.drain()
                    for k in range(STEP):
                        if k in ON_PE:
                            continue
                        dve.wait_ge(got[k % RING], 16 * (at(i, 1, j, k // RING) + 1))
                        v.scalar_tensor_tensor(h_cur[:, :], rows[:, k % RING, :], w16[:, k:k + 1], h_cur[:, :],
                                               ALU.mult, ALU.add).then_inc(used[k % RING], 1)
                        dve.drain()
                dve.sem_inc(s["gate_sub"], 1)
                dve.wait_ge(s["vacc_ps"], i + 1)
                for n in range(2):
                    cols = slice(n * 512, (n + 1) * 512)
                    if last:
                        m = v.tensor_copy(h_cur[0:NS, cols], bank[n][0:NS, :])
                    else:
                        m = v.tensor_tensor(h_cur[:, cols], h_cur[:, cols], bank[n][:, :], ALU.add)
                m.then_inc(s["vacc_free"], 1)
                dve.drain()
                dve.sem_inc(s["cur_free"], 1)

            tile(0, True, False)
            dve.wait_ge(s["g_in"], 32)
            with dve.Fori(1, TILES) as i:
                tile(i, False, False)
            v.tensor_copy(idx[NS:P, TILES * SLOTS:TILES * SLOTS + HALF],
                          idx[NS:P, TILES * SLOTS + HALF:ALLT * SLOTS]).then_inc(s["idx_ready"], 1)
            tile(TILES, False, True)
            gate_norm(TILES, NS)
            gate_T(TILES, NS)
            gate_sum(TILES, NS)
            last_norm(TILES, NS)


def program(nc, a, out):
    h_rows = nc.dram_tensor("h_after_mixer", [ALLT * P, D], F32).ap()
    with ExitStack() as sems:
        mixer_block(nc, sems, a, out, h_rows)
        peer_block(nc, sems, a, out, h_rows)


_INS = ['x_prompt', 'x_sample', 'p_prompt', 'p_sample', 'cache_swa_k', 'cache_swa_v', 'state_conv', 'state_delta',
        'norm_mix', 'w_in', 'conv_w', 'attn_sinks', 'dn_a_log', 'dn_dt_bias', 'dn_norm', 'w_out', 'norm_ffn',
        'peer_wq', 'peer_keys1', 'peer_keys2', 'peer_u', 'peer_v', 'norm_ple', 'ple_in', 'ple_gate', 'norm_final']
_OUTS = [('y_p', (1, SEQ, D)), ('y_s', (DB, DS, D)), ('k_p', (1, 1, WIN, KVH, HD)), ('v_p', (1, 1, WIN, KVH, HD)),
         ('c_p', (1, 1, TAPS - 1, DQKV)), ('s_p', (1, 1, DH, HD, HD)), ('k_s', (1, DB, WIN, KVH, HD)),
         ('v_s', (1, DB, WIN, KVH, HD)), ('c_s', (1, DB, TAPS - 1, DQKV)), ('s_s', (1, DB, DH, HD, HD))]


def kernel(**inputs):
    import numpy as _np
    import concourse.bacc as _bacc
    from concourse.bass_utils import run_bass_kernel_spmd as _run

    nc = _bacc.Bacc("TRN2", target_bir_lowering=False, num_devices=1)
    arrays, a, out = {}, {}, {}
    for name in _INS:
        arrays[f"in_{name}_dram"] = _np.ascontiguousarray(inputs[name])
        a[name] = nc.dram_tensor(f"in_{name}_dram", arrays[f"in_{name}_dram"].shape, F32, kind="ExternalInput").ap()
    i, j = _np.arange(GRP * DS)[:, None] % DS, _np.arange(SKEYS)[None]
    far = (WIN + i - j < 0) | (WIN + i - j > WIN)
    consts = {"c_dist": _np.where(far, FAR, WIN + i - j).astype(_np.float32),
              "c_slope": _np.array([[SLOPE[g * GRP + n // DS] for g in range(KVH)] for n in range(GRP * DS)], _np.float32)}
    for name, value in consts.items():
        arrays[f"in_{name}_dram"] = value
        a[name] = nc.dram_tensor(f"in_{name}_dram", value.shape, F32, kind="ExternalInput").ap()
    for name, shape in _OUTS:
        out[name] = nc.dram_tensor(f"out_{name}_dram", shape, F32, kind="ExternalOutput").ap()
    program(nc, a, out)
    r = _run(nc, [arrays], core_ids=[0])
    return tuple(r.results[0][f"out_{name}_dram"] for name, _ in _OUTS)
```
